# Optimizing a Trainium2 kernel written in Bass

```python
import jax
import jax.numpy as jnp
from jax import lax
import numpy as np
import jax, jax.numpy as jnp

D_MODEL = 1024
BATCH = 1
SEQ = 1024
DEPTH = 2

GRID_W = 64
CTX_LEN = 256
D_MIX = D_MODEL
CONV_WIDTH = D_MIX // 4
CONV_KERNEL = 31
ATTN_WIDTH = D_MIX // 2
ATTN_HEAD_DIM = 64
ATTN_HEADS = ATTN_WIDTH // ATTN_HEAD_DIM
ATTN_KV_HEADS = 2
ATTN_GROUP = ATTN_HEADS // ATTN_KV_HEADS
ATTN_WINDOW = 128
ATTN_BLOCK = 128
ROPE_THETA = 10000.0
GLA_WIDTH = D_MIX - CONV_WIDTH - ATTN_WIDTH
GLA_HEADS = 4
GLA_DV = GLA_WIDTH // GLA_HEADS
GLA_DK = GLA_DV // 2
GLA_LOW_RANK = 16
GLA_TAU = 16.0
GLA_CHUNK = 64
NORM_EPS = 1e-6
NEG_INF = -1e30
F32 = jnp.float32

IN_COLUMNS = (
    ('a_val', CONV_WIDTH), ('a_glu', CONV_WIDTH), ('a_gate', CONV_WIDTH),
    ('b_q', ATTN_WIDTH), ('b_k', ATTN_KV_HEADS * ATTN_HEAD_DIM), ('b_v', ATTN_KV_HEADS * ATTN_HEAD_DIM), ('b_gate', ATTN_WIDTH),
    ('c_q', GLA_HEADS * GLA_DK), ('c_k', GLA_HEADS * GLA_DK), ('c_v', GLA_WIDTH),
    ('c_lr_f', GLA_LOW_RANK), ('c_lr_b', GLA_LOW_RANK), ('c_gate', GLA_WIDTH),
)
N_IN = (3 * CONV_WIDTH + 2 * ATTN_WIDTH + 2 * ATTN_KV_HEADS * ATTN_HEAD_DIM
        + 2 * GLA_HEADS * GLA_DK + 2 * GLA_WIDTH + 2 * GLA_LOW_RANK)
CTX_KV_COLUMNS = ('b_k', 'b_v', 'c_k', 'c_v', 'c_lr_f', 'c_lr_b')


def _rms_norm(x):
    xf = x.astype(F32)
    return (xf * lax.rsqrt(jnp.mean(xf * xf, axis=-1, keepdims=True) + NORM_EPS)).astype(x.dtype)

def _column_slices():
    out, off = {}, 0
    for name, size in IN_COLUMNS:
        out[name] = (off, size)
        off += size
    return out

def _project(h, w_in, names=None):
    sl = _column_slices()
    if names is None:
        z = h @ w_in
        return {n: z[..., o:o + s] for n, (o, s) in sl.items()}
    return {n: h @ w_in[:, sl[n][0]:sl[n][0] + sl[n][1]] for n in names}

def _heads(t, n_heads):
    return t.reshape(t.shape[:2] + (n_heads, t.shape[-1] // n_heads))

def _rope_tables(n_tokens):
    rows = n_tokens // GRID_W
    r = jnp.repeat(jnp.arange(rows, dtype=F32), GRID_W)
    col = jnp.tile(jnp.arange(GRID_W, dtype=F32), rows)
    n_freq = ATTN_HEAD_DIM // 4
    inv = ROPE_THETA ** (-jnp.arange(n_freq, dtype=F32) / n_freq)
    ang = jnp.concatenate([r[:, None] * inv, col[:, None] * inv], axis=-1)
    ang = jnp.concatenate([ang, ang], axis=-1)
    return jnp.cos(ang), jnp.sin(ang)

def _apply_rope(x, cos, sin):
    xf = x.astype(F32)
    half = ATTN_HEAD_DIM // 2
    rot = jnp.concatenate([-xf[..., half:], xf[..., :half]], axis=-1)
    return (xf * cos[None, :, None, :] + rot * sin[None, :, None, :]).astype(x.dtype)

def _conv_branch(p, conv_w, conv_b, ln_w, ln_b):
    u = p['a_val'] * jax.nn.sigmoid(p['a_glu'])
    u = lax.conv_general_dilated(
        u, conv_w[:, None, :].astype(u.dtype), window_strides=(1,),
        padding=((CONV_KERNEL // 2, CONV_KERNEL // 2),),
        dimension_numbers=('NWC', 'WIO', 'NWC'), feature_group_count=CONV_WIDTH) + conv_b
    uf = u.astype(F32)
    mu = jnp.mean(uf, axis=-1, keepdims=True)
    var = jnp.mean(jnp.square(uf - mu), axis=-1, keepdims=True)
    u = ((uf - mu) * lax.rsqrt(var + NORM_EPS) * ln_w + ln_b).astype(p['a_val'].dtype)
    return jax.nn.silu(u) * jax.nn.silu(p['a_gate'])

def _windowed_attention(q, k, v, kc, vc, sink):
    B, S, H, Dh = q.shape
    nb = S // ATTN_BLOCK
    nc = kc.shape[1]
    qb = (q * Dh ** -0.5).reshape(B, nb, ATTN_BLOCK, ATTN_KV_HEADS, ATTN_GROUP, Dh).transpose(1, 0, 2, 3, 4, 5)

    def band(t):
        tb = t.reshape(B, nb, ATTN_BLOCK, ATTN_KV_HEADS, Dh)
        tp = jnp.pad(tb, ((0, 0), (1, 1), (0, 0), (0, 0), (0, 0)))
        return jnp.concatenate([tp[:, :-2], tp[:, 1:-1], tp[:, 2:]], axis=2).transpose(1, 0, 2, 3, 4)

    kw, vw = band(k), band(v)
    qi = jnp.arange(ATTN_BLOCK)
    kj = jnp.arange(3 * ATTN_BLOCK)
    rel = ATTN_BLOCK + qi[:, None] - kj[None, :]
    kpos = (jnp.arange(nb)[:, None] - 1) * ATTN_BLOCK + kj[None, :]
    mask = (jnp.abs(rel)[None] <= ATTN_WINDOW) & ((kpos >= 0) & (kpos < S))[:, None, :]
    sink_l = sink.astype(F32).reshape(ATTN_KV_HEADS, ATTN_GROUP)

    def one_block(args):
        qn, kn, vn, mn = args
        s_loc = jnp.einsum('bqhgd,bkhd->bhgqk', qn, kn).astype(F32)
        s_loc = jnp.where(mn, s_loc, NEG_INF)
        s_ctx = jnp.einsum('bqhgd,bchd->bhgqc', qn, kc).astype(F32)
        s_sink = jnp.broadcast_to(sink_l[None, :, :, None, None], s_ctx.shape[:-1] + (1,))
        p = jax.nn.softmax(jnp.concatenate([s_sink, s_ctx, s_loc], axis=-1), axis=-1)
        p_ctx = p[..., 1:1 + nc].astype(vn.dtype)
        p_loc = p[..., 1 + nc:].astype(vn.dtype)
        return (jnp.einsum('bhgqc,bchd->bqhgd', p_ctx, vc)
                + jnp.einsum('bhgqk,bkhd->bqhgd', p_loc, vn))

    o = lax.map(one_block, (qb, kw, vw, mask))
    return o.transpose(1, 0, 2, 3, 4, 5).reshape(B, S, H * Dh)

def _ctx_attention(qc, kc, vc, sink):
    B, Nc, H, Dh = qc.shape
    qg = (qc * Dh ** -0.5).reshape(B, Nc, ATTN_KV_HEADS, ATTN_GROUP, Dh)
    s = jnp.einsum('bqhgd,bkhd->bhgqk', qg, kc).astype(F32)
    s_sink = jnp.broadcast_to(sink.astype(F32).reshape(ATTN_KV_HEADS, ATTN_GROUP)[None, :, :, None, None],
                              s.shape[:-1] + (1,))
    p = jax.nn.softmax(jnp.concatenate([s_sink, s], axis=-1), axis=-1)[..., 1:].astype(vc.dtype)
    return jnp.einsum('bhgqk,bkhd->bqhgd', p, vc).reshape(B, Nc, H * Dh)

def _gla_decay(lr, w_up, b_up):
    z = lr.astype(F32) @ w_up.astype(F32) + b_up.astype(F32)
    return (jax.nn.log_sigmoid(z) / GLA_TAU).reshape(lr.shape[:2] + (GLA_HEADS, GLA_DK))

def _gla_chunked(q, k, v, log_a, s0):
    B, T, H, _ = q.shape
    dv = v.shape[-1]
    n = T // GLA_CHUNK

    def chunks(t):
        return t.astype(F32).reshape(B, n, GLA_CHUNK, H, t.shape[-1]).transpose(1, 0, 2, 3, 4)

    qc, kc, vc, la = chunks(q), chunks(k), chunks(v), chunks(log_a)
    b = jnp.cumsum(la, axis=2)
    b_last = b[:, :, -1:]
    q_in = qc * jnp.exp(b)
    k_in = kc * jnp.exp(-b)
    causal = jnp.tril(jnp.ones((GLA_CHUNK, GLA_CHUNK), dtype=bool))
    att = jnp.where(causal, jnp.einsum('nbthd,nbshd->nbhts', q_in, k_in), 0.0)
    o_intra = jnp.einsum('nbhts,nbshv->nbthv', att, vc)
    chunk_state = jnp.einsum('nbshd,nbshv->nbhdv', kc * jnp.exp(b_last - b), vc)
    chunk_decay = jnp.exp(b_last[:, :, 0])

    def step(s, xs):
        q_n, dec_n, st_n = xs
        o = jnp.einsum('bthd,bhdv->bthv', q_n, s)
        return dec_n[..., None] * s + st_n, o

    s_final, o_inter = lax.scan(step, s0.astype(F32), (q_in, chunk_decay, chunk_state))
    o = (o_intra + o_inter).transpose(1, 0, 2, 3, 4).reshape(B, T, H, dv)
    return o, s_final

def _gla_final_state(k, v, log_a):
    L = jnp.cumsum(log_a.astype(F32), axis=1)
    w = jnp.exp(L[:, -1:] - L)
    return jnp.einsum('bthd,bthv->bhdv', k.astype(F32) * w, v.astype(F32))

def _gla_output(o, gate, norm_w):
    B, T = o.shape[:2]
    of = o * lax.rsqrt(jnp.mean(o * o, axis=-1, keepdims=True) + NORM_EPS)
    of = of * norm_w.astype(F32).reshape(GLA_HEADS, GLA_DV)
    return of.reshape(B, T, GLA_WIDTH).astype(gate.dtype) * jax.nn.silu(gate)

def _flip(t):
    return jnp.flip(t, axis=1)

def _hybrid_layer(xl, xc, c, c_ctx, w_mod, b_mod, w_in, conv_w, conv_b, conv_ln_w, conv_ln_b,
                  attn_sink, gla_w_up, gla_b_up, gla_norm_w, w_out, rope_cos, rope_sin, update_ctx):
    B, S, _ = xl.shape
    D = D_MODEL
    shift, scale, gate = jnp.split(jax.nn.silu(c) @ w_mod + b_mod, 3, axis=-1)
    n_mod_c = 3 * D if update_ctx else 2 * D
    mod_c = jax.nn.silu(c_ctx) @ w_mod[:, :n_mod_c] + b_mod[:n_mod_c]
    hl = _rms_norm(xl) * (1.0 + scale[:, None]) + shift[:, None]
    hc = _rms_norm(xc) * (1.0 + mod_c[D:2 * D]) + mod_c[:D]
    pl = _project(hl, w_in)
    pc = _project(hc, w_in) if update_ctx else _project(hc, w_in, CTX_KV_COLUMNS)

    a_l = _conv_branch(pl, conv_w, conv_b, conv_ln_w, conv_ln_b)

    q_l = _apply_rope(_heads(pl['b_q'], ATTN_HEADS), rope_cos, rope_sin)
    k_l = _apply_rope(_heads(pl['b_k'], ATTN_KV_HEADS), rope_cos, rope_sin)
    v_l = _heads(pl['b_v'], ATTN_KV_HEADS)
    k_cx = _heads(pc['b_k'], ATTN_KV_HEADS)
    v_cx = _heads(pc['b_v'], ATTN_KV_HEADS)
    b_l = _windowed_attention(q_l, k_l, v_l, k_cx, v_cx, attn_sink) * jax.nn.silu(pl['b_gate'])

    gq_l = _heads(pl['c_q'], GLA_HEADS) * GLA_DK ** -0.5
    gk_l = _heads(pl['c_k'], GLA_HEADS)
    gv_l = _heads(pl['c_v'], GLA_HEADS)
    la_lf = _gla_decay(pl['c_lr_f'], gla_w_up[0], gla_b_up[0])
    la_lb = _gla_decay(pl['c_lr_b'], gla_w_up[1], gla_b_up[1])
    gk_c = _heads(pc['c_k'], GLA_HEADS)
    gv_c = _heads(pc['c_v'], GLA_HEADS)
    la_cf = _gla_decay(pc['c_lr_f'], gla_w_up[0], gla_b_up[0])
    la_cb = _gla_decay(pc['c_lr_b'], gla_w_up[1], gla_b_up[1])
    if update_ctx:
        gq_c = _heads(pc['c_q'], GLA_HEADS) * GLA_DK ** -0.5
        zeros = jnp.zeros((B, GLA_HEADS, GLA_DK, GLA_DV), F32)
        o_cf, s_f = _gla_chunked(gq_c, gk_c, gv_c, la_cf, zeros)
        o_cb, s_b = _gla_chunked(_flip(gq_c), _flip(gk_c), _flip(gv_c), _flip(la_cb), zeros)
    else:
        s_f = _gla_final_state(gk_c, gv_c, la_cf)
        s_b = _gla_final_state(_flip(gk_c), _flip(gv_c), _flip(la_cb))
    o_lf, _ = _gla_chunked(gq_l, gk_l, gv_l, la_lf, s_f)
    o_lb, _ = _gla_chunked(_flip(gq_l), _flip(gk_l), _flip(gv_l), _flip(la_lb), s_b)
    c_l = _gla_output(o_lf + _flip(o_lb), pl['c_gate'], gla_norm_w)

    y_l = jnp.concatenate([a_l, b_l, c_l], axis=-1) @ w_out
    xl = xl + gate[:, None] * y_l

    if update_ctx:
        a_c = _conv_branch(pc, conv_w, conv_b, conv_ln_w, conv_ln_b)
        q_cx = _heads(pc['b_q'], ATTN_HEADS)
        b_c = _ctx_attention(q_cx, k_cx, v_cx, attn_sink) * jax.nn.silu(pc['b_gate'])
        c_c = _gla_output(o_cf + _flip(o_cb), pc['c_gate'], gla_norm_w)
        y_c = jnp.concatenate([a_c, b_c, c_c], axis=-1) @ w_out
        xc = xc + mod_c[2 * D:] * y_c
    return xl, xc

def first_inputs(seed: int = 0) -> dict:
    key = jax.random.key(seed)
    ks = jax.random.split(key, 17)
    nrm = jax.random.normal
    return {
        'x': nrm(ks[0], (BATCH, SEQ, D_MODEL), F32),
        'c': nrm(ks[1], (BATCH, D_MODEL), F32),
        'ctx': nrm(ks[2], (BATCH, CTX_LEN, D_MODEL), F32),
        'c_ctx': nrm(ks[3], (D_MODEL,), F32),
        'w_mod': nrm(ks[4], (DEPTH, D_MODEL, 3 * D_MODEL), F32) * (0.5 * D_MODEL ** -0.5),
        'b_mod': 0.01 * nrm(ks[5], (DEPTH, 3 * D_MODEL), F32),
        'w_in': nrm(ks[6], (DEPTH, D_MODEL, N_IN), F32) * D_MODEL ** -0.5,
        'conv_w': nrm(ks[7], (DEPTH, CONV_KERNEL, CONV_WIDTH), F32) * CONV_KERNEL ** -0.5,
        'conv_b': 0.01 * nrm(ks[8], (DEPTH, CONV_WIDTH), F32),
        'conv_ln_w': 1.0 + 0.01 * nrm(ks[9], (DEPTH, CONV_WIDTH), F32),
        'conv_ln_b': 0.01 * nrm(ks[10], (DEPTH, CONV_WIDTH), F32),
        'attn_sink': 0.5 * nrm(ks[11], (DEPTH, ATTN_HEADS), F32),
        'gla_w_up': nrm(ks[12], (DEPTH, 2, GLA_LOW_RANK, GLA_HEADS * GLA_DK), F32) * GLA_LOW_RANK ** -0.5,
        'gla_b_up': 0.1 * nrm(ks[13], (DEPTH, 2, GLA_HEADS * GLA_DK), F32),
        'gla_norm_w': 1.0 + 0.01 * nrm(ks[14], (DEPTH, GLA_WIDTH), F32),
        'w_out': nrm(ks[15], (DEPTH, D_MIX, D_MODEL), F32) * D_MIX ** -0.5,
        'final_norm_w': 1.0 + 0.01 * nrm(ks[16], (D_MODEL,), F32),
    }

def first_block(x, c, ctx, c_ctx, w_mod, b_mod, w_in, conv_w, conv_b, conv_ln_w, conv_ln_b,
              attn_sink, gla_w_up, gla_b_up, gla_norm_w, w_out, final_norm_w):
    rope_cos, rope_sin = _rope_tables(x.shape[1])
    xl, xc = x, ctx
    for i in range(DEPTH):
        xl, xc = _hybrid_layer(
            xl, xc, c, c_ctx, w_mod[i], b_mod[i], w_in[i], conv_w[i], conv_b[i], conv_ln_w[i], conv_ln_b[i],
            attn_sink[i], gla_w_up[i], gla_b_up[i], gla_norm_w[i], w_out[i], rope_cos, rope_sin,
            update_ctx=(i < DEPTH - 1))
    return _rms_norm(xl) * final_norm_w


_first_inputs = first_inputs


def first_inputs(seed=0):
    import zlib

    import numpy as np

    out = dict(_first_inputs(seed))
    spreads = {}
    factors = {'ctx': 3.28,
     'b_mod': 7.232,
     'conv_b': 8.0,
     'conv_ln_w': 8.0,
     'conv_ln_b': 8.0,
     'attn_sink': 8.0,
     'gla_w_up': 2.765,
     'gla_b_up': 8.0,
     'gla_norm_w': 8.0,
     'final_norm_w': 5.714}
    for name, (base, spread) in spreads.items():
        noise = np.random.default_rng([zlib.crc32(name.encode()), seed]).standard_normal(out[name].shape)
        drawn = base * np.exp(spread * noise) if base else spread * noise
        out[name] = jnp.asarray(drawn.astype(out[name].dtype))
    for name, factor in factors.items():
        out[name] = (out[name] * factor).astype(out[name].dtype)
    return out


_narrow_inputs = first_inputs


def first_inputs(seed=0):
    out = dict(_narrow_inputs(seed))
    wider = {'conv_ln_w': 9.6,
     'conv_ln_b': 9.36,
     'attn_sink': 6.42,
     'gla_norm_w': 7.97,
     'final_norm_w': 6.33}
    for name, times in wider.items():
        mean = out[name].mean()
        out[name] = (mean + times * (out[name] - mean)).astype(out[name].dtype)
    return out


CHUNK = 64
D_MIX_2 = D_MODEL
A_WIDTH = D_MIX_2 // 4
A_HEADS = 4
A_HEAD_DIM = A_WIDTH // A_HEADS
A_BLOCK = 128
POOL_WINDOWS = (2, 4, 8, 16)
B_WIDTH = D_MIX_2 // 4
B_GROUP_DIM = B_WIDTH // len(POOL_WINDOWS)
C_WIDTH = D_MIX_2 - A_WIDTH - B_WIDTH
C_HEADS = 8
C_HEAD_DIM = C_WIDTH // C_HEADS
ROPE_BASE = 10000.0
IN_COLS = 2 * A_WIDTH + B_WIDTH + 4 * C_WIDTH
D_FF = ((8 * D_MODEL // 3 + 127) // 128) * 128
CONV_WIDTH_2 = 3
EPS = 1e-6


def rms_norm(x, g):
    xf = x.astype(jnp.float32)
    y = xf * lax.rsqrt(jnp.mean(xf * xf, axis=-1, keepdims=True) + EPS)
    return (y * g.astype(jnp.float32)).astype(x.dtype)

def spatial_gating(z, vnorm_g, ws, bs):
    bsz, s_len, _ = z.shape
    u, v = jnp.split(z, 2, axis=-1)
    v = rms_norm(v, vnorm_g)
    nb = s_len // A_BLOCK
    v = v.reshape(bsz, nb, A_BLOCK, A_HEADS, A_HEAD_DIM)
    chunk_id = jnp.arange(A_BLOCK) // CHUNK
    mask = chunk_id[:, None] >= chunk_id[None, :]
    w = jnp.where(mask[None], ws, jnp.zeros_like(ws))
    sv = jnp.einsum('hts,bnshd->bnthd', w, v) + bs.T[None, None, :, :, None]
    return u * sv.reshape(bsz, s_len, A_WIDTH)

def multiscale_pool(xb, w_grp, scale):
    bsz, s_len, _ = xb.shape
    xf = xb.astype(jnp.float32)
    cs = jnp.concatenate([jnp.zeros((bsz, 1, B_WIDTH), jnp.float32), jnp.cumsum(xf, axis=1)], axis=1)
    t = jnp.arange(s_len)
    outs = []
    for gi, win in enumerate(POOL_WINDOWS):
        sl = slice(gi * B_GROUP_DIM, (gi + 1) * B_GROUP_DIM)
        lo = jnp.maximum(t + 1 - win, 0)
        cnt = (t + 1 - lo).astype(jnp.float32)
        outs.append((cs[:, 1:, sl] - cs[:, lo, sl]) / cnt[None, :, None])
    pooled = jnp.concatenate(outs, axis=-1).astype(xb.dtype) - xb
    pooled = pooled.reshape(bsz, s_len, len(POOL_WINDOWS), B_GROUP_DIM)
    y = jnp.einsum('bsgc,gcd->bsgd', pooled, w_grp).reshape(bsz, s_len, B_WIDTH)
    return y * scale

def rotary(x, pos):
    half = x.shape[-1] // 2
    inv = ROPE_BASE ** (-jnp.arange(half, dtype=jnp.float32) / half)
    ang = pos.astype(jnp.float32)[:, None] * inv[None, :]
    cos = jnp.cos(ang)[None, :, None, :]
    sin = jnp.sin(ang)[None, :, None, :]
    xf = x.astype(jnp.float32)
    x1, x2 = xf[..., :half], xf[..., half:]
    return jnp.concatenate([x1 * cos - x2 * sin, x2 * cos + x1 * sin], axis=-1).astype(x.dtype)

def retention(q, k, v, g, norm_g):
    bsz, s_len, _ = q.shape
    n_chunks = s_len // CHUNK
    dt = q.dtype
    pos = jnp.arange(s_len)
    q = rotary(q.reshape(bsz, s_len, C_HEADS, C_HEAD_DIM), pos) * (C_HEAD_DIM ** -0.5)
    k = rotary(k.reshape(bsz, s_len, C_HEADS, C_HEAD_DIM), pos)
    v = v.reshape(bsz, s_len, C_HEADS, C_HEAD_DIM)
    log_gamma = jnp.log1p(-jnp.exp2(-5.0 - jnp.arange(C_HEADS, dtype=jnp.float32)))
    idx = jnp.arange(CHUNK, dtype=jnp.float32)
    d_intra = jnp.exp(log_gamma[:, None, None] * jnp.abs(idx[:, None] - idx[None, :])).astype(dt)
    k_dec = jnp.exp(log_gamma[None, :] * (CHUNK - 1 - idx)[:, None]).astype(dt)
    q_dec = jnp.exp(log_gamma[None, :] * (idx + 1)[:, None]).astype(dt)
    chunk_dec = jnp.exp(log_gamma * CHUNK).astype(dt)
    qc = q.reshape(bsz, n_chunks, CHUNK, C_HEADS, C_HEAD_DIM)
    kc = k.reshape(bsz, n_chunks, CHUNK, C_HEADS, C_HEAD_DIM)
    vc = v.reshape(bsz, n_chunks, CHUNK, C_HEADS, C_HEAD_DIM)
    scores = jnp.einsum('bnthd,bnshd->bnhts', qc, kc) * d_intra
    y_intra = jnp.einsum('bnhts,bnshe->bnthe', scores, vc)
    kv = jnp.einsum('bnshd,bnshe->nbhde', kc * k_dec[:, :, None], vc)

    def step(state, kv_n):
        return state * chunk_dec[None, :, None, None] + kv_n, state

    _, s_prev = lax.scan(step, jnp.zeros(kv.shape[1:], kv.dtype), kv)
    y_cross = jnp.einsum('bnthd,nbhde->bnthe', qc * q_dec[:, :, None], s_prev)
    y = (y_intra + y_cross).reshape(bsz, s_len, C_HEADS, C_HEAD_DIM)
    yf = y.astype(jnp.float32)
    mu = jnp.mean(yf, axis=-1, keepdims=True)
    var = jnp.mean(jnp.square(yf - mu), axis=-1, keepdims=True)
    yf = (yf - mu) * lax.rsqrt(var + EPS)
    y = (yf.reshape(bsz, s_len, C_WIDTH) * norm_g.astype(jnp.float32)).astype(dt)
    return jax.nn.silu(g) * y

def conv_ffn(h, w_up, conv_w, conv_b, w_down):
    up = h @ w_up
    s_len = up.shape[1]
    padded = jnp.pad(up, ((0, 0), (CONV_WIDTH_2 - 1, 0), (0, 0)))
    conv = conv_b + padded[:, 0:s_len] * conv_w[0]
    for j in range(1, CONV_WIDTH_2):
        conv = conv + padded[:, j:j + s_len] * conv_w[j]
    gate, val = jnp.split(conv, 2, axis=-1)
    return (jax.nn.silu(gate) * val) @ w_down

def second_inputs(seed: int = 0) -> dict:
    key = jax.random.key(seed)
    ks = jax.random.split(key, 20)
    f32 = jnp.float32
    nrm = lambda k, shape, s: jax.random.normal(k, shape, f32) * s
    return {
        "x": jax.random.normal(ks[0], (BATCH, SEQ, D_MODEL), f32),
        "norm1_g": 1.0 + nrm(ks[1], (DEPTH, D_MODEL), 0.05),
        "w_in": nrm(ks[2], (DEPTH, D_MODEL, IN_COLS), D_MODEL ** -0.5),
        "a_vnorm_g": 1.0 + nrm(ks[3], (DEPTH, A_WIDTH), 0.05),
        "a_ws": nrm(ks[4], (DEPTH, A_HEADS, A_BLOCK, A_BLOCK), 0.5 * A_BLOCK ** -0.5),
        "a_bs": 1.0 + nrm(ks[5], (DEPTH, A_HEADS, A_BLOCK), 0.1),
        "b_w": nrm(ks[6], (DEPTH, len(POOL_WINDOWS), B_GROUP_DIM, B_GROUP_DIM), B_GROUP_DIM ** -0.5),
        "b_scale": 1.0 + nrm(ks[7], (DEPTH, B_WIDTH), 0.1),
        "c_norm_g": 1.0 + nrm(ks[8], (DEPTH, C_WIDTH), 0.05),
        "w_out": nrm(ks[9], (DEPTH, D_MIX_2, D_MODEL), D_MIX_2 ** -0.5),
        "norm2_g": 1.0 + nrm(ks[10], (DEPTH, D_MODEL), 0.05),
        "w_up": nrm(ks[11], (DEPTH, D_MODEL, 2 * D_FF), D_MODEL ** -0.5),
        "conv_w": nrm(ks[12], (DEPTH, CONV_WIDTH_2, 2 * D_FF), CONV_WIDTH_2 ** -0.5),
        "conv_b": nrm(ks[13], (DEPTH, 2 * D_FF), 0.02),
        "w_down": nrm(ks[14], (DEPTH, D_FF, D_MODEL), D_FF ** -0.5),
        "final_g": 1.0 + nrm(ks[15], (D_MODEL,), 0.05),
    }

def second_block(x, norm1_g, w_in, a_vnorm_g, a_ws, a_bs, b_w, b_scale, c_norm_g,
              w_out, norm2_g, w_up, conv_w, conv_b, w_down, final_g):
    splits = [2 * A_WIDTH, 2 * A_WIDTH + B_WIDTH, 2 * A_WIDTH + B_WIDTH + C_WIDTH,
              2 * A_WIDTH + B_WIDTH + 2 * C_WIDTH, 2 * A_WIDTH + B_WIDTH + 3 * C_WIDTH]
    for l in range(DEPTH):
        h = rms_norm(x, norm1_g[l])
        proj = h @ w_in[l]
        za, xb, q, k, v, g = jnp.split(proj, splits, axis=-1)
        ya = spatial_gating(jax.nn.gelu(za), a_vnorm_g[l], a_ws[l], a_bs[l])
        yb = multiscale_pool(xb, b_w[l], b_scale[l])
        yc = retention(q, k, v, g, c_norm_g[l])
        x = x + jnp.concatenate([ya, yb, yc], axis=-1) @ w_out[l]
        x = x + conv_ffn(rms_norm(x, norm2_g[l]), w_up[l], conv_w[l], conv_b[l], w_down[l])
    return rms_norm(x, final_g)


def setup_inputs(seed=0):
    out = dict(first_inputs(seed))
    for name, value in second_inputs(seed + 1).items():
        if name != "x":
            out[name + "_2"] = value
    return out


def reference(
    x, c, ctx, c_ctx, w_mod, b_mod, w_in, conv_w, conv_b, conv_ln_w, conv_ln_b, attn_sink,
    gla_w_up, gla_b_up, gla_norm_w, w_out, final_norm_w, norm1_g_2, w_in_2, a_vnorm_g_2, a_ws_2,
    a_bs_2, b_w_2, b_scale_2, c_norm_g_2, w_out_2, norm2_g_2, w_up_2, conv_w_2, conv_b_2,
    w_down_2, final_g_2,
):
    x = first_block(
        x, c, ctx, c_ctx, w_mod, b_mod, w_in, conv_w, conv_b, conv_ln_w, conv_ln_b, attn_sink,
        gla_w_up, gla_b_up, gla_norm_w, w_out, final_norm_w,
    )
    return second_block(
        x, norm1_g_2, w_in_2, a_vnorm_g_2, a_ws_2, a_bs_2, b_w_2, b_scale_2, c_norm_g_2,
        w_out_2, norm2_g_2, w_up_2, conv_w_2, conv_b_2, w_down_2, final_g_2,
    )


_drawn_inputs = setup_inputs


def setup_inputs(seed=0):
    import zlib

    import numpy as np

    out = dict(_drawn_inputs(seed))
    spreads = {}
    factors = {'norm1_g_2': 4.268,
     'a_vnorm_g_2': 24.273,
     'a_bs_2': 7.157,
     'b_scale_2': 5.646,
     'c_norm_g_2': 8.0,
     'norm2_g_2': 5.067,
     'conv_b_2': 8.0}
    for name, (base, spread) in spreads.items():
        noise = np.random.default_rng([zlib.crc32(name.encode()), seed]).standard_normal(out[name].shape)
        drawn = base * np.exp(spread * noise) if base else spread * noise
        out[name] = jnp.asarray(drawn.astype(out[name].dtype))
    for name, factor in factors.items():
        out[name] = (out[name] * factor).astype(out[name].dtype)
    return out
```

```python
import numpy as np
import concourse.bass as bass
from concourse import mybir
from concourse.alu_op_type import AluOpType as ALU

F32 = mybir.dt.float32
F32R = mybir.dt.float32r
ACT = mybir.ActivationFunctionType
AX = mybir.AxisListType.X

P = 128
D = 1024
DT = D // P
S, C = 1024, 256
T = S + C
CH_ALL = [(0, 512), (512, 512), (1024, 256)]
CH_LAT = CH_ALL[:2]
NBLK = S // P
NTT = T // P
CK = 31
PAD = CK // 2
HD = 64
EPS = 1e-6
GD = 32
IN1 = ["glu0", "val0", "glu1", "val1", "gate0", "gate1", "bk", "bv",
       "q0", "bg0", "q1", "bg1", "q2", "bg2", "q3", "bg3",
       "lr", "cq", "ck", "cv0", "cv1", "cg0", "cg1"]
KV1 = {"bk", "bv", "lr", "ck", "cv0", "cv1"}
IN2 = ["sv0", "sv1", "su0", "su1", "x0", "x1"] + [f"{a}{j}" for j in range(4) for a in "qkvg"]
NF = 22
GROUPS = [(0, 5), (5, 10), (10, 14), (14, 18), (18, 22)]
V1 = dict(conv_w=0, conv_b=62, ln_w=64, ln_b=66, norm=68, b_mod=70)
NV1 = 94
V2 = dict(g1=0, vn=8, bs=10, cn=12, g2=16, conv_w=24, conv_b=156)
NV2 = 200
NRAW, NSPL = 3, 3


def stream():
    seq = []
    for l in range(2):
        for i, n in enumerate(IN1):
            seq.append(("in1", l, i, 8, CH_ALL if l == 0 or n in KV1 else CH_LAT))
        for d in range(DT):
            seq.append(("out1", l, d, 8, CH_ALL if l == 0 else CH_LAT))
    for l in range(2):
        for i, n in enumerate(IN2):
            seq.append(("in2", l, i, 8, CH_LAT))
        for d in range(DT):
            seq.append(("out2", l, d, 8, CH_LAT))
        for g, (f0, f1) in enumerate(GROUPS):
            for f in range(f0, f1):
                seq.append(("up", l, 2 * f, 8, CH_LAT))
                seq.append(("up", l, 2 * f + 1, 8, CH_LAT))
            for d in range(DT):
                seq.append(("down", l, (g, d), f1 - f0, CH_LAT))
    return seq


SEQ = stream()
INDEX = {e[:3]: g for g, e in enumerate(SEQ)}
FIRST_CHUNK = np.cumsum([0] + [len(e[4]) for e in SEQ]).tolist()


def masks():
    s, t = np.arange(P)[:, None], np.arange(P)[None, :]
    same = (s // 64) == (t // 64)
    rot = np.zeros((P, P))
    for h in (0, 64):
        for i in range(32):
            rot[h + 32 + i, h + i] = -1.0
            rot[h + i, h + 32 + i] = 1.0
    kj = np.arange(384)[None, :]
    local = np.where(np.abs(P + np.arange(P)[:, None] - kj) <= P, 0.0, -1e30)
    heads = (np.arange(P)[:, None] // GD) == (np.arange(256)[None, :] // 64)
    parts = [("ident", np.eye(P)), ("rot", rot), ("ones", np.full((P, P), 1.0 / D)),
             ("ones256", np.full((P, P), 1.0 / 256)),
             ("ones64", ((s // 64) == (t // 64)) / 64.0),
             ("cumf", (same & (s <= t)) / 16.0), ("cumb", (same & (s >= t)) / 16.0),
             ("aftf", (same & (s > t)) / 16.0), ("aftb", (same & (s < t)) / 16.0),
             ("maskf", same & (s <= t)), ("maskb", same & (s >= t)),
             ("headrows", (np.arange(P)[:, None] // GD) == np.arange(4)[None, :]),
             ("chunkrows", (np.arange(P)[:, None] // 64) == np.arange(2)[None, :]),
             ("heads", heads), ("local", local), ("pairs", same)]
    lg = np.log1p(-np.exp2(-5.0 - np.arange(8)))
    dec = np.zeros((P, 8, P))
    for h in range(8):
        dec[:, h] = np.where((s // 64) <= (t // 64), np.exp(lg[h] * np.abs(s - t)), 0.0) * HD ** -0.5
    parts.append(("dec", dec.reshape(P, 1024)))
    tile_h = lambda j: 2 * j + (np.arange(P) // 64)
    qd = np.stack([np.exp(lg[tile_h(j)][:, None] * (t + 1)) * HD ** -0.5 for j in range(4)], 1)
    parts.append(("qdec", qd.reshape(P, 512)))
    kd = np.stack([np.exp(lg[tile_h(j)][None, :] * (P - 1 - s)) for j in range(4)], 1)
    parts.append(("kdec", kd.reshape(P, 512)))
    parts.append(("gam", np.stack([np.exp(lg[tile_h(j)] * P) for j in range(4)], 1)))
    win = np.array([[2, 4], [8, 16]])
    w = np.stack([win[j][np.arange(P) // 64] for j in range(2)], 1)
    parts.append(("winv", 1.0 / w))
    cnt = np.minimum(np.arange(16)[None, None, :] + 1, w[:, :, None])
    parts.append(("cinv", (1.0 / cnt).reshape(P, 32)))
    at, cols = {}, 0
    for n, a in parts:
        at[n] = (cols, a.shape[1])
        cols += a.shape[1]
    return at, np.concatenate([np.asarray(a, np.float32) for _, a in parts], 1)


def rope_tables():
    f32 = np.float32
    r = np.repeat(np.arange(S // 64, dtype=f32), 64)
    c = np.tile(np.arange(64, dtype=f32), S // 64)
    inv = (f32(10000.0) ** (-np.arange(16, dtype=f32) / f32(16))).astype(f32)
    ang = np.concatenate([r[:, None] * inv, c[:, None] * inv], 1)
    ang = np.concatenate([ang] * 4, 1).T
    inv2 = (f32(10000.0) ** (-np.arange(32, dtype=f32) / f32(32))).astype(f32)
    ang2 = np.arange(S, dtype=f32)[:, None] * inv2[None, :]
    ang2 = np.concatenate([ang2] * 4, 1).T
    return [np.ascontiguousarray(x, dtype=f32) for x in
            (np.concatenate([np.cos(ang), np.sin(ang)], 1), np.concatenate([np.cos(ang2), np.sin(ang2)], 1))]


CONST_AT, CONSTS = masks()
NC1 = CONST_AT["dec"][0]
NCONST = CONSTS.shape[1]


def two_mixers(nc, xT, cT, w_mod, w_in1, w_out1, w_up, vec1, vec2, vec3, sinks, gla_up,
               w_in2, w_out2, w_ffn, w_down, a_ws, a_bs, b_w, const, rope1, rope2, out, upto=None, dump=None):
    place = {}
    at = [16512]

    def put(name, floats, dt=F32, where=None):
        offset = at[0] if where is None else where
        place[name] = offset
        if where is None:
            at[0] += (floats + -floats % 8) * 4
        assert offset + floats * 4 <= 229368, name
        return nc.alloc_sbuf_tensor_at(name, [P, floats], dt, offset=offset)

    raw = put("raw", 2 * 1024)
    w_hi = put("w_hi", 2 * 1024, F32R)
    w_lo = put("w_lo", 2 * 1024, F32R)
    cst = put("cst", 2224)
    v1 = put("v1", 2 * NV1)
    v2 = put("v2", 2 * NV2)
    v3 = put("v3", 16)
    nsink = put("nsink", 16)
    mod = put("mod", 2 * 48)
    csil = put("csil", 16)
    craw = put("craw", 16)
    at[0] += -at[0] % 32
    x_ = put("x", DT * T)
    x = x_[:, :].rearrange("p (j t) -> p j t", t=T)
    x2 = x_[:, 0:DT * S].rearrange("p (j t) -> p j t", t=S)
    cst2 = x_[:, DT * S:DT * T]
    body = at[0]
    h_hi_ = put("h_hi", DT * T, F32R)
    h_lo_ = put("h_lo", DT * T, F32R)
    h_hi = h_hi_[:, :].rearrange("p (j t) -> p j t", t=T)
    h_lo = h_lo_[:, :].rearrange("p (j t) -> p j t", t=T)
    work1 = at[0]
    n1 = (229368 - work1) // 4
    at[0] = body
    h2_hi_ = put("h2_hi", DT * S, F32R)
    h2_lo_ = put("h2_lo", DT * S, F32R)
    h2_hi = h2_hi_[:, :].rearrange("p (j t) -> p j t", t=S)
    h2_lo = h2_lo_[:, :].rearrange("p (j t) -> p j t", t=S)
    work2 = at[0]
    n2 = (229368 - work2) // 4
    wk1 = put("wk1", n1, where=work1)
    wk2 = put("wk2", n2, where=work2)
    gw = put("gw", 2 * DT * T, where=body)

    class Area:
        def __init__(self, tensor, start, end):
            self.t, self.at, self.end = tensor, start, end

        def take(self, n):
            self.at += n
            assert self.at <= self.end, (self.at, self.end)
            return self.t[:, self.at - n:self.at]

    def k(name):
        c, n = CONST_AT[name]
        if name in ("dec", "qdec", "kdec"):
            c -= NC1
            return cst2[:, c:c + n]
        if c > NC1:
            c -= 2048
        return cst[:, c:c + n]

    a = Area(wk1, 0, n1)
    n_t, n_h, n_sq = [a.take(T) for _ in range(2)], [a.take(T) for _ in range(2)], [a.take(T) for _ in range(2)]
    n_rs = a.take(T)
    wm = a.take(4 * 1024)
    xold1 = n_t
    a = Area(wk1, 0, n1)
    cv_sig, cv_sq, cv_rs = a.take(T), a.take(T), a.take(T)
    cv_u = [a.take(S + C + 4 * PAD) for _ in range(2)]
    cv_a = [a.take(T) for _ in range(2)]
    a = Area(wk1, 0, n1)
    at_kz = [a.take(T) for _ in range(2)]
    at_vz_ = a.take(NTT * 256)
    at_vz = at_vz_.rearrange("p (t g e) -> p t g e", g=2, e=P)
    at_raw, at_q, at_tmp = a.take(T), a.take(T), a.take(512)
    at_cs = a.take(2 * S)
    at_s = [a.take(640) for _ in range(2)]
    at_pt = [a.take(640) for _ in range(2)]
    at_col = a.take(16)
    a = Area(wk1, 0, n1)
    gl_lr, gl_q, gl_k = a.take(T), a.take(T), a.take(T)
    gl_g = [a.take(T) for _ in range(2)]
    gl_up = a.take(256)
    a = Area(gw, 0, 2 * DT * T)
    gl_v = a.take(NTT * 256).rearrange("p (t v) -> p t v", v=256)
    gl_vz_ = [a.take(512) for _ in range(2)]
    gl_qf, gl_qb, gl_kd = a.take(T), a.take(T), a.take(T)
    gl_e = a.take(768)
    gl_la = a.take(256)
    gl_x1, gl_x2 = a.take(512), a.take(256)
    gl_kz = [a.take(512) for _ in range(2)]
    gl_a = a.take(512)
    gl_kdf, gl_kdz, gl_uz = a.take(P), a.take(256), a.take(512)
    gl_s = [a.take(256) for _ in range(4)]
    gl_dec = a.take(2 * NTT)
    gl_dcol = a.take(2)
    gl_sq, gl_rs = a.take(512), a.take(512)

    a = Area(wk2, 0, n2)
    m_t, m_h, m_sq = [a.take(S) for _ in range(2)], [a.take(S) for _ in range(2)], [a.take(S) for _ in range(2)]
    m_rs = a.take(S)
    xold2 = m_t
    a = Area(wk2, 0, n2)
    sg_v = [a.take(S) for _ in range(2)]
    sg_vz_ = a.take(NBLK * 512)
    sg_vz = sg_vz_.rearrange("p (t h e) -> p t h e", h=4, e=P)
    sg_sq, sg_ws, sg_bs, sg_tmp, sg_col = a.take(256), a.take(512), a.take(256), a.take(512), a.take(8)
    po_x = [a.take(S + 16) for _ in range(2)]
    po_s = [a.take(S + 16) for _ in range(2)]
    po_p, po_w = a.take(S), a.take(256)
    a = Area(wk2, 0, n2)
    re_cs, re_raw, re_q, re_k = a.take(2 * S), a.take(S), a.take(S), a.take(S)
    re_kz = [a.take(S) for _ in range(2)]
    re_v, re_vz_ = a.take(S), a.take(2 * S)
    re_vz = re_vz_.rearrange("p (t g e) -> p t g e", g=2, e=P)
    re_kd, re_qd, re_y, re_tmp = a.take(S), a.take(S), a.take(S), a.take(512)
    re_a, re_u = a.take(S), a.take(S)
    re_sq, re_rs = a.take(512), a.take(512)
    g_n = max(f1 - f0 for f0, f1 in GROUPS)
    g_hi = put("g_hi", g_n * S, F32R, where=work2)[:, :].rearrange("p (f t) -> p f t", t=S)
    g_lo = put("g_lo", g_n * S, F32R, where=work2 + g_n * S * 4)[:, :].rearrange("p (f t) -> p f t", t=S)
    a = Area(wk2, 2 * g_n * S, n2)
    ff_up = [a.take(S + 2) for _ in range(4)]
    ff_c = [a.take(S) for _ in range(2)]

    psum = [nc.alloc_psum_tensor(f"bank{i}", [P, 512], F32) for i in range(8)]
    scratch = [nc.dram_tensor(f"residual{i}", [P, DT, S], F32, kind="Internal").ap() for i in range(3)]

    names = """raw_in0 raw_in1 params_in x_in cond_in wm_in0 wm_in1 wm_in2 wm_in3 rope_in up_in
        w_split acc_ready acc_free0 acc_free1 acc_free2
        cond_silu mod_sum mod_ready wm_used
        sq_ready sq_used ms_ready rs_ready t_ready hf_ready h_ready
        act_step dve_step pool_step
        glu_ready u_ready conv_ready mean_ready cent_ready csq_ready var_ready csd_ready cn_ready csilu_ready
        gate_ready mixc_ready pads_clear
        kv_clear raw_ready rot_ready cosm_ready rope_ready kz_ready vt_ready vn_ready vz_ready
        sc_ready sca_copied scm_ready nmax_ready exp_ready p_ready pt_ready pt0_copied pt1_copied o_ready mixa_ready
        z_ready vk_ready sp_ready la_ready cum_ready ex_ready vcopied kin_ready att_ready am_ready
        u_sum st_ready ob_ready ob_copied gvz_clear kdz_ready ub_sum sb_ready obb_ready obb_added
        gsq_ready gms_ready gsd_ready grn_ready gmix_ready proj_in
        m_tables sg_ready sg_turned sg_col_ready sg_vz_ready sg_sum sg_mixed po_in po_ready po_sum po_mixed
        re_clear re_cs_in re_raw_ready re_rot re_cos re_roped re_vt re_vt_turned re_v_in re_kt re_kd_ready re_kz_ready
        re_usum re_states re_scores re_am re_ysum re_ycopied re_mean re_cent re_sq_ready re_var re_sd re_mixed
        ff_up_ready ff_conv ff_gated ff_prod ff_hi g_ready ff_pads fin_ready
        hi_ready lo_ready xold_in0 xold_in1 res_ready store0 store1 store2 out_done""".split()
    sem = {n: nc.alloc_semaphore(n) for n in names}
    block = nc.Block()
    GLU0 = [0, 2 * len(CH_ALL)]
    layers = range(2)
    GORD = [8, 9, 0, 1, 2, 3, 4, 5, 6, 7]
    BORD = [9, 8, 7, 6, 5, 4, 3, 2, 1, 0]
    CH_OUT = [CH_ALL, CH_LAT]
    ATT = [[(j, n, g) for j in range(4) for n in range(NTT if l == 0 else NBLK) for g in range(2)] for l in layers]
    ATT0 = [0, len(ATT[0])]

    def near(n):
        lo, hi = (max(n - 1, 0), min(n + 2, NBLK)) if n < NBLK else (0, 0)
        return lo, hi, (lo - n + 1) * P

    def chunk_count(l):
        return sum(len(CH_OUT[m]) for m in range(l))

    def proj_index(l, name):
        return INDEX[("in1", l, IN1.index(name))]

    def psum_of(q):
        return psum[q % 3]

    with block:
        @block.sync
        def _(sp):
            def load_weights(g):
                kind, l, i, nk, _ = SEQ[g]
                if g >= 2:
                    sp.wait_ge(sem["w_split"], g - 1)
                src = {"in1": w_in1, "out1": w_out1, "in2": w_in2, "out2": w_out2, "up": w_ffn}.get(kind)
                if kind == "down":
                    grp, d = i
                    f0, f1 = GROUPS[grp]
                    src = w_down[l, d, :, f0 * P:f1 * P]
                else:
                    src = src[l, i]
                sp.dma_start(raw[:, (g % 2) * 1024:(g % 2) * 1024 + nk * P], src)\
                  .then_inc(sem[f"raw_in{g % 2}"], 16)

            def load_mod(l):
                for m in range(24):
                    n = 24 * l + m
                    if n >= 4:
                        sp.wait_ge(sem["wm_used"], n - 3)
                    sp.dma_start(wm[:, (n % 4) * 1024:(n % 4 + 1) * 1024], w_mod[l, m]).then_inc(sem[f"wm_in{n % 4}"], 16)

            def load_old(n, src, width, dst):
                if n >= 2:
                    sp.wait_ge(sem["res_ready"], n - 1)
                sp.dma_start(dst[n % 2][:, 0:width], src).then_inc(sem[f"xold_in{n % 2}"], 16)

            sp.dma_start(cst[:, 0:NC1], const[:, 0:NC1]).then_inc(sem["params_in"], 16)
            sp.dma_start(cst[:, NC1:NC1 + 38], const[:, NC1 + 2048:NC1 + 2086]).then_inc(sem["params_in"], 16)
            sp.dma_start(craw[:, :], cT).then_inc(sem["params_in"], 16)
            sp.dma_start(v1[:, :], vec1).then_inc(sem["params_in"], 16)
            sp.dma_start(v2[:, :], vec2).then_inc(sem["params_in"], 16)
            sp.dma_start(v3[:, :], vec3).then_inc(sem["params_in"], 16)
            sp.dma_start(nsink[:, :], sinks).then_inc(sem["params_in"], 16)
            sp.dma_start(x, xT).then_inc(sem["x_in"], 16)
            load_mod(0)
            for l in layers:
                for i, name in enumerate(IN1):
                    if name == "bk":
                        sp.wait_ge(sem["mixc_ready"], 2 * (l + 1))
                        sp.dma_start(at_cs, rope1).then_inc(sem["rope_in"], 16)
                    if name == "lr":
                        sp.wait_ge(sem["mixa_ready"], (ATT0[l] + len(ATT[l])) // 2)
                        sp.dma_start(gl_up, gla_up[l]).then_inc(sem["up_in"], 16)
                    load_weights(proj_index(l, name))
                if upto and upto[0] == "in" and upto[1] == l:
                    break
                sp.wait_ge(sem["lo_ready"], 8 * (l + 1))
                for d in range(DT):
                    load_weights(INDEX[("out1", l, d)])
                    if l == 0:
                        load_old(d, xT[:, d], T, xold1)
                    else:
                        if d == 0:
                            sp.wait_ge(sem["store0"], 16)
                        load_old(8 + d, scratch[0][:, d], S, xold1)
                if l == 0:
                    load_mod(1)
                    sp.wait_ge(sem["res_ready"], 8)
                    sp.dma_start(scratch[0], x[:, :, 0:S]).then_inc(sem["store0"], 16)
                if upto and upto[0] == "layer" and upto[1] == l:
                    break
            if not upto or upto[0] == "two":
                sp.wait_ge(sem["fin_ready"], 8)
                sp.dma_start(scratch[1], x2).then_inc(sem["store1"], 16)
                sp.dma_start(cst2, const[:, NC1:NC1 + 2048]).then_inc(sem["m_tables"], 16)
                for l in layers:
                    for i, name in enumerate(IN2):
                        if name == "sv0":
                            sp.wait_ge(sem["h_ready"], 8 * (3 + 2 * l))
                            sp.dma_start(sg_ws, a_ws[l]).then_inc(sem["m_tables"], 16)
                            sp.dma_start(sg_bs, a_bs[l]).then_inc(sem["m_tables"], 16)
                            sp.dma_start(po_w, b_w[l]).then_inc(sem["m_tables"], 16)
                        if name == "q0":
                            sp.wait_ge(sem["po_mixed"], 2 * (l + 1))
                            sp.wait_ge(sem["sg_mixed"], 2 * (l + 1))
                            sp.dma_start(re_cs, rope2).then_inc(sem["re_cs_in"], 16)
                        load_weights(INDEX[("in2", l, i)])
                    if upto and upto[1] == l:
                        break
                    sp.wait_ge(sem["lo_ready"], 16 + 8 * (l + 1))
                    if l == 0:
                        sp.wait_ge(sem["store1"], 16)
                    else:
                        sp.wait_ge(sem["store2"], 16)
                    for d in range(DT):
                        load_weights(INDEX[("out2", l, d)])
                        if d >= 2:
                            sp.wait_ge(sem["res_ready"], 16 + 16 * l + d - 1)
                        sp.dma_start(xold2[d % 2], scratch[1 + l][:, d]).then_inc(sem[f"xold_in{d % 2}"], 16)
                    for g, (f0, f1) in enumerate(GROUPS):
                        for f in range(f0, f1):
                            load_weights(INDEX[("up", l, 2 * f)])
                            load_weights(INDEX[("up", l, 2 * f + 1)])
                        for d in range(DT):
                            load_weights(INDEX[("down", l, (g, d))])
                    if l == 0:
                        sp.wait_ge(sem["res_ready"], 32)
                        sp.dma_start(scratch[2], x2).then_inc(sem["store2"], 16)
                if not upto:
                    for j in range(DT):
                        sp.wait_ge(sem["fin_ready"], 8 + j + 1)
                        sp.dma_start(out[:, j], x2[:, j]).then_inc(sem["out_done"], 16)
                    sp.wait_ge(sem["out_done"], 16 * DT)
                else:
                    sp.wait_ge(sem["re_mixed"], 8 * (upto[1] + 1))
                    sp.wait_ge(sem["store1"], 16)
                    sp.dma_start(dump, x_[:, :]).then_inc(sem["out_done"], 16)
                    sp.wait_ge(sem["out_done"], 16)
            elif upto:
                sp.wait_ge(sem["res_ready"] if upto[0] == "layer" else sem["gmix_ready"], 8 * (upto[1] + 1) if upto[0] == "layer" else 2 * (3 if upto[1] == 0 else 5))
                if upto[1] == 0 and upto[0] == "layer":
                    sp.wait_ge(sem["store0"], 16)
                sp.dma_start(dump, x).then_inc(sem["out_done"], 16)
                sp.wait_ge(sem["out_done"], 16)

        @block.tensor
        def _(pe):
            mm = nc.tensor.matmul
            ident = k("ident")

            def project(g, hi, lo):
                _, _, _, nk, chunks = SEQ[g]
                pe.wait_ge(sem["w_split"], g + 1)
                wh, wl = w_hi[:, (g % 2) * 1024:], w_lo[:, (g % 2) * 1024:]
                for ci, (t0, n) in enumerate(chunks):
                    q = FIRST_CHUNK[g] + ci
                    if q >= 3:
                        pe.wait_ge(sem[f"acc_free{q % 3}"], q // 3)
                    o = psum_of(q)[:, 0:n]
                    for kt in range(nk):
                        ws = slice(kt * P, (kt + 1) * P)
                        mm(o, wh[:, ws], hi[:, kt, t0:t0 + n], start=kt == 0, stop=False)
                        mm(o, wh[:, ws], lo[:, kt, t0:t0 + n], start=False, stop=False)
                        last = mm(o, wl[:, ws], hi[:, kt, t0:t0 + n], start=False, stop=kt == nk - 1)
                    last.then_inc(sem["acc_ready"], 1)

            def modulation(l):
                for m in range(24):
                    n = 24 * l + m
                    pe.wait_ge(sem[f"wm_in{n % 4}"], 16 * (n // 4 + 1))
                    for kt in range(8):
                        last = mm(psum[7][:, 2 * m:2 * m + 2], wm[:, (n % 4) * 1024 + kt * P:(n % 4) * 1024 + (kt + 1) * P],
                                  csil[:, 2 * kt:2 * kt + 2], start=kt == 0, stop=kt == 7)
                    last.then_inc(sem["wm_used"], 1)

            def mean_square(n, chunks, sq=n_sq):
                for j in range(DT):
                    pe.wait_ge(sem["sq_ready"], 8 * n + j + 1)
                    for ci, (t0, w) in enumerate(chunks):
                        last = mm(psum[3 + ci][:, 0:w], k("ones"), sq[j % 2][:, t0:t0 + w], start=j == 0, stop=j == 7)
                    last.then_inc(sem["sq_used"], 1)

            pe.wait_ge(sem["cond_silu"], 1)
            modulation(0)
            for l in layers:
                mean_square(l, CH_ALL)
                pe.wait_ge(sem["h_ready"], 8 * (l + 1))
                for name in IN1[:6]:
                    project(proj_index(l, name), h_hi, h_lo)
                chunks = CH_OUT[l]
                c0 = chunk_count(l)
                for j in range(2):
                    pe.wait_ge(sem["conv_ready"], 2 * l + j + 1)
                    for ci, (t0, w) in enumerate(chunks):
                        last = mm(psum[3 + ci][:, 0:w], k("ones256"), cv_a[j][:, t0:t0 + w], start=j == 0, stop=j == 1)
                last.then_inc(sem["mean_ready"], 1)
                for j in range(2):
                    pe.wait_ge(sem["csq_ready"], 2 * l + j + 1)
                    for ci, (t0, w) in enumerate(chunks):
                        last = mm(psum[3 + ci][:, 0:w], k("ones256"), cv_sq[:, t0:t0 + w], start=j == 0, stop=j == 1)
                    last.then_inc(sem["var_ready"], 1)
                project(proj_index(l, "bk"), h_hi, h_lo)

                def rotate(n):
                    pe.wait_ge(sem["raw_ready"], n + 1)
                    if n == 5 * l:
                        pe.wait_ge(sem["csd_ready"], l + 1)
                    if n % 5:
                        pe.wait_ge(sem["mixa_ready"], (ATT0[l] + (n % 5 - 1) * len(ATT[l]) // 4) // 2)
                    for ci in range(2):
                        last = mm(psum[3 + ci][:, :], k("rot"), at_raw[:, ci * 512:(ci + 1) * 512], start=True, stop=True)
                    last.then_inc(sem["rot_ready"], 1)

                rotate(5 * l)
                project(proj_index(l, "bv"), h_hi, h_lo)
                pe.wait_ge(sem["vt_ready"], l + 1)
                pe.wait_ge(sem["rope_ready"], 5 * l + 1)
                for t in range(NTT):
                    last = nc.tensor.transpose(psum[3 + t // 4][:, (t % 4) * P:(t % 4 + 1) * P], at_raw[:, t * P:(t + 1) * P], ident)
                last.then_inc(sem["vn_ready"], 1)

                def scores(i):
                    j, n, g = ATT[l][i]
                    lo, hi, _ = near(n)
                    if ATT0[l] + i > 0:
                        pe.wait_ge(sem["sca_copied"], ATT0[l] + i)
                        pe.wait_ge(sem["scm_ready"], ATT0[l] + i)
                    q = at_q[:, n * P:(n + 1) * P]
                    last = mm(psum[3][:, 0:C], q, at_kz[g][:, S:T], start=True, stop=True)
                    if hi > lo:
                        last = mm(psum[4][:, 0:(hi - lo) * P], q, at_kz[g][:, lo * P:hi * P], start=True, stop=True)
                    last.then_inc(sem["sc_ready"], 1)

                def weigh(i):
                    j, n, g = ATT[l][i]
                    lo, hi, _ = near(n)
                    s = ATT0[l] + i
                    keys = [8, 9] + list(range(lo, hi))
                    pe.wait_ge(sem["p_ready"], s + 1)
                    if s > 0:
                        pe.wait_ge(sem["pt0_copied"], s)
                        pe.wait_ge(sem["pt1_copied"], s)
                    for c in range(len(keys)):
                        last = nc.tensor.transpose(psum[5 + c // 4][:, (c % 4) * P:(c % 4 + 1) * P],
                                                   at_s[i % 2][:, c * P:(c + 1) * P], ident)
                    last.then_inc(sem["pt_ready"], 1)
                    pe.wait_ge(sem["pt0_copied"], s + 1)
                    pe.wait_ge(sem["pt1_copied"], s + 1)
                    if g == 0 and s > 0:
                        pe.wait_ge(sem["mixa_ready"], s // 2)
                    for c, kt in enumerate(keys):
                        last = mm(psum[7][:, 0:P], at_vz[:, kt, g, :], at_pt[i % 2][:, c * P:(c + 1) * P],
                                  start=g == 0 and c == 0, stop=g == 1 and c == len(keys) - 1)
                    last.then_inc(sem["o_ready"], 1)

                pe.wait_ge(sem["kz_ready"], l + 1)
                pe.wait_ge(sem["vz_ready"], l + 1)
                per = len(ATT[l]) // 4
                for j in range(4):
                    project(proj_index(l, f"q{j}"), h_hi, h_lo)
                    rotate(5 * l + 1 + j)
                    project(proj_index(l, f"bg{j}"), h_hi, h_lo)
                    pe.wait_ge(sem["rope_ready"], 5 * l + 2 + j)
                    if l == 0:
                        pe.wait_ge(sem["raw_ready"], 5 * l + 2 + j)
                    scores(j * per)
                    for i in range(j * per, (j + 1) * per):
                        if i + 1 < (j + 1) * per:
                            scores(i + 1)
                        weigh(i)
                for name in IN1[16:]:
                    project(proj_index(l, name), h_hi, h_lo)
                pe.wait_ge(sem["up_in"], 16 * (l + 1))
                pe.wait_ge(sem["proj_in"], l + 1)
                outs = l == 0
                for n, t in enumerate(GORD):
                    gt = NTT * l + n
                    ts = slice(t * P, (t + 1) * P)
                    full = outs or t < NBLK
                    if gt:
                        pe.wait_ge(sem["la_ready"], gt)
                        pe.wait_ge(sem["kin_ready"], gt)
                        pe.wait_ge(sem["vcopied"], gt)
                    mm(psum[3][:, 0:256], gl_lr[:, ts], gl_up, start=True, stop=True).then_inc(sem["z_ready"], 1)
                    nc.tensor.transpose(psum[4][:, 0:P], x[:, 6, ts], ident)
                    nc.tensor.transpose(psum[4][:, P:2 * P], x[:, 7, ts], ident)
                    nc.tensor.transpose(psum[4][:, 2 * P:3 * P], gl_k[:, ts], ident).then_inc(sem["vk_ready"], 1)
                    pe.wait_ge(sem["la_ready"], gt + 1)
                    if gt:
                        pe.wait_ge(sem["ex_ready"], gt)
                    mm(psum[5][:, 0:P], gl_la[:, 0:P], k("cumf"), start=True, stop=True)
                    mm(psum[5][:, P:2 * P], gl_la[:, P:2 * P], k("cumb"), start=True, stop=True)
                    mm(psum[5][:, 2 * P:3 * P], k("aftf"), gl_la[:, 0:P], start=True, stop=True)
                    mm(psum[5][:, 3 * P:4 * P], k("aftb"), gl_la[:, P:2 * P], start=True, stop=True).then_inc(sem["cum_ready"], 1)
                    pe.wait_ge(sem["kin_ready"], gt + 1)
                    pe.wait_ge(sem["vcopied"], gt + 1)
                    if gt:
                        pe.wait_ge(sem["am_ready"], gt)
                        pe.wait_ge(sem["st_ready"], gt)
                        pe.wait_ge(sem["ob_copied"], gt)
                    if full:
                        for h in range(4):
                            hs = slice(h * P, (h + 1) * P)
                            mm(psum[6][:, hs], gl_kz[0][:, hs], gl_qf[:, ts], start=True, stop=True)
                            last = mm(psum[7][:, hs], gl_kz[1][:, hs], gl_qb[:, ts], start=True, stop=True)
                        last.then_inc(sem["att_ready"], 1)
                    for c in range(2):
                        last = mm(psum[0][:, c * 256:(c + 1) * 256], gl_kdz[:, c * P:(c + 1) * P], gl_v[:, t, :], start=True, stop=True)
                    last.then_inc(sem["u_sum"], 1)
                    if full:
                        pe.wait_ge(sem["am_ready"], gt + 1)
                        pe.wait_ge(sem["st_ready"], gt + 1)
                        for h in range(4):
                            mm(psum[1][:, (h // 2) * P:(h // 2 + 1) * P], gl_vz_[n % 2][:, h * P:(h + 1) * P],
                               gl_a[:, h * P:(h + 1) * P], start=h == 0, stop=False, skip_group_check=True)
                        for c in range(2):
                            for j in range(2):
                                last = mm(psum[1][:, j * P + c * 64:j * P + (c + 1) * 64],
                                          gl_s[(2 * n + c) % 4][:, j * P:(j + 1) * P],
                                          gl_qf[:, t * P + c * 64:t * P + (c + 1) * 64], start=False, stop=c == 1,
                                          skip_group_check=True)
                        last.then_inc(sem["ob_ready"], 1)
                for n, t in enumerate(BORD):
                    gt = NTT * l + n
                    pe.wait_ge(sem["kdz_ready"], gt + 1)
                    if gt:
                        pe.wait_ge(sem["sb_ready"], gt)
                    for c in range(2):
                        last = mm(psum[2][:, c * 256:(c + 1) * 256], gl_kdz[:, c * P:(c + 1) * P], gl_v[:, t, :], start=True, stop=True)
                    last.then_inc(sem["ub_sum"], 1)
                    pe.wait_ge(sem["sb_ready"], gt + 1)
                    if gt:
                        pe.wait_ge(sem["obb_added"], gt)
                    if outs or t < NBLK:
                        for c in (1, 0):
                            for j in range(2):
                                last = mm(psum[3][:, j * P + c * 64:j * P + (c + 1) * 64],
                                          gl_s[(2 * n + 1 - c) % 4][:, j * P:(j + 1) * P],
                                          gl_qb[:, t * P + c * 64:t * P + (c + 1) * 64],
                                          start=(c, j) == (1, 0), stop=c == 0, skip_group_check=True)
                        last.then_inc(sem["obb_ready"], 1)
                m0 = 2 * c0
                for j in range(2):
                    for ci, (t0, w) in enumerate(chunks):
                        m = m0 + j * len(chunks) + ci
                        pe.wait_ge(sem["gsq_ready"], m + 1)
                        mm(psum[4][:, 0:w], k("ones64"), gl_sq[:, 0:w], start=True, stop=True).then_inc(sem["gms_ready"], 1)
                if upto and upto[0] == "in" and upto[1] == l:
                    return
                pe.wait_ge(sem["lo_ready"], 8 * (l + 1))
                for d in range(DT):
                    project(INDEX[("out1", l, d)], h_hi, h_lo)
                if l == 0:
                    modulation(1)
                if upto and upto[0] == "layer" and upto[1] == l:
                    return

            mean_square(2, CH_LAT, m_sq)
            for l in layers:
                mean_square(3 + 2 * l, CH_LAT, m_sq)
                nh = 8 * (3 + 2 * l)
                pe.wait_ge(sem["h_ready"], nh)
                for i in range(6):
                    project(INDEX[("in2", l, i)], h2_hi, h2_lo)
                pe.wait_ge(sem["sg_ready"], 2 * l + 2)
                for t in range(NBLK):
                    for j in range(2):
                        o = (t % 2) * 256 + j * P
                        last = nc.tensor.transpose(psum[3 + t // 2][:, o:o + P], sg_v[j][:, t * P:(t + 1) * P], ident)
                last.then_inc(sem["sg_turned"], 1)
                pe.wait_ge(sem["sg_vz_ready"], l + 1)
                for j in range(2):
                    for n in range(NBLK):
                        for h in (2 * j, 2 * j + 1):
                            last = mm(psum[3 + 2 * j + n // 4][:, (n % 4) * P:(n % 4 + 1) * P], sg_vz[:, n, h, :],
                                      sg_ws[:, h * P:(h + 1) * P], start=h % 2 == 0, stop=h % 2 == 1)
                    last.then_inc(sem["sg_sum"], 1)
                for j in range(2):
                    pe.wait_ge(sem["po_ready"], 2 * l + j + 1)
                    if j == 0:
                        pe.wait_ge(sem["sg_mixed"], 2 * (l + 1))
                    else:
                        pe.wait_ge(sem["po_mixed"], 2 * l + 1)
                    for ci in range(2):
                        last = mm(psum[3 + ci][:, :], po_w[:, j * P:(j + 1) * P], po_p[:, ci * 512:(ci + 1) * 512], start=True, stop=True)
                    last.then_inc(sem["po_sum"], 1)
                pe.wait_ge(sem["po_mixed"], 2 * (l + 1))
                for j in range(4):
                    r = 4 * l + j
                    for m, name in enumerate("qk"):
                        project(INDEX[("in2", l, IN2.index(f"{name}{j}"))], h2_hi, h2_lo)
                        pe.wait_ge(sem["re_raw_ready"], 2 * r + m + 1)
                        for ci in range(2):
                            last = mm(psum[3 + ci][:, :], k("rot"), re_raw[:, ci * 512:(ci + 1) * 512], start=True, stop=True)
                        last.then_inc(sem["re_rot"], 1)
                    project(INDEX[("in2", l, IN2.index(f"v{j}"))], h2_hi, h2_lo)
                    pe.wait_ge(sem["re_vt"], r + 1)
                    for t in range(NBLK):
                        last = nc.tensor.transpose(psum[5 + t // 4][:, (t % 4) * P:(t % 4 + 1) * P], re_raw[:, t * P:(t + 1) * P], ident)
                    last.then_inc(sem["re_vt_turned"], 1)
                    project(INDEX[("in2", l, IN2.index(f"g{j}"))], h2_hi, h2_lo)
                    pe.wait_ge(sem["re_roped"], 2 * r + 2)
                    for t in range(NBLK):
                        last = nc.tensor.transpose(psum[3 + t // 4][:, (t % 4) * P:(t % 4 + 1) * P], re_k[:, t * P:(t + 1) * P], ident)
                    last.then_inc(sem["re_kt"], 1)
                    pe.wait_ge(sem["re_kd_ready"], r + 1)
                    pe.wait_ge(sem["re_v_in"], r + 1)
                    for t in range(NBLK):
                        last = mm(psum[5 + t // 4][:, (t % 4) * P:(t % 4 + 1) * P], re_kd[:, t * P:(t + 1) * P],
                                  re_v[:, t * P:(t + 1) * P], start=True, stop=True)
                    last.then_inc(sem["re_usum"], 1)
                    pe.wait_ge(sem["re_kz_ready"], r + 1)
                    for hf in range(2):
                        m = 2 * r + hf
                        if hf:
                            pe.wait_ge(sem["re_am"], m)
                        for g in range(2):
                            for n in range(4):
                                sl = slice((4 * hf + n) * P, (4 * hf + n + 1) * P)
                                last = mm(psum[3 + g][:, n * P:(n + 1) * P], re_kz[g][:, sl], re_q[:, sl], start=True, stop=True)
                        last.then_inc(sem["re_scores"], 1)
                        pe.wait_ge(sem["re_am"], m + 1)
                        pe.wait_ge(sem["re_states"], r + 1)
                        if m:
                            pe.wait_ge(sem["re_ycopied"], m)
                        for n in range(4):
                            b = 4 * hf + n
                            o = psum[7][:, n * P:(n + 1) * P]
                            mm(o, re_vz[:, b, 0, :], re_a[:, n * P:(n + 1) * P], start=True, stop=False)
                            last = mm(o, re_vz[:, b, 1, :], re_a[:, 512 + n * P:512 + (n + 1) * P], start=False, stop=b == 0)
                            if b:
                                last = mm(o, re_u[:, (b - 1) * P:b * P], re_qd[:, b * P:(b + 1) * P], start=False, stop=True)
                        last.then_inc(sem["re_ysum"], 1)
                        pe.wait_ge(sem["re_ycopied"], m + 1)
                        ys = re_y[:, hf * 512:(hf + 1) * 512]
                        mm(psum[5][:, :], k("ones64"), ys, start=True, stop=True).then_inc(sem["re_mean"], 1)
                        pe.wait_ge(sem["re_sq_ready"], m + 1)
                        mm(psum[6][:, :], k("ones64"), re_sq, start=True, stop=True).then_inc(sem["re_var"], 1)
                    pe.wait_ge(sem["re_mixed"], 2 * r + 2)
                if upto and upto[1] == l:
                    return
                pe.wait_ge(sem["lo_ready"], 16 + 8 * (l + 1))
                for d in range(DT):
                    project(INDEX[("out2", l, d)], h2_hi, h2_lo)
                mean_square(4 + 2 * l, CH_LAT, m_sq)
                pe.wait_ge(sem["h_ready"], nh + 8)
                for g, (f0, f1) in enumerate(GROUPS):
                    for f in range(f0, f1):
                        project(INDEX[("up", l, 2 * f)], h2_hi, h2_lo)
                        project(INDEX[("up", l, 2 * f + 1)], h2_hi, h2_lo)
                    pe.wait_ge(sem["g_ready"], NF * l + f1)
                    for d in range(DT):
                        project(INDEX[("down", l, (g, d))], g_hi, g_lo)
            mean_square(7, CH_LAT, m_sq)

        @block.scalar
        def _(act):
            A = nc.scalar.activation
            steps = [0]

            def link(ins):
                steps[0] += 1
                ins.then_inc(sem["act_step"], 1)
                act.wait_ge(sem["act_step"], steps[0])

            def norm(n, xs, width, sq, rs, chunks):
                for j in range(DT):
                    if j >= 2 or n:
                        act.wait_ge(sem["sq_used"], 8 * n + j - 1 if j >= 2 else 8 * n)
                    A(sq[j % 2][:, 0:width], xs[:, j, 0:width], ACT.Square).then_inc(sem["sq_ready"], 1)
                act.wait_ge(sem["sq_used"], 8 * n + 8)
                for ci, (t0, w) in enumerate(chunks):
                    last = A(rs[:, t0:t0 + w], psum[3 + ci][:, 0:w], ACT.Sqrt, bias=EPS)
                last.then_inc(sem["ms_ready"], 1)

            def scaled(n, nh, ts, hs, width, ci_list, scale, shift):
                for j in range(DT):
                    act.wait_ge(sem["t_ready"], 8 * n + j + 1)
                    if nh or j >= 2:
                        act.wait_ge(sem["h_ready"], 8 * nh + j - 1)
                    for (t0, w, r) in ci_list:
                        last = A(hs[j % 2][:, t0:t0 + w], ts[j % 2][:, t0:t0 + w], ACT.Identity,
                                 bias=shift(j, r), scale=scale(j, r))
                    last.then_inc(sem["hf_ready"], 1)

            act.wait_ge(sem["params_in"], 112)
            A(csil[:, :], craw[:, :], ACT.Silu).then_inc(sem["cond_silu"], 1)
            act.wait_ge(sem["x_in"], 16)
            for l in layers:
                if l:
                    act.wait_ge(sem["res_ready"], 8 * l)
                norm(l, x, T, n_sq, n_rs, CH_ALL)
                act.wait_ge(sem["mod_ready"], l + 1)
                ml = lambda kind, j, r: mod[:, 48 * l + 2 * (8 * kind + j) + r:48 * l + 2 * (8 * kind + j) + r + 1]
                scaled(l, l, n_t, n_h, T, [(0, S, 0), (S, C, 1)],
                       lambda j, r: ml(1, j, r), lambda j, r: ml(0, j, r))
                chunks = CH_OUT[l]
                c0 = chunk_count(l)

                def evacuate(g, out_of, func, scale=1.0):
                    for ci, (t0, w) in enumerate(SEQ[g][4]):
                        q = FIRST_CHUNK[g] + ci
                        act.wait_ge(sem["acc_ready"], q + 1)
                        link(A(out_of(t0, w), psum_of(q)[:, 0:w], func, scale=scale))
                        act.sem_inc(sem[f"acc_free{q % 3}"], 1)

                act.wait_ge(sem["h_ready"], 8 * (l + 1))
                for j in range(2):
                    if j:
                        act.wait_ge(sem["u_ready"], 2 * l + j)
                    g = proj_index(l, f"glu{j}")
                    for ci, (t0, w) in enumerate(SEQ[g][4]):
                        q = FIRST_CHUNK[g] + ci
                        act.wait_ge(sem["acc_ready"], q + 1)
                        link(A(cv_sig[:, t0:t0 + w], psum_of(q)[:, 0:w], ACT.Sigmoid))
                        act.sem_inc(sem[f"acc_free{q % 3}"], 1)
                        act.sem_inc(sem["glu_ready"], 1)
                for j in range(2):
                    g = proj_index(l, f"gate{j}")
                    for ci, (t0, w) in enumerate(SEQ[g][4]):
                        q = FIRST_CHUNK[g] + ci
                        act.wait_ge(sem["acc_ready"], q + 1)
                        link(A(x[:, j, t0:t0 + w], psum_of(q)[:, 0:w], ACT.Silu))
                        act.sem_inc(sem[f"acc_free{q % 3}"], 1)
                act.sem_inc(sem["gate_ready"], 1)
                end = chunks[-1][0] + chunks[-1][1]
                for j in range(2):
                    act.wait_ge(sem["cent_ready"], 2 * l + j + 1)
                    if j:
                        act.wait_ge(sem["var_ready"], 2 * l + 1)
                    A(cv_sq[:, 0:end], cv_a[j][:, 0:end], ACT.Square).then_inc(sem["csq_ready"], 1)
                act.wait_ge(sem["var_ready"], 2 * l + 2)
                for ci, (t0, w) in enumerate(chunks):
                    last = A(cv_rs[:, t0:t0 + w], psum[3 + ci][:, 0:w], ACT.Sqrt, bias=EPS)
                last.then_inc(sem["csd_ready"], 1)
                for j in range(2):
                    act.wait_ge(sem["cn_ready"], 2 * l + j + 1)
                    A(cv_u[j][:, 0:end], cv_a[j][:, 0:end], ACT.Silu, scale=v1[:, l * NV1 + V1["ln_w"] + j:l * NV1 + V1["ln_w"] + j + 1],
                      bias=v1[:, l * NV1 + V1["ln_b"] + j:l * NV1 + V1["ln_b"] + j + 1]).then_inc(sem["csilu_ready"], 1)
                act.wait_ge(sem["mixc_ready"], 2 * (l + 1))
                evacuate(proj_index(l, "bk"), lambda t0, w: at_raw[:, t0:t0 + w], ACT.Copy)
                act.sem_inc(sem["raw_ready"], 1)
                act.wait_ge(sem["kz_ready"], l + 1)
                evacuate(proj_index(l, "bv"), lambda t0, w: at_raw[:, t0:t0 + w], ACT.Copy)
                act.sem_inc(sem["vt_ready"], 1)
                act.wait_ge(sem["vn_ready"], l + 1)
                act.wait_ge(sem["kv_clear"], l + 1)
                for b, (t0, t1) in enumerate([(0, 4), (4, 8), (8, 10)]):
                    src = psum[3 + b][:, 0:(t1 - t0) * P].rearrange("p (t e) -> p t e", e=P)
                    for g in range(2):
                        last = A(at_vz[:, t0:t1, g, g * HD:(g + 1) * HD], src[:, :, g * HD:(g + 1) * HD], ACT.Copy)
                last.then_inc(sem["vz_ready"], 1)
                per = len(ATT[l]) // 4

                def copy_context(i):
                    s = ATT0[l] + i
                    if i == 0 or ATT[l][i][0] != ATT[l][i - 1][0] or True:
                        act.wait_ge(sem["sc_ready"], s + 1)
                    if s >= 2:
                        act.wait_ge(sem["pt_ready"], s - 1)
                    A(at_s[i % 2][:, 0:C], psum[3][:, 0:C], ACT.Copy).then_inc(sem["sca_copied"], 1)

                def exponentials(i):
                    j, n, g = ATT[l][i]
                    s = ATT0[l] + i
                    lo, hi, _ = near(n)
                    wd = C + (hi - lo) * P
                    c = 4 * (i % 2)
                    h = 8 * l + 4 * g + j
                    act.wait_ge(sem["nmax_ready"], s + 1)
                    A(at_s[i % 2][:, 0:wd], at_s[i % 2][:, 0:wd], ACT.Exp, bias=at_col[:, c:c + 1], scale=HD ** -0.5,
                      accum_out=at_col[:, c + 1:c + 2])
                    A(at_col[:, c + 2:c + 3], nsink[:, h:h + 1], ACT.Exp, bias=at_col[:, c:c + 1], scale=-1.0)\
                        .then_inc(sem["exp_ready"], 1)

                def copy_turned(i):
                    s = ATT0[l] + i
                    j, n, g = ATT[l][i]
                    lo, hi, _ = near(n)
                    act.wait_ge(sem["pt_ready"], s + 1)
                    if s >= 2:
                        act.wait_ge(sem["o_ready"], s - 1)
                    m = min(4, 2 + hi - lo) * P
                    A(at_pt[i % 2][:, 0:m], psum[5][:, 0:m], ACT.Copy).then_inc(sem["pt0_copied"], 1)

                for j in range(4):
                    if j or l:
                        act.wait_ge(sem["rope_ready"], 5 * l + 1 + j)
                    g = proj_index(l, f"q{j}")
                    if j == 0:
                        act.wait_ge(sem["vn_ready"], l + 1)
                    evacuate(g, lambda t0, w: at_raw[:, t0:t0 + w], ACT.Copy)
                    act.sem_inc(sem["raw_ready"], 1)
                    evacuate(proj_index(l, f"bg{j}"), lambda t0, w: x[:, 2 + j, t0:t0 + w], ACT.Silu)
                    copy_context(j * per)
                    exponentials(j * per)
                    for i in range(j * per, (j + 1) * per):
                        if i + 1 < (j + 1) * per:
                            copy_context(i + 1)
                            exponentials(i + 1)
                        copy_turned(i)
                act.wait_ge(sem["mixa_ready"], (ATT0[l] + len(ATT[l])) // 2)
                evacuate(proj_index(l, "lr"), lambda t0, w: gl_lr[:, t0:t0 + w], ACT.Copy)
                link(A(gl_lr[32:33, :], cst[32:33, 0:1].broadcast_to([1, T]), ACT.Copy, scale=0.0))
                link(nc.scalar.add(gl_lr[32:33, :], gl_lr[32:33, :], 1.0))
                evacuate(proj_index(l, "cq"), lambda t0, w: gl_q[:, t0:t0 + w], ACT.Copy, scale=GD ** -0.5)
                evacuate(proj_index(l, "ck"), lambda t0, w: gl_k[:, t0:t0 + w], ACT.Copy)
                for j in range(2):
                    evacuate(proj_index(l, f"cv{j}"), lambda t0, w: x[:, 6 + j, t0:t0 + w], ACT.Copy)
                for j in range(2):
                    evacuate(proj_index(l, f"cg{j}"), lambda t0, w: gl_g[j][:, t0:t0 + w], ACT.Silu)
                act.sem_inc(sem["proj_in"], 1)
                for n, t in enumerate(GORD):
                    gt = NTT * l + n
                    act.wait_ge(sem["z_ready"], gt + 1)
                    link(A(gl_e[:, 0:256], psum[3][:, 0:256], ACT.Abs))
                    link(A(gl_e[:, 256:512], gl_e[:, 0:256], ACT.Exp, scale=-1.0))
                    if gt:
                        act.wait_ge(sem["la_ready"], gt)
                    A(gl_e[:, 512:768], gl_e[:, 256:512], ACT.Ln, bias=1.0).then_inc(sem["sp_ready"], 1)
                    act.wait_ge(sem["vk_ready"], gt + 1)
                    A(gl_v[:, t, :], psum[4][:, 0:256], ACT.Copy).then_inc(sem["vcopied"], 1)
                    act.wait_ge(sem["cum_ready"], gt + 1)
                    if gt:
                        act.wait_ge(sem["kin_ready"], gt)
                    A(gl_x1, psum[5][:, :], ACT.Exp)
                    A(gl_x2, psum[5][:, 0:256], ACT.Exp, scale=-1.0).then_inc(sem["ex_ready"], 1)
                for j in range(2):
                    for ci, (t0, w) in enumerate(chunks):
                        m = 2 * c0 + j * len(chunks) + ci
                        if j == 0 and ci == 0:
                            act.wait_ge(sem["obb_added"], NTT * (l + 1))
                        if m:
                            act.wait_ge(sem["gms_ready"], m)
                            act.wait_ge(sem["grn_ready"], m)
                        A(gl_sq[:, 0:w], x[:, 6 + j, t0:t0 + w], ACT.Square).then_inc(sem["gsq_ready"], 1)
                        act.wait_ge(sem["gms_ready"], m + 1)
                        A(gl_rs[:, 0:w], psum[4][:, 0:w], ACT.Sqrt, bias=EPS).then_inc(sem["gsd_ready"], 1)
                if upto and upto[0] == "in" and upto[1] == l:
                    return
                end = chunks[-1][0] + chunks[-1][1]
                act.wait_ge(sem["gmix_ready"], 2 * (c0 + len(chunks)))
                for j in range(DT):
                    A(h_hi[:, j, 0:end], x[:, j, 0:end], ACT.Copy).then_inc(sem["hi_ready"], 1)
                if upto and upto[0] == "layer" and upto[1] == l:
                    return

            def evacuate2(g, dst, func, scale=1.0):
                for ci, (t0, w) in enumerate(SEQ[g][4]):
                    q = FIRST_CHUNK[g] + ci
                    act.wait_ge(sem["acc_ready"], q + 1)
                    link(A(dst[:, t0:t0 + w], psum_of(q)[:, 0:w], func, scale=scale))
                    act.sem_inc(sem[f"acc_free{q % 3}"], 1)

            def final(n, base, c0):
                for j in range(DT):
                    act.wait_ge(sem["t_ready"], 8 * n + j + 1)
                    link(A(x2[:, j], m_t[j % 2], ACT.Copy, scale=v3[:, c0 + j:c0 + j + 1]))
                    act.sem_inc(sem["fin_ready"], 1)
                    act.sem_inc(sem["hf_ready"], 1)

            act.wait_ge(sem["res_ready"], 16)
            norm(2, x, S, m_sq, m_rs, CH_LAT)
            final(2, 0, 0)
            for l in layers:
                w2 = lambda name, i: v2[:, l * NV2 + V2[name] + i:l * NV2 + V2[name] + i + 1]
                if l:
                    act.wait_ge(sem["res_ready"], 32)
                norm(3 + 2 * l, x2, S, m_sq, m_rs, CH_LAT)
                scaled(3 + 2 * l, 2 + 2 * l, m_t, m_h, S, [(0, S, 0)], lambda j, r: w2("g1", j), lambda j, r: 0.0)
                act.wait_ge(sem["h_ready"], 8 * (3 + 2 * l))
                for j in range(2):
                    evacuate2(INDEX[("in2", l, j)], sg_v[j], ACT.Gelu_apprx_tanh)
                    act.sem_inc(sem["sg_ready"], 1)
                for j in range(2):
                    evacuate2(INDEX[("in2", l, 2 + j)], x2[:, j], ACT.Gelu_apprx_tanh)
                for j in range(2):
                    evacuate2(INDEX[("in2", l, 4 + j)], po_x[j][:, 16:], ACT.Copy)
                    act.sem_inc(sem["po_in"], 1)
                act.wait_ge(sem["sg_turned"], l + 1)
                for t in range(NBLK):
                    link(A(sg_sq, psum[3 + t // 2][:, (t % 2) * 256:(t % 2 + 1) * 256], ACT.Square, accum_out=sg_col[:, t:t + 1]))
                A(sg_col, sg_col, ACT.Sqrt, bias=EPS, scale=1.0 / 256).then_inc(sem["sg_col_ready"], 1)
                for j in range(2):
                    act.wait_ge(sem["po_sum"], 2 * l + j + 1)
                    for ci in range(2):
                        last = A(x2[:, 2 + j, ci * 512:(ci + 1) * 512], psum[3 + ci][:, :], ACT.Copy, scale=w2("bs", j))
                    last.then_inc(sem["po_mixed"], 1)
                act.wait_ge(sem["po_mixed"], 2 * (l + 1))
                act.wait_ge(sem["sg_mixed"], 2 * (l + 1))
                for j in range(4):
                    r = 4 * l + j
                    for m, name in enumerate("qk"):
                        if r or m:
                            act.wait_ge(sem["re_roped"], 2 * r if not m else 2 * r + 1)
                        if not m and r:
                            act.wait_ge(sem["re_vt_turned"], r)
                        evacuate2(INDEX[("in2", l, IN2.index(f"{name}{j}"))], re_raw, ACT.Copy)
                        act.sem_inc(sem["re_raw_ready"], 1)
                    act.wait_ge(sem["re_roped"], 2 * r + 2)
                    evacuate2(INDEX[("in2", l, IN2.index(f"v{j}"))], re_raw, ACT.Copy)
                    act.sem_inc(sem["re_vt"], 1)
                    act.wait_ge(sem["re_vt_turned"], r + 1)
                    act.wait_ge(sem["re_clear"], l + 1)
                    for b in range(2):
                        src = psum[5 + b][:, :].rearrange("p (t e) -> p t e", e=P)
                        A(re_v[:, b * 512:(b + 1) * 512], psum[5 + b][:, :], ACT.Copy)
                        for g in range(2):
                            last = A(re_vz[:, 4 * b:4 * b + 4, g, g * HD:(g + 1) * HD], src[:, :, g * HD:(g + 1) * HD], ACT.Copy)
                    last.then_inc(sem["re_v_in"], 1)
                    evacuate2(INDEX[("in2", l, IN2.index(f"g{j}"))], x2[:, 4 + j], ACT.Silu)
                    for hf in range(2):
                        m = 2 * r + hf
                        ys = re_y[:, hf * 512:(hf + 1) * 512]
                        act.wait_ge(sem["re_ysum"], m + 1)
                        A(ys, psum[7][:, :], ACT.Copy).then_inc(sem["re_ycopied"], 1)
                        act.wait_ge(sem["re_cent"], m + 1)
                        A(re_sq, ys, ACT.Square).then_inc(sem["re_sq_ready"], 1)
                        act.wait_ge(sem["re_var"], m + 1)
                        if m:
                            act.wait_ge(sem["re_mixed"], m)
                        A(re_rs, psum[6][:, :], ACT.Sqrt, bias=EPS).then_inc(sem["re_sd"], 1)
                if upto and upto[1] == l:
                    return
                act.wait_ge(sem["re_mixed"], 8 * (l + 1))
                for j in range(DT):
                    A(h2_hi[:, j], x2[:, j], ACT.Copy).then_inc(sem["hi_ready"], 1)
                act.wait_ge(sem["res_ready"], 24 + 16 * l)
                norm(4 + 2 * l, x2, S, m_sq, m_rs, CH_LAT)
                scaled(4 + 2 * l, 3 + 2 * l, m_t, m_h, S, [(0, S, 0)], lambda j, r: w2("g2", j), lambda j, r: 0.0)
                act.wait_ge(sem["h_ready"], 8 * (4 + 2 * l))
                act.wait_ge(sem["ff_pads"], l + 1)

                def up(f):
                    n = NF * l + f
                    if f >= 2:
                        act.wait_ge(sem["ff_conv"], n - 1)
                    for m in range(2):
                        evacuate2(INDEX[("up", l, 2 * f + m)], ff_up[2 * (f % 2) + m][:, 2:], ACT.Copy)
                    act.sem_inc(sem["ff_up_ready"], 1)

                up(0)
                for f in range(NF):
                    n = NF * l + f
                    if f + 1 < NF and not any(f + 1 == f0 for f0, _ in GROUPS):
                        up(f + 1)
                    act.wait_ge(sem["ff_conv"], n + 1)
                    A(ff_c[0], ff_c[0], ACT.Silu).then_inc(sem["ff_gated"], 1)
                    act.wait_ge(sem["ff_prod"], n + 1)
                    fi = f - max(f0 for f0, _ in GROUPS if f0 <= f)
                    A(g_hi[:, fi], ff_c[1], ACT.Copy).then_inc(sem["ff_hi"], 1)
                    if f + 1 < NF and any(f + 1 == f0 for f0, _ in GROUPS):
                        up(f + 1)
            act.wait_ge(sem["res_ready"], 48)
            norm(7, x2, S, m_sq, m_rs, CH_LAT)
            final(7, 8, 8)

        @block.vector
        def _(dve):
            V = nc.vector
            steps = [0]

            def link(ins):
                steps[0] += 1
                ins.then_inc(sem["dve_step"], 1)
                dve.wait_ge(sem["dve_step"], steps[0])

            def norm(n, xs, width, ts, rs):
                dve.wait_ge(sem["ms_ready"], n + 1)
                link(V.reciprocal(rs[:, 0:width], rs[:, 0:width]))
                for j in range(DT):
                    if j >= 2:
                        dve.wait_ge(sem["hf_ready"], 8 * n + j - 1)
                    V.tensor_tensor(ts[j % 2][:, 0:width], xs[:, j, 0:width], rs[:, 0:width], ALU.mult)\
                     .then_inc(sem["t_ready"], 1)

            def modulation(l):
                dve.wait_ge(sem["wm_used"], 24 * (l + 1))
                m = mod[:, 48 * l:48 * (l + 1)].rearrange("p (m r) -> p m r", r=2)
                b = v1[:, l * NV1 + V1["b_mod"]:l * NV1 + V1["b_mod"] + 24].unsqueeze(2).broadcast_to([P, 24, 2])
                link(V.tensor_tensor(m, psum[7][:, 0:48].rearrange("p (m r) -> p m r", r=2), b, ALU.add))
                V.tensor_scalar(mod[:, 48 * l + 16:48 * l + 32], mod[:, 48 * l + 16:48 * l + 32], 1.0, None, ALU.add)\
                 .then_inc(sem["mod_ready"], 1)

            dve.wait_ge(sem["params_in"], 112)
            dve.wait_ge(sem["x_in"], 16)
            link(V.tensor_scalar(nsink[:, :], nsink[:, :], -1.0, None, ALU.mult))
            modulation(0)
            for l in layers:
                norm(l, x, T, n_t, n_rs)
                chunks = CH_OUT[l]
                c0 = chunk_count(l)
                end = chunks[-1][0] + chunks[-1][1]
                dve.wait_ge(sem["h_ready"], 8 * (l + 1))
                for j in range(2):
                    V.memset(cv_u[j][:, 0:PAD], 0.0)
                    V.memset(cv_u[j][:, PAD + S:3 * PAD + S], 0.0)
                    V.memset(cv_u[j][:, 3 * PAD + T:4 * PAD + T], 0.0)
                vl = lambda name, i: v1[:, l * NV1 + V1[name] + i:l * NV1 + V1[name] + i + 1]
                for j in range(2):
                    g = proj_index(l, f"val{j}")
                    nq = len(SEQ[g][4])
                    for ci, (t0, w) in enumerate(SEQ[g][4]):
                        q = FIRST_CHUNK[g] + ci
                        dve.wait_ge(sem["glu_ready"], GLU0[l] + j * nq + ci + 1)
                        dve.wait_ge(sem["acc_ready"], q + 1)
                        off = PAD + t0 if t0 < S else 3 * PAD + t0
                        link(V.tensor_tensor(cv_u[j][:, off:off + w], psum_of(q)[:, 0:w], cv_sig[:, t0:t0 + w], ALU.mult))
                        dve.sem_inc(sem[f"acc_free{q % 3}"], 1)
                    dve.sem_inc(sem["u_ready"], 1)
                for j in range(2):
                    for i in range(CK):
                        for (o, u0, w) in [(0, 0, S), (S, S + 2 * PAD, C)][:1 if l else 2]:
                            src = cv_u[j][:, u0 + i:u0 + i + w]
                            dst = cv_a[j][:, o:o + w]
                            if i == 0:
                                ins = V.tensor_scalar(dst, src, vl("conv_w", 31 * j), vl("conv_b", j), ALU.mult, ALU.add)
                            else:
                                ins = V.scalar_tensor_tensor(dst, src, vl("conv_w", 31 * j + i), dst, ALU.mult, ALU.add)
                        link(ins)
                    dve.sem_inc(sem["conv_ready"], 1)
                dve.wait_ge(sem["mean_ready"], l + 1)
                for j in range(2):
                    for ci, (t0, w) in enumerate(chunks):
                        last = V.tensor_tensor(cv_a[j][:, t0:t0 + w], cv_a[j][:, t0:t0 + w], psum[3 + ci][:, 0:w], ALU.subtract)
                    link(last)
                    if j == 1:
                        for jj in range(2):
                            dve.sem_inc(sem["cent_ready"], 1)
                dve.wait_ge(sem["csd_ready"], l + 1)
                link(V.reciprocal(cv_rs[:, 0:end], cv_rs[:, 0:end]))
                for j in range(2):
                    V.tensor_tensor(cv_a[j][:, 0:end], cv_a[j][:, 0:end], cv_rs[:, 0:end], ALU.mult).then_inc(sem["cn_ready"], 1)
                for j in range(2):
                    dve.wait_ge(sem["csilu_ready"], 2 * l + j + 1)
                    dve.wait_ge(sem["gate_ready"], l + 1)
                    V.tensor_tensor(x[:, j, 0:end], x[:, j, 0:end], cv_u[j][:, 0:end], ALU.mult).then_inc(sem["mixc_ready"], 1)
                dve.wait_ge(sem["rope_in"], 16 * (l + 1))

                def rope(n, ctx):
                    dve.wait_ge(sem["rot_ready"], n + 1)
                    dve.wait_ge(sem["cosm_ready"], n + 1)
                    for ci in range(2):
                        sl = slice(ci * 512, (ci + 1) * 512)
                        link(V.tensor_tensor(at_tmp, psum[3 + ci][:, :], at_cs[:, S + ci * 512:S + (ci + 1) * 512], ALU.mult))
                        link(V.tensor_tensor(at_q[:, sl], at_q[:, sl], at_tmp, ALU.add))

                rope(5 * l, True)
                for g in range(2):
                    link(V.tensor_copy(at_kz[g][g * HD:(g + 1) * HD, :], at_q[g * HD:(g + 1) * HD, :]))
                dve.sem_inc(sem["rope_ready"], 1)
                dve.wait_ge(sem["kv_clear"], l + 1)
                dve.sem_inc(sem["kz_ready"], 1)
                per = len(ATT[l]) // 4

                def front(i):
                    j, n, g = ATT[l][i]
                    s = ATT0[l] + i
                    lo, hi, m0 = near(n)
                    wd = (hi - lo) * P
                    b = at_s[i % 2]
                    c = 4 * (i % 2)
                    dve.wait_ge(sem["sc_ready"], s + 1)
                    if s >= 2:
                        dve.wait_ge(sem["pt_ready"], s - 1)
                    if wd:
                        link(V.tensor_tensor(b[:, C:C + wd], psum[4][:, 0:wd], k("local")[:, m0:m0 + wd], ALU.add))
                    dve.sem_inc(sem["scm_ready"], 1)
                    dve.wait_ge(sem["sca_copied"], s + 1)
                    link(V.reduce_max(at_col[:, 8:9], b[:, 0:C + wd], AX))
                    if s >= 2:
                        dve.wait_ge(sem["exp_ready"], s - 1)
                    h = 8 * l + 4 * g + j
                    V.tensor_scalar(at_col[:, c:c + 1], at_col[:, 8:9], -HD ** -0.5, nsink[:, h:h + 1], ALU.mult, ALU.min)\
                     .then_inc(sem["nmax_ready"], 1)

                def back(i):
                    j, n, g = ATT[l][i]
                    s = ATT0[l] + i
                    lo, hi, m0 = near(n)
                    wd = C + (hi - lo) * P
                    b = at_s[i % 2]
                    c = 4 * (i % 2)
                    dve.wait_ge(sem["exp_ready"], s + 1)
                    link(V.tensor_tensor(at_col[:, 9:10], at_col[:, c + 1:c + 2], at_col[:, c + 2:c + 3], ALU.add))
                    link(V.reciprocal(at_col[:, 10:11], at_col[:, 9:10]))
                    V.tensor_scalar(b[:, 0:wd], b[:, 0:wd], at_col[:, 10:11], None, ALU.mult).then_inc(sem["p_ready"], 1)
                    dve.wait_ge(sem["pt_ready"], s + 1)
                    if s >= 2:
                        dve.wait_ge(sem["o_ready"], s - 1)
                    if wd > 512:
                        V.tensor_copy(at_pt[i % 2][:, 512:wd], psum[6][:, 0:wd - 512]).then_inc(sem["pt1_copied"], 1)
                    else:
                        dve.sem_inc(sem["pt1_copied"], 1)
                    if g:
                        dve.wait_ge(sem["o_ready"], s + 1)
                        m = x[:, 2 + j, n * P:(n + 1) * P]
                        V.tensor_tensor(m, psum[7][:, 0:P], m, ALU.mult).then_inc(sem["mixa_ready"], 1)

                for j in range(4):
                    rope(5 * l + 1 + j, True)
                    dve.sem_inc(sem["rope_ready"], 1)
                    front(j * per)
                    for i in range(j * per, (j + 1) * per):
                        if i + 1 < (j + 1) * per:
                            front(i + 1)
                        back(i)
                dve.wait_ge(sem["proj_in"], l + 1)
                dve.wait_ge(sem["gvz_clear"], l + 1)
                outs = l == 0
                cum = {}
                for n, t in enumerate(GORD):
                    gt = NTT * l + n
                    ts = slice(t * P, (t + 1) * P)
                    full = outs or t < NBLK
                    dve.wait_ge(sem["sp_ready"], gt + 1)
                    V.scalar_tensor_tensor(gl_la, psum[3][:, 0:256], 0.0, gl_e[:, 512:768], ALU.min, ALU.subtract)\
                     .then_inc(sem["la_ready"], 1)
                    dve.wait_ge(sem["ex_ready"], gt + 1)
                    vz = gl_vz_[n % 2].rearrange("p (h e) -> p h e", e=P)
                    dve.wait_ge(sem["vcopied"], gt + 1)
                    vn = gl_v[:, t, :].rearrange("p (h e) -> p h e", e=HD)
                    V.tensor_copy(vz[:, 0:4:2, 0:HD], vn[:, 0:4:2, :])
                    V.tensor_copy(vz[:, 1:4:2, HD:P], vn[:, 1:4:2, :])
                    V.tensor_tensor(gl_qf[:, ts], gl_q[:, ts], gl_x1[:, 0:P], ALU.mult)
                    V.tensor_tensor(gl_qb[:, ts], gl_q[:, ts], gl_x1[:, P:2 * P], ALU.mult)
                    xk = gl_x2.rearrange("p (d t) -> p d t", t=P)
                    link(V.tensor_tensor(xk, xk, gl_k[:, ts].unsqueeze(1).broadcast_to([P, 2, P]), ALU.mult))
                    for dr in range(2):
                        V.tensor_tensor(gl_kz[dr].rearrange("p (h t) -> p h t", t=P),
                                        gl_x2[:, dr * P:(dr + 1) * P].unsqueeze(1).broadcast_to([P, 4, P]),
                                        k("headrows").unsqueeze(2).broadcast_to([P, 4, P]), ALU.mult)
                    V.tensor_copy(gl_dec[:, 2 * t:2 * t + 2], gl_x1[:, P:2 * P:64])
                    V.tensor_tensor(gl_kd[:, ts], psum[4][:, 2 * P:3 * P], gl_x1[:, 3 * P:4 * P], ALU.mult)
                    link(V.tensor_tensor(gl_kdf, psum[4][:, 2 * P:3 * P], gl_x1[:, 2 * P:3 * P], ALU.mult))
                    link(V.tensor_tensor(gl_kdz.rearrange("p (c d) -> p c d", d=P), gl_kdf.unsqueeze(1).broadcast_to([P, 2, P]),
                                         k("chunkrows").unsqueeze(2).broadcast_to([P, 2, P]), ALU.mult))
                    link(V.tensor_copy(gl_dcol[:, 0:2], gl_x1[:, 63:P:64]))
                    dve.sem_inc(sem["kin_ready"], 1)
                    if full:
                        dve.wait_ge(sem["att_ready"], (NTT * l if l < 1 else NTT) + (n if outs else n - 2) + 1)
                        a3 = gl_a.rearrange("p (h t) -> p h t", t=P)
                        V.tensor_tensor(a3, psum[6][:, :].rearrange("p (h t) -> p h t", t=P),
                                        k("maskf").unsqueeze(1).broadcast_to([P, 4, P]), ALU.mult)
                        link(V.tensor_tensor(gl_kz[0].rearrange("p (h t) -> p h t", t=P), psum[7][:, :].rearrange("p (h t) -> p h t", t=P),
                                             k("maskb").unsqueeze(1).broadcast_to([P, 4, P]), ALU.mult))
                        link(V.tensor_tensor(gl_a, gl_a, gl_kz[0], ALU.add))
                    dve.sem_inc(sem["am_ready"], 1)
                    dve.wait_ge(sem["u_sum"], gt + 1)
                    link(V.tensor_tensor(gl_uz.rearrange("p (c v) -> p c v", v=256), psum[0][:, :].rearrange("p (c v) -> p c v", v=256),
                                         k("heads").unsqueeze(1).broadcast_to([P, 2, 256]), ALU.mult))
                    if n == 0:
                        link(V.memset(gl_s[0], 0.0))
                    for c in range(2):
                        ins = V.scalar_tensor_tensor(gl_s[(2 * n + c + 1) % 4], gl_s[(2 * n + c) % 4], gl_dcol[:, c:c + 1],
                                                     gl_uz[:, c * 256:(c + 1) * 256], ALU.mult, ALU.add)
                        link(ins)
                    dve.sem_inc(sem["st_ready"], 1)
                    if full:
                        dve.wait_ge(sem["ob_ready"], (NTT * l if l < 1 else NTT) + (n if outs else n - 2) + 1)
                        link(V.tensor_copy(x[:, 6:8, ts], psum[1][:, 0:256].rearrange("p (j t) -> p j t", t=P)))
                    dve.sem_inc(sem["ob_copied"], 1)
                for n, t in enumerate(BORD):
                    gt = NTT * l + n
                    ts = slice(t * P, (t + 1) * P)
                    link(V.tensor_tensor(gl_kdz.rearrange("p (c d) -> p c d", d=P), gl_kd[:, ts].unsqueeze(1).broadcast_to([P, 2, P]),
                                         k("chunkrows").unsqueeze(2).broadcast_to([P, 2, P]), ALU.mult))
                    dve.sem_inc(sem["kdz_ready"], 1)
                    dve.wait_ge(sem["ub_sum"], gt + 1)
                    link(V.tensor_tensor(gl_uz.rearrange("p (c v) -> p c v", v=256), psum[2][:, :].rearrange("p (c v) -> p c v", v=256),
                                         k("heads").unsqueeze(1).broadcast_to([P, 2, 256]), ALU.mult))
                    if n == 0:
                        link(V.memset(gl_s[0], 0.0))
                    for m, c in enumerate((1, 0)):
                        link(V.scalar_tensor_tensor(gl_s[(2 * n + m + 1) % 4], gl_s[(2 * n + m) % 4], gl_dec[:, 2 * t + c:2 * t + c + 1],
                                                    gl_uz[:, c * 256:(c + 1) * 256], ALU.mult, ALU.add))
                    dve.sem_inc(sem["sb_ready"], 1)
                    if outs or t < NBLK:
                        dve.wait_ge(sem["obb_ready"], (NTT * l if l < 1 else NTT) + (n if outs else n - 2) + 1)
                        link(V.tensor_tensor(x[:, 6:8, ts], psum[3][:, 0:256].rearrange("p (j t) -> p j t", t=P), x[:, 6:8, ts], ALU.add))
                    dve.sem_inc(sem["obb_added"], 1)
                for j in range(2):
                    for ci, (t0, w) in enumerate(chunks):
                        m = 2 * c0 + j * len(chunks) + ci
                        dve.wait_ge(sem["gsd_ready"], m + 1)
                        link(V.reciprocal(gl_rs[:, 0:w], gl_rs[:, 0:w]))
                        xs = x[:, 6 + j, t0:t0 + w]
                        link(V.tensor_tensor(xs, xs, gl_rs[:, 0:w], ALU.mult))
                        dve.sem_inc(sem["grn_ready"], 1)
                        V.scalar_tensor_tensor(xs, xs, vl("norm", j), gl_g[j][:, t0:t0 + w], ALU.mult, ALU.mult)\
                         .then_inc(sem["gmix_ready"], 1)
                if upto and upto[0] == "in" and upto[1] == l:
                    return
                dve.wait_ge(sem["gmix_ready"], 2 * (c0 + len(chunks)))
                for j in range(DT):
                    dve.wait_ge(sem["hi_ready"], 8 * l + j + 1)
                    V.tensor_tensor(h_lo[:, j, 0:end], x[:, j, 0:end], h_hi[:, j, 0:end].bitcast(F32), ALU.subtract)\
                     .then_inc(sem["lo_ready"], 1)
                for d in range(DT):
                    n = 8 * l + d
                    g = INDEX[("out1", l, d)]
                    dve.wait_ge(sem[f"xold_in{n % 2}"], 16 * (n // 2 + 1))
                    for ci, (t0, w) in enumerate(SEQ[g][4]):
                        q = FIRST_CHUNK[g] + ci
                        c = 48 * l + 2 * (16 + d) + (t0 >= S)
                        dve.wait_ge(sem["acc_ready"], q + 1)
                        link(V.scalar_tensor_tensor(x[:, d, t0:t0 + w], psum_of(q)[:, 0:w], mod[:, c:c + 1],
                                                    xold1[n % 2][:, t0:t0 + w], ALU.mult, ALU.add))
                        dve.sem_inc(sem[f"acc_free{q % 3}"], 1)
                    dve.sem_inc(sem["res_ready"], 1)
                if l == 0:
                    modulation(1)
                if upto and upto[0] == "layer" and upto[1] == l:
                    return

            norm(2, x, S, m_t, m_rs)
            for l in layers:
                w2 = lambda name, i: v2[:, l * NV2 + V2[name] + i:l * NV2 + V2[name] + i + 1]
                norm(3 + 2 * l, x2, S, m_t, m_rs)
                dve.wait_ge(sem["h_ready"], 8 * (3 + 2 * l))
                dve.wait_ge(sem["m_tables"], 16 + 48 * (l + 1))
                link(V.memset(sg_vz_, 0.0))
                link(V.memset(sg_ws.rearrange("p (h t) -> p h t", t=P)[64:P, :, 0:64], 0.0))
                for b in po_x + po_s:
                    V.memset(b[:, 0:16], 0.0)
                dve.wait_ge(sem["sg_col_ready"], l + 1)
                link(V.reciprocal(sg_col, sg_col))
                for t in range(NBLK):
                    src = psum[3 + t // 2][:, (t % 2) * 256:(t % 2 + 1) * 256].rearrange("p (h e) -> p h e", e=HD)
                    for o in range(2):
                        last = V.tensor_scalar(sg_vz[:, t, o:4:2, o * HD:(o + 1) * HD], src[:, o:4:2, :], sg_col[:, t:t + 1], None, ALU.mult)
                last.then_inc(sem["sg_vz_ready"], 1)
                for j in range(2):
                    dve.wait_ge(sem["sg_sum"], 2 * l + j + 1)
                    for hf in range(2):
                        tv = sg_tmp.rearrange("p (n t) -> p n t", t=P)
                        link(V.scalar_tensor_tensor(tv, psum[3 + 2 * j + hf][:, :].rearrange("p (n t) -> p n t", t=P), w2("vn", j),
                                                    sg_bs[:, j * P:(j + 1) * P].unsqueeze(1).broadcast_to([P, 4, P]), ALU.mult, ALU.add))
                        xs = x2[:, j, hf * 512:(hf + 1) * 512]
                        link(V.tensor_tensor(xs, xs, sg_tmp, ALU.mult))
                    dve.sem_inc(sem["sg_mixed"], 1)
                for j in range(2):
                    dve.wait_ge(sem["po_in"], 2 * l + j + 1)
                    if j:
                        dve.wait_ge(sem["po_sum"], 2 * l + j)
                    sums = [po_x[j]]
                    for d in range(2 if j == 0 else 4):
                        src, dst = sums[-1], po_s[d % 2]
                        link(V.tensor_tensor(dst[:, 16:], src[:, 16:], src[:, 16 - 2 ** d:16 - 2 ** d + S], ALU.add))
                        sums.append(dst)
                    for g in range(2):
                        rs_ = slice(g * 64, (g + 1) * 64)
                        sm = sums[-2 + g]
                        link(V.scalar_tensor_tensor(po_p[rs_, :], sm[rs_, 16:], k("winv")[rs_, j:j + 1], po_x[j][rs_, 16:], ALU.mult, ALU.subtract))
                        link(V.tensor_tensor(po_p[rs_, 0:16], sm[rs_, 16:32], k("cinv")[rs_, j * 16:(j + 1) * 16], ALU.mult))
                        link(V.tensor_tensor(po_p[rs_, 0:16], po_p[rs_, 0:16], po_x[j][rs_, 16:32], ALU.subtract))
                    dve.sem_inc(sem["po_ready"], 1)
                dve.wait_ge(sem["re_cs_in"], 16 * (l + 1))
                for j in range(4):
                    r = 4 * l + j
                    for m, dst in enumerate((re_q, re_k)):
                        dve.wait_ge(sem["re_rot"], 2 * r + m + 1)
                        dve.wait_ge(sem["re_cos"], 2 * r + m + 1)
                        for ci in range(2):
                            sl = slice(ci * 512, (ci + 1) * 512)
                            link(V.tensor_tensor(re_tmp, psum[3 + ci][:, :], re_cs[:, S + ci * 512:S + (ci + 1) * 512], ALU.mult))
                            link(V.tensor_tensor(dst[:, sl], dst[:, sl], re_tmp, ALU.add))
                        dve.sem_inc(sem["re_roped"], 1)
                    dve.wait_ge(sem["re_kt"], r + 1)
                    for b in range(2):
                        V_ = V.tensor_tensor(re_kd[:, b * 512:(b + 1) * 512].rearrange("p (t d) -> p t d", d=P),
                                             psum[3 + b][:, :].rearrange("p (t d) -> p t d", d=P),
                                             k("kdec")[:, j * P:(j + 1) * P].unsqueeze(1).broadcast_to([P, 4, P]), ALU.mult)
                    link(V_)
                    dve.sem_inc(sem["re_kd_ready"], 1)
                    dve.wait_ge(sem["re_usum"], r + 1)
                    for b in range(2):
                        V_ = V.tensor_tensor(re_u[:, b * 512:(b + 1) * 512].rearrange("p (t d) -> p t d", d=P),
                                             psum[5 + b][:, :].rearrange("p (t d) -> p t d", d=P),
                                             k("pairs").unsqueeze(1).broadcast_to([P, 4, P]), ALU.mult)
                    link(V_)
                    for n in range(1, NBLK - 1):
                        link(V.scalar_tensor_tensor(re_u[:, n * P:(n + 1) * P], re_u[:, (n - 1) * P:n * P], k("gam")[:, j:j + 1],
                                                    re_u[:, n * P:(n + 1) * P], ALU.mult, ALU.add))
                    dve.sem_inc(sem["re_states"], 1)
                    for hf in range(2):
                        m = 2 * r + hf
                        dve.wait_ge(sem["re_scores"], m + 1)
                        for g in range(2):
                            h = 2 * j + g
                            V_ = V.tensor_tensor(re_a[:, g * 512:(g + 1) * 512].rearrange("p (n t) -> p n t", t=P),
                                                 psum[3 + g][:, :].rearrange("p (n t) -> p n t", t=P),
                                                 k("dec")[:, h * P:(h + 1) * P].unsqueeze(1).broadcast_to([P, 4, P]), ALU.mult)
                        link(V_)
                        dve.sem_inc(sem["re_am"], 1)
                        ys = re_y[:, hf * 512:(hf + 1) * 512]
                        dve.wait_ge(sem["re_mean"], m + 1)
                        link(V.tensor_tensor(ys, ys, psum[5][:, :], ALU.subtract))
                        dve.sem_inc(sem["re_cent"], 1)
                        dve.wait_ge(sem["re_sd"], m + 1)
                        link(V.reciprocal(re_rs, re_rs))
                        link(V.tensor_tensor(ys, ys, re_rs, ALU.mult))
                        xs = x2[:, 4 + j, hf * 512:(hf + 1) * 512]
                        link(V.scalar_tensor_tensor(xs, ys, w2("cn", j), xs, ALU.mult, ALU.mult))
                        dve.sem_inc(sem["re_mixed"], 1)
                if upto and upto[1] == l:
                    return
                for j in range(DT):
                    dve.wait_ge(sem["hi_ready"], 16 + 8 * l + j + 1)
                    V.tensor_tensor(h2_lo[:, j], x2[:, j], h2_hi[:, j].bitcast(F32), ALU.subtract).then_inc(sem["lo_ready"], 1)
                for d in range(DT):
                    n = 16 + 8 * l + d
                    g = INDEX[("out2", l, d)]
                    dve.wait_ge(sem[f"xold_in{n % 2}"], 16 * (n // 2 + 1))
                    for ci, (t0, w) in enumerate(SEQ[g][4]):
                        q = FIRST_CHUNK[g] + ci
                        dve.wait_ge(sem["acc_ready"], q + 1)
                        link(V.tensor_tensor(x2[:, d, t0:t0 + w], psum_of(q)[:, 0:w], xold2[n % 2][:, t0:t0 + w], ALU.add))
                        dve.sem_inc(sem[f"acc_free{q % 3}"], 1)
                    dve.sem_inc(sem["res_ready"], 1)
                norm(4 + 2 * l, x2, S, m_t, m_rs)
                dve.wait_ge(sem["h_ready"], 8 * (4 + 2 * l))
                for b in ff_up:
                    link(V.memset(b[:, 0:2], 0.0))
                dve.sem_inc(sem["ff_pads"], 1)
                for gi, (f0, f1) in enumerate(GROUPS):
                    for f in range(f0, f1):
                        n = NF * l + f
                        dve.wait_ge(sem["ff_up_ready"], n + 1)
                        if f:
                            dve.wait_ge(sem["ff_hi"], n)
                        for m in range(2):
                            u, c, wi = ff_up[2 * (f % 2) + m], ff_c[m], 22 * m + f
                            link(V.tensor_scalar(c, u[:, 2:], w2("conv_w", 88 + wi), w2("conv_b", wi), ALU.mult, ALU.add))
                            link(V.scalar_tensor_tensor(c, u[:, 1:S + 1], w2("conv_w", 44 + wi), c, ALU.mult, ALU.add))
                            link(V.scalar_tensor_tensor(c, u[:, 0:S], w2("conv_w", wi), c, ALU.mult, ALU.add))
                        dve.sem_inc(sem["ff_conv"], 1)
                        dve.wait_ge(sem["ff_gated"], n + 1)
                        if f == f0 and gi:
                            dve.wait_ge(sem["acc_ready"], FIRST_CHUNK[INDEX[("down", l, (gi - 1, DT - 1))] + 1])
                        link(V.tensor_tensor(ff_c[1], ff_c[1], ff_c[0], ALU.mult))
                        dve.sem_inc(sem["ff_prod"], 1)
                        dve.wait_ge(sem["ff_hi"], n + 1)
                        link(V.tensor_tensor(g_lo[:, f - f0], ff_c[1], g_hi[:, f - f0].bitcast(F32), ALU.subtract))
                        dve.sem_inc(sem["g_ready"], 1)
                    for d in range(DT):
                        g = INDEX[("down", l, (gi, d))]
                        for ci, (t0, w) in enumerate(SEQ[g][4]):
                            q = FIRST_CHUNK[g] + ci
                            dve.wait_ge(sem["acc_ready"], q + 1)
                            link(V.tensor_tensor(x2[:, d, t0:t0 + w], psum_of(q)[:, 0:w], x2[:, d, t0:t0 + w], ALU.add))
                            dve.sem_inc(sem[f"acc_free{q % 3}"], 1)
                        if gi == len(GROUPS) - 1:
                            dve.sem_inc(sem["res_ready"], 1)
            norm(7, x2, S, m_t, m_rs)

        @block.gpsimd
        def _(pool):
            G = nc.gpsimd
            steps = [0]

            def link(ins):
                steps[0] += 1
                ins.then_inc(sem["pool_step"], 1)
                pool.wait_ge(sem["pool_step"], steps[0])

            def split_weights(g):
                kind, l, i, nk, _ = SEQ[g]
                o = (g % 2) * 1024
                sl = slice(o, o + nk * P)
                pool.wait_ge(sem[f"raw_in{g % 2}"], 16 * (g // 2 + 1))
                if g >= 2:
                    pool.wait_ge(sem["acc_ready"], FIRST_CHUNK[g - 1])
                link(G.tensor_copy(w_hi[:, sl], raw[:, sl]))
                link(G.tensor_tensor(w_lo[:, sl], raw[:, sl], w_hi[:, sl].bitcast(F32), ALU.subtract))
                pool.sem_inc(sem["w_split"], 1)

            def split_h(n, hs, hi, lo, width):
                for j in range(DT):
                    pool.wait_ge(sem["hf_ready"], 8 * n + j + 1)
                    link(G.tensor_copy(hi[:, j, 0:width], hs[j % 2][:, 0:width]))
                    link(G.tensor_tensor(lo[:, j, 0:width], hs[j % 2][:, 0:width], hi[:, j, 0:width].bitcast(F32), ALU.subtract))
                    pool.sem_inc(sem["h_ready"], 1)

            for l in layers:
                split_h(l, n_h, h_hi, h_lo, T)
                for i in range(6):
                    split_weights(proj_index(l, IN1[i]))
                split_weights(proj_index(l, "bk"))
                pool.wait_ge(sem["mixc_ready"], 2 * (l + 1))
                link(G.memset(at_kz[0][HD:P, :], 0.0))
                link(G.memset(at_kz[1][0:HD, :], 0.0))
                link(G.memset(at_vz_, 0.0))
                pool.sem_inc(sem["kv_clear"], 1)

                def cosines(n):
                    pool.wait_ge(sem["raw_ready"], n + 1)
                    pool.wait_ge(sem["rope_in"], 16 * (l + 1))
                    if n % 5:
                        if n % 5 == 1:
                            pool.wait_ge(sem["kz_ready"], l + 1)
                        else:
                            pool.wait_ge(sem["sc_ready"], ATT0[l] + (n % 5 - 1) * len(ATT[l]) // 4)
                    link(G.tensor_tensor(at_q[:, 0:S], at_raw[:, 0:S], at_cs[:, 0:S], ALU.mult))
                    link(G.tensor_copy(at_q[:, S:T], at_raw[:, S:T]))
                    pool.sem_inc(sem["cosm_ready"], 1)

                split_weights(proj_index(l, "bv"))
                cosines(5 * l)
                for j in range(4):
                    split_weights(proj_index(l, f"q{j}"))
                    split_weights(proj_index(l, f"bg{j}"))
                    cosines(5 * l + 1 + j)
                for name in IN1[16:]:
                    split_weights(proj_index(l, name))
                pool.wait_ge(sem["proj_in"], l + 1)
                for b in gl_vz_:
                    link(G.memset(b, 0.0))
                pool.sem_inc(sem["gvz_clear"], 1)
                if upto and upto[0] == "in" and upto[1] == l:
                    return
                for d in range(DT):
                    split_weights(INDEX[("out1", l, d)])
                if upto and upto[0] == "layer" and upto[1] == l:
                    return

            for l in layers:
                split_h(3 + 2 * l, m_h, h2_hi, h2_lo, S)
                for i in range(6):
                    split_weights(INDEX[("in2", l, i)])
                pool.wait_ge(sem["po_mixed"], 2 * (l + 1))
                pool.wait_ge(sem["sg_mixed"], 2 * (l + 1))
                link(G.memset(re_kz[0][HD:P, :], 0.0))
                link(G.memset(re_kz[1][0:HD, :], 0.0))
                link(G.memset(re_vz_, 0.0))
                pool.sem_inc(sem["re_clear"], 1)
                pool.wait_ge(sem["re_cs_in"], 16 * (l + 1))
                for j in range(4):
                    r = 4 * l + j
                    for m, (name, dst) in enumerate((("q", re_q), ("k", re_k))):
                        split_weights(INDEX[("in2", l, IN2.index(f"{name}{j}"))])
                        pool.wait_ge(sem["re_raw_ready"], 2 * r + m + 1)
                        if r:
                            pool.wait_ge(sem["re_ysum"], 2 * r)
                        link(G.tensor_tensor(dst, re_raw, re_cs[:, 0:S], ALU.mult))
                        pool.sem_inc(sem["re_cos"], 1)
                    split_weights(INDEX[("in2", l, IN2.index(f"v{j}"))])
                    pool.wait_ge(sem["re_roped"], 2 * r + 2)
                    for g in range(2):
                        link(G.tensor_copy(re_kz[g][g * HD:(g + 1) * HD, :], re_k[g * HD:(g + 1) * HD, :]))
                    link(G.tensor_tensor(re_qd.rearrange("p (n t) -> p n t", t=P), re_q.rearrange("p (n t) -> p n t", t=P),
                                         k("qdec")[:, j * P:(j + 1) * P].unsqueeze(1).broadcast_to([P, NBLK, P]), ALU.mult))
                    pool.sem_inc(sem["re_kz_ready"], 1)
                    split_weights(INDEX[("in2", l, IN2.index(f"g{j}"))])
                if upto and upto[1] == l:
                    return
                for d in range(DT):
                    split_weights(INDEX[("out2", l, d)])
                split_h(4 + 2 * l, m_h, h2_hi, h2_lo, S)
                for g, (f0, f1) in enumerate(GROUPS):
                    for f in range(f0, f1):
                        split_weights(INDEX[("up", l, 2 * f)])
                        split_weights(INDEX[("up", l, 2 * f + 1)])
                    for d in range(DT):
                        split_weights(INDEX[("down", l, (g, d))])


_NAMES = ["xT", "cT", "w_mod", "w_in1", "w_out1", "w_up", "vec1", "vec2", "vec3", "sinks", "gla_up",
          "w_in2", "w_out2", "w_ffn", "w_down", "a_ws", "a_bs", "b_w", "const", "rope1", "rope2"]


def lay_out(v):
    f = lambda a: np.ascontiguousarray(a, dtype=np.float32)

    def tiles(w, cols):
        w = np.asarray(w)
        out = np.zeros((w.shape[0], len(cols), P, w.shape[1] // P, P), np.float32)
        for i, c in enumerate(cols):
            out[:, i, :, :, :len(c)] = w[:, :, c].reshape(w.shape[0], -1, P, len(c)).transpose(0, 2, 1, 3)
        return out.reshape(w.shape[0], len(cols), P, -1)

    r = lambda o, n: list(range(o, o + n))
    bq, bg = 768, 768 + 512 + 256
    cb = bg + 512
    heads = lambda o, j: r(o + 64 * j, 64) + r(o + 64 * (j + 4), 64)
    cols = {"val0": r(0, P), "val1": r(P, P), "glu0": r(256, P), "glu1": r(384, P), "gate0": r(512, P), "gate1": r(640, P),
            "bk": r(bq + 512, P), "bv": r(bq + 640, P), "cq": r(cb, P), "ck": r(cb + P, P),
            "cv0": r(cb + 256, P), "cv1": r(cb + 384, P), "lr": r(cb + 512, 32), "cg0": r(cb + 544, P), "cg1": r(cb + 672, P)}
    for j in range(4):
        cols[f"q{j}"], cols[f"bg{j}"] = heads(bq, j), heads(bg, j)
    rows = r(0, 256) + sum((heads(256, j) for j in range(4)), []) + r(768, 256)
    cols2 = {"su0": r(0, P), "su1": r(P, P), "sv0": r(256, P), "sv1": r(384, P), "x0": r(512, P), "x1": r(640, P)}
    for j in range(4):
        for a, o in zip("qkvg", (768, 1280, 1792, 2304)):
            cols2[f"{a}{j}"] = r(o + P * j, P)
    per = lambda a: np.asarray(a).reshape(a.shape[:-1] + (-1, P))
    v1 = [np.concatenate([per(v["conv_w"][l]).transpose(1, 0, 2).reshape(62, P)] +
                         [per(v[n][l]) for n in ("conv_b", "conv_ln_w", "conv_ln_b", "gla_norm_w", "b_mod")]) for l in range(2)]
    v2 = [np.concatenate([per(v[n + "_2"][l]) for n in ("norm1_g", "a_vnorm_g", "b_scale", "c_norm_g", "norm2_g")] +
                         [per(v["conv_w_2"][l]).reshape(132, P), per(v["conv_b_2"][l])]) for l in range(2)]
    up = np.zeros((2, P, 256), np.float32)
    for d in range(2):
        up[:, 16 * d:16 * (d + 1), P * d:P * (d + 1)] = v["gla_w_up"][:, d]
        up[:, 32, P * d:P * (d + 1)] = v["gla_b_up"][:, d]
    tok = np.concatenate([v["x"][0], v["ctx"][0]])
    dff = NF * P
    bw = np.zeros((2, 2, P, P), np.float32)
    for g in range(4):
        o = 64 * (g % 2)
        bw[:, g // 2, o:o + 64, o:o + 64] = v["b_w_2"][:, g]
    wd = np.asarray(v["w_down_2"])
    ffn = sum(([r(f * P, P), r(dff + f * P, P)] for f in range(NF)), [])
    return {
        "xT": f(tok.T.reshape(DT, P, T).transpose(1, 0, 2)),
        "cT": f(np.stack([v["c"][0], v["c_ctx"]], -1).reshape(DT, P, 2).transpose(1, 0, 2).reshape(P, 16)),
        "w_mod": tiles(v["w_mod"], [r(P * i, P) for i in range(24)]),
        "w_in1": tiles(v["w_in"], [cols[n] for n in IN1]),
        "w_out1": tiles(np.asarray(v["w_out"])[:, rows], [r(P * i, P) for i in range(8)]),
        "w_up": f(np.zeros(1)) if False else f(up),
        "vec1": f(np.concatenate(v1).T), "vec2": f(np.concatenate(v2).T),
        "vec3": f(np.concatenate([per(v["final_norm_w"]), per(v["final_g_2"])]).T),
        "sinks": f(np.broadcast_to(np.asarray(v["attn_sink"]).reshape(1, 16), (P, 16))),
        "gla_up": f(up),
        "w_in2": tiles(v["w_in_2"], [cols2[n] for n in IN2]),
        "w_out2": tiles(v["w_out_2"], [r(P * i, P) for i in range(8)]),
        "w_ffn": tiles(v["w_up_2"], ffn),
        "w_down": f(wd.reshape(2, NF, P, DT, P).transpose(0, 3, 2, 1, 4).reshape(2, DT, P, dff)),
        "a_ws": f(np.asarray(v["a_ws_2"]).transpose(0, 3, 1, 2).reshape(2, P, 512)),
        "a_bs": f(np.asarray(v["a_bs_2"]).reshape(2, 2, 2, 1, P).repeat(64, 3).reshape(2, 2, P, P).transpose(0, 2, 1, 3).reshape(2, P, 256)),
        "b_w": f(bw.transpose(0, 2, 1, 3).reshape(2, P, 256)),
        "const": CONSTS, "rope1": rope_tables()[0], "rope2": rope_tables()[1],
    }


def kernel(**inputs):
    import concourse.bacc as bacc
    from concourse.bass_utils import run_bass_kernel_spmd as run

    arrays = lay_out(inputs)
    nc = bacc.Bacc("TRN2", target_bir_lowering=False, num_devices=1)
    args = [nc.dram_tensor(n, arrays[n].shape, F32, kind="ExternalInput").ap() for n in _NAMES]
    out = nc.dram_tensor("out", (P, DT, S), F32, kind="ExternalOutput").ap()
    two_mixers(nc, *args, out)
    r = run(nc, [{n: arrays[n] for n in _NAMES}], core_ids=[0])
    return np.ascontiguousarray(r.results[0]["out"].transpose(1, 0, 2).reshape(D, S).T)[None]
```

```python
import numpy as np
import concourse.bass as bass
from concourse import mybir
from concourse.alu_op_type import AluOpType as ALU

F32 = mybir.dt.float32
F32R = mybir.dt.float32r
ACT = mybir.ActivationFunctionType
AX = mybir.AxisListType.X

P = 128
D = 1024
DT = D // P
S, C = 1024, 256
T = S + C
CH_ALL = [(0, 512), (512, 512), (1024, 256)]
CH_LAT = CH_ALL[:2]
NBLK = S // P
NTT = T // P
CK = 31
PAD = CK // 2
HD = 64
EPS = 1e-6
GD = 32
IN1 = ["glu0", "val0", "glu1", "val1", "gate0", "gate1", "bk", "bv",
       "q0", "bg0", "q1", "bg1", "q2", "bg2", "q3", "bg3",
       "lr", "cq", "ck", "cv0", "cv1", "cg0", "cg1"]
KV1 = {"bk", "bv", "lr", "ck", "cv0", "cv1"}
IN2 = ["sv0", "sv1", "su0", "su1", "x0", "x1"] + [f"{a}{j}" for j in range(4) for a in "qkvg"]
NF = 22
GROUPS = [(0, 4), (4, 8), (8, 12), (12, 16), (16, 19), (19, 22)]
NG = 5
AFTER = {min(f1, NF - 1): g for g, (f0, f1) in enumerate(GROUPS)}
V1 = dict(conv_w=0, conv_b=62, ln_w=64, ln_b=66, norm=68, b_mod=70)
NV1 = 94
V2 = dict(g1=0, vn=8, bs=10, cn=12, g2=16, conv_w=24, conv_b=156)
NV2 = 200
NRAW, NSPL = 3, 3


def stream():
    seq = []
    for l in range(2):
        for i, n in enumerate(IN1):
            seq.append(("in1", l, i, 8, CH_ALL if l == 0 or n in KV1 else CH_LAT))
        for d in range(DT):
            seq.append(("out1", l, d, 8, CH_ALL if l == 0 else CH_LAT))
    for l in range(2):
        for i, n in enumerate(IN2):
            seq.append(("in2", l, i, 8, CH_LAT))
        for d in range(DT):
            seq.append(("out2", l, d, 8, CH_LAT))
        for f in range(NF):
            seq.append(("up", l, 2 * f, 8, CH_LAT))
            seq.append(("up", l, 2 * f + 1, 8, CH_LAT))
            if f in AFTER:
                g = AFTER[f]
                for d in range(DT):
                    seq.append(("down", l, (g, d), GROUPS[g][1] - GROUPS[g][0], CH_LAT))
    return seq


SEQ = stream()
INDEX = {e[:3]: g for g, e in enumerate(SEQ)}
FIRST_CHUNK = np.cumsum([0] + [len(e[4]) for e in SEQ]).tolist()


def masks():
    s, t = np.arange(P)[:, None], np.arange(P)[None, :]
    same = (s // 64) == (t // 64)
    rot = np.zeros((P, P))
    for h in (0, 64):
        for i in range(32):
            rot[h + 32 + i, h + i] = -1.0
            rot[h + i, h + 32 + i] = 1.0
    kj = np.arange(384)[None, :]
    local = np.where(np.abs(P + np.arange(P)[:, None] - kj) <= P, 0.0, -1e30)
    heads = (np.arange(P)[:, None] // GD) == (np.arange(256)[None, :] // 64)
    parts = [("ident", np.eye(P)), ("rot", rot), ("ones", np.full((P, P), 1.0 / D)),
             ("ones256", np.full((P, P), 1.0 / 256)),
             ("ones64", ((s // 64) == (t // 64)) / 64.0),
             ("cumf", (same & (s <= t)) / 16.0), ("cumb", (same & (s >= t)) / 16.0),
             ("aftf", (same & (s > t)) / 16.0), ("aftb", (same & (s < t)) / 16.0),
             ("maskf", same & (s <= t)), ("maskb", same & (s >= t)),
             ("headrows", (np.arange(P)[:, None] // GD) == np.arange(4)[None, :]),
             ("chunkrows", (np.arange(P)[:, None] // 64) == np.arange(2)[None, :]),
             ("heads", heads), ("local", local), ("pairs", same)]
    lg = np.log1p(-np.exp2(-5.0 - np.arange(8)))
    dec = np.zeros((P, 8, P))
    for h in range(8):
        dec[:, h] = np.where((s // 64) <= (t // 64), np.exp(lg[h] * np.abs(s - t)), 0.0) * HD ** -0.5
    parts.append(("dec", dec.reshape(P, 1024)))
    tile_h = lambda j: 2 * j + (np.arange(P) // 64)
    qd = np.stack([np.exp(lg[tile_h(j)][:, None] * (t + 1)) * HD ** -0.5 for j in range(4)], 1)
    parts.append(("qdec", qd.reshape(P, 512)))
    kd = np.stack([np.exp(lg[tile_h(j)][None, :] * (P - 1 - s)) for j in range(4)], 1)
    parts.append(("kdec", kd.reshape(P, 512)))
    parts.append(("gam", np.stack([np.exp(lg[tile_h(j)] * P) for j in range(4)], 1)))
    win = np.array([[2, 4], [8, 16]])
    w = np.stack([win[j][np.arange(P) // 64] for j in range(2)], 1)
    parts.append(("winv", 1.0 / w))
    cnt = np.minimum(np.arange(16)[None, None, :] + 1, w[:, :, None])
    parts.append(("cinv", (1.0 / cnt).reshape(P, 32)))
    at, cols = {}, 0
    for n, a in parts:
        at[n] = (cols, a.shape[1])
        cols += a.shape[1]
    return at, np.concatenate([np.asarray(a, np.float32) for _, a in parts], 1)


def rope_tables():
    f32 = np.float32
    r = np.repeat(np.arange(S // 64, dtype=f32), 64)
    c = np.tile(np.arange(64, dtype=f32), S // 64)
    inv = (f32(10000.0) ** (-np.arange(16, dtype=f32) / f32(16))).astype(f32)
    ang = np.concatenate([r[:, None] * inv, c[:, None] * inv], 1)
    ang = np.concatenate([ang] * 4, 1).T
    inv2 = (f32(10000.0) ** (-np.arange(32, dtype=f32) / f32(32))).astype(f32)
    ang2 = np.arange(S, dtype=f32)[:, None] * inv2[None, :]
    ang2 = np.concatenate([ang2] * 4, 1).T
    return [np.ascontiguousarray(x, dtype=f32) for x in
            (np.concatenate([np.cos(ang), np.sin(ang)], 1), np.concatenate([np.cos(ang2), np.sin(ang2)], 1))]


CONST_AT, CONSTS = masks()
NC1 = CONST_AT["dec"][0]
NCONST = CONSTS.shape[1]


def two_mixers(nc, xT, cT, w_mod, w_in1, w_out1, w_up, vec1, vec2, vec3, sinks, gla_up,
               w_in2, w_out2, w_ffn, w_down, a_ws, a_bs, b_w, const, rope1, rope2, out, upto=None, dump=None):
    place = {}
    at = [16512]

    def put(name, floats, dt=F32, where=None):
        offset = at[0] if where is None else where
        place[name] = offset
        if where is None:
            at[0] += (floats + -floats % 8) * 4
        assert offset + floats * 4 <= 229368, name
        return nc.alloc_sbuf_tensor_at(name, [P, floats], dt, offset=offset)

    raw = put("raw", 2 * 1024)
    w_hi = put("w_hi", 2 * 1024, F32R)
    w_lo = put("w_lo", 2 * 1024, F32R)
    cst = put("cst", 2224)
    v1 = put("v1", 2 * NV1)
    v2 = put("v2", 2 * NV2)
    v3 = put("v3", 16)
    nsink = put("nsink", 16)
    mod = put("mod", 2 * 48)
    csil = put("csil", 16)
    craw = put("craw", 16)
    at[0] += -at[0] % 32
    x_ = put("x", DT * T)
    x = x_[:, :].rearrange("p (j t) -> p j t", t=T)
    x2 = x_[:, 0:DT * S].rearrange("p (j t) -> p j t", t=S)
    cst2 = x_[:, DT * S:DT * T]
    body = at[0]
    h_hi_ = put("h_hi", DT * T, F32R)
    h_lo_ = put("h_lo", DT * T, F32R)
    h_hi = h_hi_[:, :].rearrange("p (j t) -> p j t", t=T)
    h_lo = h_lo_[:, :].rearrange("p (j t) -> p j t", t=T)
    work1 = at[0]
    n1 = (229368 - work1) // 4
    at[0] = body
    h2_hi_ = put("h2_hi", DT * S, F32R)
    h2_lo_ = put("h2_lo", DT * S, F32R)
    h2_hi = h2_hi_[:, :].rearrange("p (j t) -> p j t", t=S)
    h2_lo = h2_lo_[:, :].rearrange("p (j t) -> p j t", t=S)
    work2 = at[0]
    n2 = (229368 - work2) // 4
    wk1 = put("wk1", n1, where=work1)
    f_sq_ = put("f_sq", 2 * S, where=body)
    f_sq = [f_sq_[:, 0:S], f_sq_[:, S:2 * S]]
    wk2 = put("wk2", n2, where=work2)
    gw = put("gw", 2 * DT * T, where=body)

    class Area:
        def __init__(self, tensor, start, end):
            self.t, self.at, self.end = tensor, start, end

        def take(self, n):
            self.at += n
            assert self.at <= self.end, (self.at, self.end)
            return self.t[:, self.at - n:self.at]

    def k(name):
        c, n = CONST_AT[name]
        if name in ("dec", "qdec", "kdec"):
            c -= NC1
            return cst2[:, c:c + n]
        if c > NC1:
            c -= 2048
        return cst[:, c:c + n]

    a = Area(wk1, 0, n1)
    n_t, n_h, n_sq = [a.take(T) for _ in range(2)], [a.take(T) for _ in range(2)], [a.take(T) for _ in range(2)]
    n_rs = a.take(T)
    xold1 = n_t
    a = Area(wk1, 0, n1)
    cv_sig, cv_sq, cv_rs = a.take(T), a.take(T), a.take(T)
    cv_u = [a.take(S + C + 4 * PAD) for _ in range(2)]
    cv_a = [a.take(T) for _ in range(2)]
    a = Area(wk1, 0, n1)
    at_kz = [a.take(T) for _ in range(2)]
    at_vz_ = a.take(NTT * 256)
    at_vz = at_vz_.rearrange("p (t g e) -> p t g e", g=2, e=P)
    at_raw, at_q, at_tmp = a.take(T), a.take(T), a.take(512)
    at_cs = a.take(2 * S)
    at_s = [a.take(640) for _ in range(2)] + [x[:, 6, 0:640], x[:, 7, 0:640]]
    at_pt = [a.take(640) for _ in range(2)]
    at_col = a.take(16)
    a = Area(wk1, 0, n1)
    gl_lr, gl_q, gl_k = a.take(T), a.take(T), a.take(T)
    gl_g = [a.take(T) for _ in range(2)]
    gl_up = a.take(256)
    gl_e = a.take(2 * NTT * P)
    gl_la = a.take(2 * NTT * P)
    gl_v = gl_e.rearrange("p (t v) -> p t v", v=256)
    gl_kt = a.take(T)
    a = Area(gw, 0, 2 * DT * T)
    gl_kdz_ = a.take(NTT * 4 * P)
    gl_kdz = gl_kdz_.rearrange("p (t c r d) -> p t c r d", c=2, r=2, d=P)
    gl_qd_ = a.take(2 * T)
    gl_qd = gl_qd_.rearrange("p (r t) -> p r t", t=T)
    gl_x1 = [a.take(512) for _ in range(2)]
    gl_x2 = [a.take(256) for _ in range(2)]
    gl_kz = [a.take(1024) for _ in range(2)]
    gl_a = [a.take(512) for _ in range(2)]
    gl_tmp = a.take(512)
    gl_vz = [a.take(512) for _ in range(2)]
    gl_uz = a.take(512)
    gl_s = [a.take(256) for _ in range(6)]
    gl_dec = a.take(4 * NTT)
    gl_sq, gl_rs = gl_la, gl_e

    a = Area(wk2, 0, n2)
    m_t, m_h, m_sq = [a.take(S) for _ in range(2)], [a.take(S) for _ in range(2)], [a.take(S) for _ in range(2)]
    m_rs = a.take(S)
    xold2 = m_t
    a = Area(wk2, 0, n2)
    sg_v = [a.take(S) for _ in range(2)]
    sg_vz_ = a.take(NBLK * 512)
    sg_vz = sg_vz_.rearrange("p (t h e) -> p t h e", h=4, e=P)
    sg_sq, sg_ws, sg_bs, sg_tmp, sg_col = a.take(256), a.take(512), a.take(256), a.take(512), a.take(8)
    po_x = [a.take(S + 16) for _ in range(2)]
    po_s = [a.take(S + 16) for _ in range(2)]
    po_p, po_w = [a.take(S) for _ in range(2)], a.take(256)
    assert a.at <= n2 - 2 * S
    re_raw = [wk2[:, n2 - 2 * S:n2 - S], wk2[:, n2 - S:n2]]
    a = Area(wk2, 0, n2)
    re_cs, re_q, re_k = a.take(2 * S), a.take(S), a.take(S)
    re_kz = [a.take(S) for _ in range(2)]
    re_v, re_vz_ = a.take(S), a.take(2 * S)
    re_vz = re_vz_.rearrange("p (t g e) -> p t g e", g=2, e=P)
    re_kd, re_qd, re_y = a.take(S), a.take(S), a.take(S)
    re_a, re_u = a.take(S), a.take(S)
    re_sq, re_rs = a.take(512), a.take(512)
    assert a.at <= n2 - 2 * S
    g_n = NG
    g_hi = put("g_hi", g_n * S, F32R, where=work2)[:, :].rearrange("p (f t) -> p f t", t=S)
    g_lo = put("g_lo", g_n * S, F32R, where=work2 + g_n * S * 4)[:, :].rearrange("p (f t) -> p f t", t=S)
    a = Area(wk2, 2 * g_n * S, n2)
    ff_up = [a.take(S + 2) for _ in range(4)]
    ff_c = [a.take(S) for _ in range(2)]

    psum = [nc.alloc_psum_tensor(f"bank{i}", [P, 512], F32) for i in range(8)]
    scratch = [nc.dram_tensor(f"residual{i}", [P, DT, S], F32, kind="Internal").ap() for i in range(3)]

    names = """raw_in0 raw_in1 params_in x_in cond_in wm_in0 wm_in1 wm_in2 wm_in3 wm_in4 wm_in5 rope_in up_in
        w_split acc_ready acc_free0 acc_free1 acc_free2
        cond_silu mod_ready wm_used
        sq_ready sq_used ms_ready rs_ready t_ready hhi_ready h_ready
        act_step dve_step pool_step
        glu_ready u_ready conv_ready mean_ready cent_ready csq_ready var_ready csd_ready cn_ready csilu_ready
        gate_ready mixc_ready pads_clear
        kv_clear raw_ready rot_ready cosm_ready rope_ready kz_ready vt_ready vn_ready vz_ready
        sc_ready sca_copied scm_ready nmax_ready exp_ready p_ready pt_ready pt0_copied o_ready mixa_ready
        z_ready zabs_ready sp_ready la_ready turned v_copied kt_copied cum_ready ex_ready xk_ready kz_split kin_ready
        u_sum st_ready gvz_ready ob_ready ob_copied ub_sum sb_ready obb_ready obb_added
        gsq_ready gms_ready gsd_ready gmix_ready proj_in lr_in cv_in
        m_tables sg_ready sg_turned sg_col_ready sg_vz_ready sg_sum sg_mixed po_in po_ready po_sum po_mixed
        re_clear re_cs_in re_raw_ready re_rot re_cos re_roped re_vt re_vt_turned re_v_in re_kt re_kd_ready re_kz_ready
        re_usum re_states re_scores re_am re_ysum re_ycopied re_mean re_cent re_sq_ready re_var re_sd re_mixed
        ff_up_ready ff_conv ff_gated ff_prod ff_hi g_ready ff_pads fin_ready
        hi_ready lo_ready xold_in0 xold_in1 res_ready store0 store1 store2 out_done""".split()
    sem = {n: nc.alloc_semaphore(n) for n in names}
    block = nc.Block()
    GLU0 = [0, 2 * len(CH_ALL)]
    layers = range(2)
    GORD = [8, 9, 0, 1, 2, 3, 4, 5, 6, 7]
    BORD = [9, 8, 7, 6, 5, 4, 3, 2, 1, 0]
    CH_OUT = [CH_ALL, CH_LAT]
    ATT = [[(j, n, g) for j in range(4) for n in range(NTT if l == 0 else NBLK) for g in range(2)] for l in layers]
    ATT0 = [0, len(ATT[0])]

    def turned_banks(i):
        return (psum[5], psum[6]) if i % 2 == 0 else (psum[0], psum[1])

    def out_bank(i):
        return psum[7] if i // 2 % 2 == 0 else psum[2]

    LATE_MOD = [(0, m) for m in range(16, 24)] + [(1, m) for m in range(24)]

    def outputs(l, n):
        return n + 1 if l == 0 else NTT + max(n - 1, 0)

    def near(n):
        lo, hi = (max(n - 1, 0), min(n + 2, NBLK)) if n < NBLK else (0, 0)
        return lo, hi, (lo - n + 1) * P

    def chunk_count(l):
        return sum(len(CH_OUT[m]) for m in range(l))

    def proj_index(l, name):
        return INDEX[("in1", l, IN1.index(name))]

    def psum_of(q):
        return psum[q % 3]


    with block:
        @block.sync
        def _(sp):
            def load_weights(g):
                kind, l, i, nk, _ = SEQ[g]
                if g >= 2:
                    sp.wait_ge(sem["w_split"], g - 1)
                src = {"in1": w_in1, "out1": w_out1, "in2": w_in2, "out2": w_out2, "up": w_ffn}.get(kind)
                if kind == "down":
                    grp, d = i
                    f0, f1 = GROUPS[grp]
                    src = w_down[l, d, :, f0 * P:f1 * P]
                else:
                    src = src[l, i]
                sp.dma_start(raw[:, (g % 2) * 1024:(g % 2) * 1024 + nk * P], src)\
                  .then_inc(sem[f"raw_in{g % 2}"], 16)

            def load_late_mod(a):
                l, m = LATE_MOD[a]
                sp.wait_ge(sem["wm_used"], 16 + max(a - 5, 0))
                sp.dma_start(x[:, 2 + a % 6, 0:D], w_mod[l, m]).then_inc(sem[f"wm_in{a % 6}"], 16)

            def load_old(n, src, width, dst):
                if n >= 2:
                    sp.wait_ge(sem["res_ready"], n - 1)
                sp.dma_start(dst[n % 2][:, 0:width], src).then_inc(sem[f"xold_in{n % 2}"], 16)

            sp.dma_start(cst[:, 0:NC1], const[:, 0:NC1]).then_inc(sem["params_in"], 16)
            sp.dma_start(cst[:, NC1:NC1 + 38], const[:, NC1 + 2048:NC1 + 2086]).then_inc(sem["params_in"], 16)
            sp.dma_start(craw[:, :], cT).then_inc(sem["params_in"], 16)
            sp.dma_start(v1[:, :], vec1).then_inc(sem["params_in"], 16)
            sp.dma_start(v2[:, :], vec2).then_inc(sem["params_in"], 16)
            sp.dma_start(v3[:, :], vec3).then_inc(sem["params_in"], 16)
            sp.dma_start(nsink[:, :], sinks).then_inc(sem["params_in"], 16)
            sp.dma_start(x, xT).then_inc(sem["x_in"], 16)
            for u in range(4):
                sp.dma_start(gw[:, 4 * u * 1024:4 * (u + 1) * 1024].rearrange("p (m c) -> p m c", c=1024),
                             w_mod[0, 4 * u:4 * (u + 1)].rearrange("m p c -> p m c")).then_inc(sem[f"wm_in{u}"], 16)
            for l in layers:
                for i, name in enumerate(IN1):
                    if l == 1 and i < 2:
                        continue
                    if name == "q0":
                        sp.wait_ge(sem["mixc_ready"], 2 * (l + 1))
                        sp.dma_start(at_cs, rope1).then_inc(sem["rope_in"], 16)
                    if name == "ck":
                        sp.wait_ge(sem["mixa_ready"], (ATT0[l] + len(ATT[l])) // 2)
                        sp.dma_start(gl_up, gla_up[l]).then_inc(sem["up_in"], 16)
                    load_weights(proj_index(l, name))
                    if l == 0 and name == "gate1":
                        sp.wait_ge(sem["h_ready"], 8)
                        for a in range(len(LATE_MOD)):
                            load_late_mod(a)
                if upto and upto[0] == "in" and upto[1] == l:
                    break
                sp.wait_ge(sem["kin_ready"], NTT * (l + 1))
                for d in range(DT):
                    load_weights(INDEX[("out1", l, d)])
                    if l == 0:
                        load_old(d, xT[:, d], T, xold1)
                    else:
                        if d == 0:
                            sp.wait_ge(sem["store0"], 16)
                        load_old(8 + d, scratch[0][:, d], S, xold1)
                load_weights(proj_index(1, IN1[0]) if l == 0 else INDEX[("in2", 0, 0)])
                load_weights(proj_index(1, IN1[1]) if l == 0 else INDEX[("in2", 0, 1)])
                if l == 0:
                    sp.wait_ge(sem["res_ready"], 8)
                    sp.dma_start(scratch[0], x[:, :, 0:S]).then_inc(sem["store0"], 16)
                if upto and upto[0] == "layer" and upto[1] == l:
                    break
            if not upto or upto[0] == "two":
                sp.wait_ge(sem["fin_ready"], 8)
                sp.dma_start(scratch[1], x2).then_inc(sem["store1"], 16)
                sp.dma_start(cst2, const[:, NC1:NC1 + 2048]).then_inc(sem["m_tables"], 16)
                for l in layers:
                    for i, name in enumerate(IN2):
                        if name in ("sv0", "sv1"):
                            continue
                        if name == "su0":
                            sp.wait_ge(sem["h_ready"], 8 * (3 + 2 * l))
                            sp.dma_start(sg_ws, a_ws[l]).then_inc(sem["m_tables"], 16)
                            sp.dma_start(sg_bs, a_bs[l]).then_inc(sem["m_tables"], 16)
                            sp.dma_start(po_w, b_w[l]).then_inc(sem["m_tables"], 16)
                        if name == "g0":
                            sp.wait_ge(sem["po_mixed"], 2 * (l + 1))
                            sp.wait_ge(sem["sg_mixed"], 2 * (l + 1))
                            sp.dma_start(re_cs, rope2).then_inc(sem["re_cs_in"], 16)
                        load_weights(INDEX[("in2", l, i)])
                    if upto and upto[1] == l:
                        break
                    for d in range(DT):
                        load_weights(INDEX[("out2", l, d)])
                        if d == 0:
                            sp.wait_ge(sem["re_kz_ready"], 4 * (l + 1))
                            sp.wait_ge(sem[f"store{1 + l}"], 16)
                        if d >= 2:
                            sp.wait_ge(sem["res_ready"], 16 + 16 * l + d - 1)
                        sp.dma_start(xold2[d % 2], scratch[1 + l][:, d]).then_inc(sem[f"xold_in{d % 2}"], 16)
                    for f in range(NF):
                        load_weights(INDEX[("up", l, 2 * f)])
                        load_weights(INDEX[("up", l, 2 * f + 1)])
                        for d in range(DT if f in AFTER else 0):
                            load_weights(INDEX[("down", l, (AFTER[f], d))])
                    if l == 0:
                        load_weights(INDEX[("in2", 1, 0)])
                        load_weights(INDEX[("in2", 1, 1)])
                        sp.wait_ge(sem["res_ready"], 32)
                        sp.dma_start(scratch[2], x2).then_inc(sem["store2"], 16)
                if not upto:
                    for j in range(DT):
                        sp.wait_ge(sem["fin_ready"], 8 + j + 1)
                        sp.dma_start(out[:, j], x2[:, j]).then_inc(sem["out_done"], 16)
                    sp.wait_ge(sem["out_done"], 16 * DT)
                else:
                    sp.wait_ge(sem["re_mixed"], 8 * (upto[1] + 1))
                    sp.wait_ge(sem["store1"], 16)
                    sp.dma_start(dump, x_[:, :]).then_inc(sem["out_done"], 16)
                    sp.wait_ge(sem["out_done"], 16)
            elif upto:
                sp.wait_ge(sem["res_ready"] if upto[0] == "layer" else sem["gmix_ready"], 8 * (upto[1] + 1) if upto[0] == "layer" else 2 * (upto[1] + 1))
                if upto[1] == 0 and upto[0] == "layer":
                    sp.wait_ge(sem["store0"], 16)
                sp.dma_start(dump, x).then_inc(sem["out_done"], 16)
                sp.wait_ge(sem["out_done"], 16)

        @block.tensor
        def _(pe):
            mm = nc.tensor.matmul
            ident = k("ident")

            def row_tile(g, kt, hi, lo, ready, before):
                _, _, _, nk, chunks = SEQ[g]
                wh, wl = w_hi[:, (g % 2) * 1024:], w_lo[:, (g % 2) * 1024:]
                if kt == 0:
                    pe.wait_ge(sem["w_split"], g + 1)
                    for ci in range(len(chunks)):
                        q = FIRST_CHUNK[g] + ci
                        if q >= 3:
                            pe.wait_ge(sem[f"acc_free{q % 3}"], q // 3)
                ws = slice(kt * P, (kt + 1) * P)
                pe.wait_ge(sem[ready], before + kt + 1)
                for ci, (t0, n) in enumerate(chunks):
                    o = psum_of(FIRST_CHUNK[g] + ci)[:, 0:n]
                    mm(o, wh[:, ws], hi[:, kt, t0:t0 + n], start=kt == 0, stop=False)
                    mm(o, wh[:, ws], lo[:, kt, t0:t0 + n], start=False, stop=False)
                    last = mm(o, wl[:, ws], hi[:, kt, t0:t0 + n], start=False, stop=kt == nk - 1)
                    if kt == nk - 1:
                        last.then_inc(sem["acc_ready"], 1)

            def project_as_ready(g, hi, lo, ready, before):
                for kt in range(SEQ[g][3]):
                    row_tile(g, kt, hi, lo, ready, before)

            def project(g, hi, lo, f0=None, only=None):
                _, _, _, nk, chunks = SEQ[g]
                pe.wait_ge(sem["w_split"], g + 1)
                wh, wl = w_hi[:, (g % 2) * 1024:], w_lo[:, (g % 2) * 1024:]
                for ci, (t0, n) in enumerate(chunks):
                    if only is not None and ci != only:
                        continue
                    q = FIRST_CHUNK[g] + ci
                    if q >= 3:
                        pe.wait_ge(sem[f"acc_free{q % 3}"], q // 3)
                    o = psum_of(q)[:, 0:n]
                    for kt in range(nk):
                        ws = slice(kt * P, (kt + 1) * P)
                        at_ = kt if f0 is None else (f0 + kt) % NG
                        mm(o, wh[:, ws], hi[:, at_, t0:t0 + n], start=kt == 0, stop=False)
                        mm(o, wh[:, ws], lo[:, at_, t0:t0 + n], start=False, stop=False)
                        last = mm(o, wl[:, ws], hi[:, at_, t0:t0 + n], start=False, stop=kt == nk - 1)
                    last.then_inc(sem["acc_ready"], 1)

            def modulate(o, w):
                for kt in range(8):
                    last = mm(o, w[:, kt * P:(kt + 1) * P], csil[:, 2 * kt:2 * kt + 2], start=kt == 0, stop=kt == 7)
                last.then_inc(sem["wm_used"], 1)

            def add_square(n, j, chunks, sq):
                pe.wait_ge(sem["sq_ready"], 8 * n + j + 1)
                for ci, (t0, w) in enumerate(chunks):
                    last = mm(psum[3 + ci][:, 0:w], k("ones"), sq[j % 2][:, t0:t0 + w], start=j == 0, stop=j == 7)
                last.then_inc(sem["sq_used"], 1)

            def mean_square(n, chunks, sq):
                for j in range(DT):
                    add_square(n, j, chunks, sq)

            pe.wait_ge(sem["cond_silu"], 1)
            mean_square(0, CH_ALL, n_sq)
            for m in range(16):
                pe.wait_ge(sem[f"wm_in{m // 4}"], 16)
                modulate(psum[7][:, 2 * m:2 * m + 2], gw[:, m * 1024:(m + 1) * 1024])
            for l in layers:
                project_as_ready(proj_index(l, IN1[0]), h_hi, h_lo, "h_ready", 8 * l)
                for name in IN1[1:6]:
                    project(proj_index(l, name), h_hi, h_lo)
                chunks = CH_OUT[l]
                c0 = chunk_count(l)
                if l == 0:
                    for a in range(len(LATE_MOD)):
                        pe.wait_ge(sem[f"wm_in{a % 6}"], 16 * (a // 6 + (2 if a % 6 < 4 else 1)))
                        if a == 0:
                            pe.wait_ge(sem["mod_ready"], 1)
                        modulate(psum[7][:, 2 * a:2 * a + 2], x[:, 2 + a % 6, 0:D])
                for j in range(2):
                    pe.wait_ge(sem["conv_ready"], 2 * l + j + 1)
                    for ci, (t0, w) in enumerate(chunks):
                        last = mm(psum[3 + ci][:, 0:w], k("ones256"), cv_a[j][:, t0:t0 + w], start=j == 0, stop=j == 1)
                last.then_inc(sem["mean_ready"], 1)
                for j in range(2):
                    pe.wait_ge(sem["csq_ready"], 2 * l + j + 1)
                    for ci, (t0, w) in enumerate(chunks):
                        last = mm(psum[3 + ci][:, 0:w], k("ones256"), cv_sq[:, t0:t0 + w], start=j == 0, stop=j == 1)
                    last.then_inc(sem["var_ready"], 1)
                project(proj_index(l, "bk"), h_hi, h_lo)

                def rotate(n):
                    pe.wait_ge(sem["raw_ready"], n + 1)
                    if n == 5 * l:
                        pe.wait_ge(sem["csd_ready"], l + 1)
                    if n % 5:
                        pe.wait_ge(sem["mixa_ready"], (ATT0[l] + (n % 5 - 1) * len(ATT[l]) // 4) // 2)
                    for ci in range(2):
                        last = mm(psum[3 + ci][:, :], k("rot"), at_raw[:, ci * 512:(ci + 1) * 512], start=True, stop=True)
                    last.then_inc(sem["rot_ready"], 1)

                rotate(5 * l)
                project(proj_index(l, "bv"), h_hi, h_lo)
                pe.wait_ge(sem["vt_ready"], l + 1)
                pe.wait_ge(sem["rope_ready"], 5 * l + 1)
                for t in range(NTT):
                    last = nc.tensor.transpose(psum[3 + t // 4][:, (t % 4) * P:(t % 4 + 1) * P], at_raw[:, t * P:(t + 1) * P], ident)
                last.then_inc(sem["vn_ready"], 1)

                def scores(i):
                    j, n, g = ATT[l][i]
                    lo, hi, _ = near(n)
                    if ATT0[l] + i > 0:
                        pe.wait_ge(sem["sca_copied"], ATT0[l] + i)
                        pe.wait_ge(sem["scm_ready"], ATT0[l] + i)
                    q = at_q[:, n * P:(n + 1) * P]
                    last = mm(psum[3][:, 0:C], q, at_kz[g][:, S:T], start=True, stop=True)
                    if hi > lo:
                        last = mm(psum[4][:, 0:(hi - lo) * P], q, at_kz[g][:, lo * P:hi * P], start=True, stop=True)
                    last.then_inc(sem["sc_ready"], 1)

                def turn(i):
                    j, n, g = ATT[l][i]
                    lo, hi, _ = near(n)
                    pe.wait_ge(sem["p_ready"], ATT0[l] + i + 1)
                    for c in range(2 + hi - lo):
                        last = nc.tensor.transpose(turned_banks(i)[c // 4][:, (c % 4) * P:(c % 4 + 1) * P],
                                                   at_s[i % 4][:, c * P:(c + 1) * P], ident)
                    last.then_inc(sem["pt_ready"], 1)

                def weigh(i):
                    j, n, g = ATT[l][i]
                    lo, hi, _ = near(n)
                    s = ATT0[l] + i
                    keys = [8, 9] + list(range(lo, hi))
                    pe.wait_ge(sem["pt0_copied"], s + 1)
                    if g == 0 and s >= 4:
                        pe.wait_ge(sem["mixa_ready"], s // 2 - 1)
                    for c, kt in enumerate(keys):
                        last = mm(out_bank(i)[:, 0:P], at_vz[:, kt, g, :], at_pt[i % 2][:, c * P:(c + 1) * P],
                                  start=g == 0 and c == 0, stop=g == 1 and c == len(keys) - 1)
                    last.then_inc(sem["o_ready"], 1)

                pe.wait_ge(sem["kz_ready"], l + 1)
                pe.wait_ge(sem["vz_ready"], l + 1)
                per = len(ATT[l]) // 4
                for j in range(4):
                    project(proj_index(l, f"q{j}"), h_hi, h_lo)
                    rotate(5 * l + 1 + j)
                    project(proj_index(l, f"bg{j}"), h_hi, h_lo)
                    pe.wait_ge(sem["rope_ready"], 5 * l + 2 + j)
                    if l == 0:
                        pe.wait_ge(sem["raw_ready"], 5 * l + 2 + j)
                    i0, i1 = j * per, (j + 1) * per
                    for i in range(i0, i0 + 4):
                        scores(i)
                    for q in range(FIRST_CHUNK[proj_index(l, f"bg{j}") + 1] - 3, FIRST_CHUNK[proj_index(l, f"bg{j}") + 1]):
                        pe.wait_ge(sem[f"acc_free{q % 3}"], q // 3 + 1)
                    for i in range(i0, i1):
                        turn(i)
                        if i > i0:
                            weigh(i - 1)
                        if i + 4 < i1:
                            scores(i + 4)
                    weigh(i1 - 1)
                    pe.wait_ge(sem["mixa_ready"], (ATT0[l] + i1) // 2)
                project(proj_index(l, "lr"), h_hi, h_lo)
                project(proj_index(l, "cq"), h_hi, h_lo)
                pe.wait_ge(sem["up_in"], 16 * (l + 1))
                pe.wait_ge(sem["mixa_ready"], (ATT0[l] + len(ATT[l])) // 2)
                pe.wait_ge(sem["lr_in"], l + 1)
                for t in range(NTT):
                    mm(psum[3 + t // 2][:, (t % 2) * 256:(t % 2 + 1) * 256], gl_lr[:, t * P:(t + 1) * P], gl_up,
                       start=True, stop=True).then_inc(sem["z_ready"], 1)
                for name in ("ck", "cv0", "cv1"):
                    project(proj_index(l, name), h_hi, h_lo)
                project(proj_index(l, "cg0"), h_hi, h_lo)
                pe.wait_ge(sem["cv_in"], l + 1)
                pe.wait_ge(sem["sp_ready"], l + 1)
                pe.wait_ge(sem["la_ready"], l + 1)
                for t in range(NTT):
                    ts = slice(t * P, (t + 1) * P)
                    b = psum[3 + t % 5]
                    if t >= 5:
                        pe.wait_ge(sem["v_copied"], NTT * l + t - 4)
                        pe.wait_ge(sem["kt_copied"], NTT * l + t - 4)
                    nc.tensor.transpose(b[:, 0:P], x[:, 6, ts], ident)
                    nc.tensor.transpose(b[:, P:2 * P], x[:, 7, ts], ident)
                    nc.tensor.transpose(b[:, 2 * P:3 * P], gl_k[:, ts], ident).then_inc(sem["turned"], 1)
                project(proj_index(l, "cg1"), h_hi, h_lo)
                outs = l == 0

                def sums(n):
                    ts = slice(GORD[n] * 256, GORD[n] * 256 + 256)
                    la = gl_la[:, ts]
                    if n:
                        pe.wait_ge(sem["ex_ready"], NTT * l + n)
                    mm(psum[5][:, 0:P], la[:, 0:P], k("cumf"), start=True, stop=True)
                    mm(psum[5][:, P:2 * P], la[:, P:2 * P], k("cumb"), start=True, stop=True)
                    mm(psum[5][:, 2 * P:3 * P], k("aftf"), la[:, 0:P], start=True, stop=True)
                    mm(psum[5][:, 3 * P:4 * P], k("aftb"), la[:, P:2 * P], start=True, stop=True).then_inc(sem["cum_ready"], 1)

                def within(n):
                    t, gt = GORD[n], NTT * l + n
                    pe.wait_ge(sem["kin_ready"], gt + 1)
                    if n >= 2:
                        pe.wait_ge(sem["st_ready"], gt - 1)
                    if outs or t < NBLK:
                        pe.wait_ge(sem["kz_split"], outputs(l, n))
                        bf, bb = (6, 7) if n % 2 == 0 else (3, 4)
                        for h in range(4):
                            hs = slice(h * P, (h + 1) * P)
                            mm(psum[bf][:, hs], gl_kz[n % 2][:, hs], gl_qd[:, 0, t * P:(t + 1) * P], start=True, stop=True)
                            mm(psum[bb][:, hs], gl_kz[n % 2][:, 512 + h * P:512 + (h + 1) * P], gl_qd[:, 1, t * P:(t + 1) * P],
                               start=True, stop=True)
                    for c in range(2):
                        last = mm(psum[2 * (n % 2)][:, c * 256:(c + 1) * 256], gl_kdz[:, t, c, 0, :], gl_v[:, t, :], start=True, stop=True)
                    last.then_inc(sem["u_sum"], 1)

                def output(n):
                    t, gt = GORD[n], NTT * l + n
                    if not (outs or t < NBLK):
                        return
                    pe.wait_ge(sem["st_ready"], gt + 1)
                    pe.wait_ge(sem["gvz_ready"], outputs(l, n))
                    if outputs(l, n) > 1:
                        pe.wait_ge(sem["ob_copied"], outputs(l, n) - 1)
                    for h in range(4):
                        mm(psum[1][:, (h // 2) * P:(h // 2 + 1) * P], gl_vz[n % 2][:, h * P:(h + 1) * P],
                           gl_a[n % 2][:, h * P:(h + 1) * P], start=h == 0, stop=False, skip_group_check=True)
                    for c in range(2):
                        for j in range(2):
                            last = mm(psum[1][:, j * P + c * 64:j * P + (c + 1) * 64], gl_s[(2 * n + c) % 6][:, j * P:(j + 1) * P],
                                      gl_qd[:, 0, t * P + c * 64:t * P + (c + 1) * 64], start=False, stop=c == 1,
                                      skip_group_check=True)
                    last.then_inc(sem["ob_ready"], 1)

                pe.wait_ge(sem["proj_in"], l + 1)
                pe.wait_ge(sem["kt_copied"], NTT * (l + 1))
                sums(0)
                sums(1)
                within(0)
                for n in range(NTT):
                    if n + 2 < NTT:
                        sums(n + 2)
                    if n + 1 < NTT:
                        within(n + 1)
                    output(n)

                def update_back(n):
                    t, gt = BORD[n], NTT * l + n
                    if n >= 2:
                        pe.wait_ge(sem["sb_ready"], gt - 1)
                    for c in range(2):
                        last = mm(psum[3 + n % 2][:, c * 256:(c + 1) * 256], gl_kdz[:, t, c, 1, :], gl_v[:, t, :], start=True, stop=True)
                    last.then_inc(sem["ub_sum"], 1)

                pe.wait_ge(sem["st_ready"], NTT * (l + 1))
                update_back(0)
                update_back(1)
                for n, t in enumerate(BORD):
                    gt = NTT * l + n
                    pe.wait_ge(sem["sb_ready"], gt + 1)
                    if outs or t < NBLK:
                        if n >= 2:
                            pe.wait_ge(sem["obb_added"], outputs(l, n) - 2)
                        for c in (1, 0):
                            for j in range(2):
                                last = mm(psum[5 + n % 2][:, j * P + c * 64:j * P + (c + 1) * 64],
                                          gl_s[(2 * n + 1 - c) % 6][:, j * P:(j + 1) * P],
                                          gl_qd[:, 1, t * P + c * 64:t * P + (c + 1) * 64],
                                          start=(c, j) == (1, 0), stop=c == 0, skip_group_check=True)
                        last.then_inc(sem["obb_ready"], 1)
                    if n + 2 < NTT:
                        update_back(n + 2)
                pe.wait_ge(sem["gsq_ready"], l + 1)
                for j in range(2):
                    for ci, (t0, w) in enumerate(chunks):
                        b, o = [(3, 0), (4, 0), (5, 0)][ci] if j == 0 else [(6, 0), (7, 0), (5, 256)][ci]
                        last = mm(psum[b][:, o:o + w], k("ones64"), gl_sq[:, j * T + t0:j * T + t0 + w], start=True, stop=True)
                last.then_inc(sem["gms_ready"], 1)
                if upto and upto[0] == "in" and upto[1] == l:
                    return
                project_as_ready(INDEX[("out1", l, 0)], h_hi, h_lo, "lo_ready", 8 * l)
                for d in range(1, DT):
                    project(INDEX[("out1", l, d)], h_hi, h_lo)
                    add_square(1 + l, d - 1, chunks, n_sq)
                add_square(1 + l, DT - 1, chunks, n_sq)
                if upto and upto[0] == "layer" and upto[1] == l:
                    return

            mean_square(3, CH_LAT, m_sq)
            for l in layers:
                nh = 8 * (3 + 2 * l)
                project_as_ready(INDEX[("in2", l, 0)], h2_hi, h2_lo, "h_ready", nh - 8)
                for i in range(1, 6):
                    project(INDEX[("in2", l, i)], h2_hi, h2_lo)
                pe.wait_ge(sem["sg_ready"], 2 * l + 2)
                for t in range(NBLK):
                    for j in range(2):
                        o = (t % 2) * 256 + j * P
                        last = nc.tensor.transpose(psum[3 + t // 2][:, o:o + P], sg_v[j][:, t * P:(t + 1) * P], ident)
                last.then_inc(sem["sg_turned"], 1)
                project(INDEX[("in2", l, IN2.index("q0"))], h2_hi, h2_lo)
                pe.wait_ge(sem["sg_vz_ready"], l + 1)
                for j in range(2):
                    for n in range(NBLK):
                        for h in (2 * j, 2 * j + 1):
                            last = mm(psum[3 + 2 * j + n // 4][:, (n % 4) * P:(n % 4 + 1) * P], sg_vz[:, n, h, :],
                                      sg_ws[:, h * P:(h + 1) * P], start=h % 2 == 0, stop=h % 2 == 1)
                    last.then_inc(sem["sg_sum"], 1)
                project(INDEX[("in2", l, IN2.index("k0"))], h2_hi, h2_lo)
                for j in range(2):
                    pe.wait_ge(sem["po_ready"], 2 * l + j + 1)
                    if j == 0:
                        pe.wait_ge(sem["sg_mixed"], 2 * (l + 1))
                    else:
                        pe.wait_ge(sem["po_mixed"], 2 * l + 1)
                    for ci in range(2):
                        last = mm(psum[3 + ci][:, :], po_w[:, j * P:(j + 1) * P], po_p[j][:, ci * 512:(ci + 1) * 512], start=True, stop=True)
                    last.then_inc(sem["po_sum"], 1)
                pe.wait_ge(sem["po_mixed"], 2 * (l + 1))
                def part(name, ci):
                    if name[1] != "4":
                        project(INDEX[("in2", l, IN2.index(name))], h2_hi, h2_lo, only=ci)
                    else:
                        row_tile(INDEX[("out2", l, 0)], ci + 2 * (name[0] == "k"), h2_hi, h2_lo, "lo_ready", 16 + 8 * l)

                def rotate2(r, m):
                    pe.wait_ge(sem["re_raw_ready"], 2 * r + m + 1)
                    for ci in range(2):
                        last = mm(psum[3 + 2 * m + ci][:, :], k("rot"), re_raw[m][:, ci * 512:(ci + 1) * 512], start=True, stop=True)
                    last.then_inc(sem["re_rot"], 1)

                def turn2(b0, src, signal):
                    for t in range(NBLK):
                        last = nc.tensor.transpose(psum[b0 + t // 4][:, (t % 4) * P:(t % 4 + 1) * P], src[:, t * P:(t + 1) * P], ident)
                    last.then_inc(sem[signal], 1)

                def scores2(m):
                    for g in range(2):
                        for n in range(4):
                            sl = slice((4 * (m % 2) + n) * P, (4 * (m % 2) + n + 1) * P)
                            last = mm(psum[3 + g][:, n * P:(n + 1) * P], re_kz[g][:, sl], re_q[:, sl], start=True, stop=True)
                    last.then_inc(sem["re_scores"], 1)

                def output2(m):
                    pe.wait_ge(sem["re_am"], m + 1)
                    pe.wait_ge(sem["re_states"], m // 2 + 1)
                    if m:
                        pe.wait_ge(sem["re_ycopied"], m)
                    for n in range(4):
                        b = 4 * (m % 2) + n
                        o = psum[7][:, n * P:(n + 1) * P]
                        mm(o, re_vz[:, b, 0, :], re_a[:, n * P:(n + 1) * P], start=True, stop=False)
                        last = mm(o, re_vz[:, b, 1, :], re_a[:, 512 + n * P:512 + (n + 1) * P], start=False, stop=b == 0)
                        if b:
                            last = mm(o, re_u[:, (b - 1) * P:b * P], re_qd[:, b * P:(b + 1) * P], start=False, stop=True)
                    last.then_inc(sem["re_ysum"], 1)

                def mean2(m):
                    pe.wait_ge(sem["re_ycopied"], m + 1)
                    if m % 2:
                        pe.wait_ge(sem["re_cent"], m)
                    mm(psum[5][:, :], k("ones64"), re_y[:, (m % 2) * 512:(m % 2 + 1) * 512], start=True, stop=True).then_inc(sem["re_mean"], 1)

                def variance2(m):
                    pe.wait_ge(sem["re_sq_ready"], m + 1)
                    if m % 2:
                        pe.wait_ge(sem["re_sd"], m)
                    mm(psum[6][:, :], k("ones64"), re_sq, start=True, stop=True).then_inc(sem["re_var"], 1)

                for j in range(4):
                    r = 4 * l + j
                    if r:
                        pe.wait_ge(sem["re_am"], 2 * r)
                    rotate2(r, 0)
                    if r:
                        pe.wait_ge(sem["re_cent"], 2 * r)
                        pe.wait_ge(sem["re_sd"], 2 * r)
                    rotate2(r, 1)
                    part(f"v{j}", 0)
                    part(f"v{j}", 1)
                    part(f"g{j}", 0)
                    pe.wait_ge(sem["re_vt"], r + 1)
                    pe.wait_ge(sem["re_roped"], 2 * r + 1)
                    turn2(3, re_raw[0], "re_vt_turned")
                    pe.wait_ge(sem["re_roped"], 2 * r + 2)
                    turn2(5, re_k, "re_kt")
                    part(f"g{j}", 1)
                    pe.wait_ge(sem["re_kd_ready"], r + 1)
                    pe.wait_ge(sem["re_v_in"], r + 1)
                    for t in range(NBLK):
                        last = mm(psum[5 + t // 4][:, (t % 4) * P:(t % 4 + 1) * P], re_kd[:, t * P:(t + 1) * P],
                                  re_v[:, t * P:(t + 1) * P], start=True, stop=True)
                    last.then_inc(sem["re_usum"], 1)
                    pe.wait_ge(sem["re_kz_ready"], r + 1)
                    scores2(2 * r)
                    part(f"q{j + 1}", 0)
                    output2(2 * r)
                    scores2(2 * r + 1)
                    part(f"q{j + 1}", 1)
                    output2(2 * r + 1)
                    mean2(2 * r)
                    part(f"k{j + 1}", 0)
                    mean2(2 * r + 1)
                    variance2(2 * r)
                    part(f"k{j + 1}", 1)
                    variance2(2 * r + 1)
                for kt in range(4, DT):
                    row_tile(INDEX[("out2", l, 0)], kt, h2_hi, h2_lo, "lo_ready", 16 + 8 * l)
                for d in range(1, DT):
                    project(INDEX[("out2", l, d)], h2_hi, h2_lo)
                    add_square(4 + 2 * l, d - 1, CH_LAT, m_sq)
                add_square(4 + 2 * l, DT - 1, CH_LAT, m_sq)
                for f in range(NF):
                    if f == 0:
                        project_as_ready(INDEX[("up", l, 0)], h2_hi, h2_lo, "h_ready", nh)
                    else:
                        project(INDEX[("up", l, 2 * f)], h2_hi, h2_lo)
                    project(INDEX[("up", l, 2 * f + 1)], h2_hi, h2_lo)
                    if f in AFTER:
                        g = AFTER[f]
                        f0, f1 = GROUPS[g]
                        pe.wait_ge(sem["g_ready"], NF * l + f1)
                        for d in range(DT):
                            project(INDEX[("down", l, (g, d))], g_hi, g_lo, f0)
                            if f == NF - 1 and d:
                                add_square(5 + 2 * l, d - 1, CH_LAT, f_sq)
                add_square(5 + 2 * l, DT - 1, CH_LAT, f_sq)

        @block.scalar
        def _(act):
            A = nc.scalar.activation
            steps = [0]

            def link(ins):
                steps[0] += 1
                ins.then_inc(sem["act_step"], 1)
                act.wait_ge(sem["act_step"], steps[0])

            def square(n, j, src, sq):
                if j >= 2 or n:
                    act.wait_ge(sem["sq_used"], 8 * n + j - 1 if j >= 2 else 8 * n)
                A(sq[j % 2][:, 0:src.shape[-1]], src, ACT.Square).then_inc(sem["sq_ready"], 1)

            def norm(n, rs, chunks):
                act.wait_ge(sem["sq_used"], 8 * n + 8)
                for ci, (t0, w) in enumerate(chunks):
                    last = A(rs[:, t0:t0 + w], psum[3 + ci][:, 0:w], ACT.Ln, bias=EPS)
                link(last)
                end = chunks[-1][0] + chunks[-1][1]
                A(rs[:, 0:end], rs[:, 0:end], ACT.Exp, scale=-0.5).then_inc(sem["ms_ready"], 1)

            def rounded(n, nh, ts, hi, parts, shift):
                for j in range(DT):
                    act.wait_ge(sem["t_ready"], 8 * n + j + 1)
                    for t0, w, r in parts:
                        last = A(hi[:, j, t0:t0 + w], ts[j % 2][:, t0:t0 + w], ACT.Identity, bias=shift(j, r))
                    last.then_inc(sem["hhi_ready"], 1)

            act.wait_ge(sem["params_in"], 112)
            A(csil[:, :], craw[:, :], ACT.Silu).then_inc(sem["cond_silu"], 1)
            act.wait_ge(sem["x_in"], 16)
            for j in range(DT):
                square(0, j, x[:, j], n_sq)
            for l in layers:
                norm(l, n_rs, CH_ALL)
                act.wait_ge(sem["mod_ready"], l + 1)
                ml = lambda kind, j, r: mod[:, 48 * l + 2 * (8 * kind + j) + r:48 * l + 2 * (8 * kind + j) + r + 1]
                rounded(l, l, n_t, h_hi, [(0, S, 0), (S, C, 1)], lambda j, r: ml(0, j, r))
                chunks = CH_OUT[l]
                c0 = chunk_count(l)

                def evacuate(g, out_of, func, scale=1.0):
                    for ci, (t0, w) in enumerate(SEQ[g][4]):
                        q = FIRST_CHUNK[g] + ci
                        act.wait_ge(sem["acc_ready"], q + 1)
                        link(A(out_of(t0, w), psum_of(q)[:, 0:w], func, scale=scale))
                        act.sem_inc(sem[f"acc_free{q % 3}"], 1)

                act.wait_ge(sem["h_ready"], 8 * (l + 1))
                for j in range(2):
                    if j:
                        act.wait_ge(sem["u_ready"], 2 * l + j)
                    g = proj_index(l, f"glu{j}")
                    for ci, (t0, w) in enumerate(SEQ[g][4]):
                        q = FIRST_CHUNK[g] + ci
                        act.wait_ge(sem["acc_ready"], q + 1)
                        link(A(cv_sig[:, t0:t0 + w], psum_of(q)[:, 0:w], ACT.Sigmoid))
                        act.sem_inc(sem[f"acc_free{q % 3}"], 1)
                        act.sem_inc(sem["glu_ready"], 1)
                if l:
                    act.wait_ge(sem["store0"], 16)
                for j in range(2):
                    g = proj_index(l, f"gate{j}")
                    for ci, (t0, w) in enumerate(SEQ[g][4]):
                        q = FIRST_CHUNK[g] + ci
                        act.wait_ge(sem["acc_ready"], q + 1)
                        link(A(x[:, j, t0:t0 + w], psum_of(q)[:, 0:w], ACT.Silu))
                        act.sem_inc(sem[f"acc_free{q % 3}"], 1)
                act.sem_inc(sem["gate_ready"], 1)
                end = chunks[-1][0] + chunks[-1][1]
                for j in range(2):
                    act.wait_ge(sem["cent_ready"], 2 * l + j + 1)
                    if j:
                        act.wait_ge(sem["var_ready"], 2 * l + 1)
                    A(cv_sq[:, 0:end], cv_a[j][:, 0:end], ACT.Square).then_inc(sem["csq_ready"], 1)
                act.wait_ge(sem["var_ready"], 2 * l + 2)
                for ci, (t0, w) in enumerate(chunks):
                    last = A(cv_rs[:, t0:t0 + w], psum[3 + ci][:, 0:w], ACT.Sqrt, bias=EPS)
                last.then_inc(sem["csd_ready"], 1)
                for j in range(2):
                    act.wait_ge(sem["cn_ready"], 2 * l + j + 1)
                    A(cv_u[j][:, 0:end], cv_a[j][:, 0:end], ACT.Silu, scale=v1[:, l * NV1 + V1["ln_w"] + j:l * NV1 + V1["ln_w"] + j + 1],
                      bias=v1[:, l * NV1 + V1["ln_b"] + j:l * NV1 + V1["ln_b"] + j + 1]).then_inc(sem["csilu_ready"], 1)
                act.wait_ge(sem["mixc_ready"], 2 * (l + 1))
                evacuate(proj_index(l, "bk"), lambda t0, w: at_raw[:, t0:t0 + w], ACT.Copy)
                act.sem_inc(sem["raw_ready"], 1)
                act.wait_ge(sem["kz_ready"], l + 1)
                evacuate(proj_index(l, "bv"), lambda t0, w: at_raw[:, t0:t0 + w], ACT.Copy)
                act.sem_inc(sem["vt_ready"], 1)
                act.wait_ge(sem["vn_ready"], l + 1)
                act.wait_ge(sem["kv_clear"], l + 1)
                for b, (t0, t1) in enumerate([(0, 4), (4, 8), (8, 10)]):
                    src = psum[3 + b][:, 0:(t1 - t0) * P].rearrange("p (t e) -> p t e", e=P)
                    for g in range(2):
                        last = A(at_vz[:, t0:t1, g, g * HD:(g + 1) * HD], src[:, :, g * HD:(g + 1) * HD], ACT.Copy)
                last.then_inc(sem["vz_ready"], 1)
                per = len(ATT[l]) // 4

                def copy_context(i):
                    s = ATT0[l] + i
                    act.wait_ge(sem["sc_ready"], s + 1)
                    if s >= 4:
                        act.wait_ge(sem["pt_ready"], s - 3)
                    A(at_s[i % 4][:, 0:C], psum[3][:, 0:C], ACT.Copy).then_inc(sem["sca_copied"], 1)

                def exponentials(i):
                    j, n, g = ATT[l][i]
                    s = ATT0[l] + i
                    lo, hi, _ = near(n)
                    wd = C + (hi - lo) * P
                    c = 3 * (i % 4)
                    h = 8 * l + 4 * g + j
                    act.wait_ge(sem["nmax_ready"], s + 1)
                    A(at_s[i % 4][:, 0:wd], at_s[i % 4][:, 0:wd], ACT.Exp, bias=at_col[:, c:c + 1], scale=HD ** -0.5,
                      accum_out=at_col[:, c + 1:c + 2])
                    A(at_col[:, c + 2:c + 3], nsink[:, h:h + 1], ACT.Exp, bias=at_col[:, c:c + 1], scale=-1.0)\
                        .then_inc(sem["exp_ready"], 1)

                def copy_turned(i):
                    s = ATT0[l] + i
                    j, n, g = ATT[l][i]
                    lo, hi, _ = near(n)
                    act.wait_ge(sem["pt_ready"], s + 1)
                    if s >= 2:
                        act.wait_ge(sem["o_ready"], s - 1)
                    m = (2 + hi - lo) * P
                    for b in range(2 if m > 512 else 1):
                        last = A(at_pt[i % 2][:, b * 512:min(m, b * 512 + 512)],
                                 turned_banks(i)[b][:, 0:min(512, m - b * 512)], ACT.Copy)
                    last.then_inc(sem["pt0_copied"], 1)

                for j in range(4):
                    if j or l:
                        act.wait_ge(sem["rope_ready"], 5 * l + 1 + j)
                    g = proj_index(l, f"q{j}")
                    if j == 0:
                        act.wait_ge(sem["vn_ready"], l + 1)
                    evacuate(g, lambda t0, w: at_raw[:, t0:t0 + w], ACT.Copy)
                    act.sem_inc(sem["raw_ready"], 1)
                    evacuate(proj_index(l, f"bg{j}"), lambda t0, w: x[:, 2 + j, t0:t0 + w], ACT.Silu)
                    copy_context(j * per)
                    for i in range(j * per, j * per + 2):
                        copy_context(i + 1)
                        exponentials(i)
                    for i in range(j * per, (j + 1) * per):
                        if i + 3 < (j + 1) * per:
                            copy_context(i + 3)
                        if i + 2 < (j + 1) * per:
                            exponentials(i + 2)
                        copy_turned(i)
                act.wait_ge(sem["mixa_ready"], (ATT0[l] + len(ATT[l])) // 2)
                evacuate(proj_index(l, "lr"), lambda t0, w: gl_lr[:, t0:t0 + w], ACT.Copy)
                link(A(gl_lr[32:33, :], cst[32:33, 0:1].broadcast_to([1, T]), ACT.Copy, scale=0.0))
                link(nc.scalar.add(gl_lr[32:33, :], gl_lr[32:33, :], 1.0))
                act.sem_inc(sem["lr_in"], 1)
                evacuate(proj_index(l, "cq"), lambda t0, w: gl_q[:, t0:t0 + w], ACT.Copy, scale=GD ** -0.5)
                for p in range(NTT // 2):
                    act.wait_ge(sem["z_ready"], NTT * l + 2 * p + 2)
                    A(gl_e[:, p * 512:(p + 1) * 512], psum[3 + p][:, :], ACT.Abs).then_inc(sem["zabs_ready"], 1)
                act.wait_ge(sem["zabs_ready"], NTT // 2 * (l + 1))
                evacuate(proj_index(l, "ck"), lambda t0, w: gl_k[:, t0:t0 + w], ACT.Copy)
                link(A(gl_e, gl_e, ACT.Exp, scale=-1.0))
                for j in range(2):
                    evacuate(proj_index(l, f"cv{j}"), lambda t0, w: x[:, 6 + j, t0:t0 + w], ACT.Copy)
                act.sem_inc(sem["cv_in"], 1)
                A(gl_e, gl_e, ACT.Ln, bias=1.0).then_inc(sem["sp_ready"], 1)
                evacuate(proj_index(l, "cg0"), lambda t0, w: gl_g[0][:, t0:t0 + w], ACT.Silu)
                act.wait_ge(sem["la_ready"], l + 1)
                for t in range(NTT):
                    act.wait_ge(sem["turned"], NTT * l + t + 1)
                    A(gl_v[:, t, :], psum[3 + t % 5][:, 0:256], ACT.Copy).then_inc(sem["v_copied"], 1)
                evacuate(proj_index(l, "cg1"), lambda t0, w: gl_g[1][:, t0:t0 + w], ACT.Silu)
                act.sem_inc(sem["proj_in"], 1)

                def decays(n):
                    gt = NTT * l + n
                    act.wait_ge(sem["cum_ready"], gt + 1)
                    if n >= 2:
                        act.wait_ge(sem["kin_ready"], gt - 1)
                        if outs or GORD[n - 2] < NBLK:
                            act.wait_ge(sem["kz_split"], outputs(l, n - 2))
                    A(gl_x1[n % 2], psum[5][:, :], ACT.Exp)
                    A(gl_dec[:, 4 * GORD[n]:4 * GORD[n] + 2], psum[5][:, 63:P:64], ACT.Exp)
                    A(gl_dec[:, 4 * GORD[n] + 2:4 * GORD[n] + 4], psum[5][:, P:2 * P:64], ACT.Exp)
                    A(gl_x2[n % 2], psum[5][:, 0:256], ACT.Exp, scale=-1.0).then_inc(sem["ex_ready"], 1)

                outs = l == 0
                decays(0)
                decays(1)
                for n, t in enumerate(GORD):
                    if n + 2 < NTT:
                        decays(n + 2)
                    if outs or t < NBLK:
                        act.wait_ge(sem["ob_ready"], outputs(l, n))
                        A(x[:, 6:8, t * P:(t + 1) * P], psum[1][:, 0:256].rearrange("p (j t) -> p j t", t=P), ACT.Copy)\
                            .then_inc(sem["ob_copied"], 1)
                end = chunks[-1][0] + chunks[-1][1]
                act.wait_ge(sem["obb_added"], outputs(l, NTT - 1))
                for j in range(2):
                    last = A(gl_sq[:, j * T:j * T + end], x[:, 6 + j, 0:end], ACT.Square)
                last.then_inc(sem["gsq_ready"], 1)

                def round_mix(j):
                    A(h_hi[:, j, 0:end], x[:, j, 0:end], ACT.Copy).then_inc(sem["hi_ready"], 1)

                for j in range(3):
                    round_mix(j)
                act.wait_ge(sem["gms_ready"], l + 1)
                for j in range(2):
                    for ci, (t0, w) in enumerate(chunks):
                        b, o = [(3, 0), (4, 0), (5, 0)][ci] if j == 0 else [(6, 0), (7, 0), (5, 256)][ci]
                        last = A(gl_rs[:, j * T + t0:j * T + t0 + w], psum[b][:, o:o + w], ACT.Ln, bias=EPS)
                link(last)
                for j in range(2):
                    A(gl_rs[:, j * T:j * T + end], gl_rs[:, j * T:j * T + end], ACT.Exp, scale=-0.5).then_inc(sem["gsd_ready"], 1)
                if upto and upto[0] == "in" and upto[1] == l:
                    return
                for j in range(3, DT):
                    if j >= 6:
                        act.wait_ge(sem["gmix_ready"], 2 * l + j - 5)
                    round_mix(j)
                for d in range(DT):
                    act.wait_ge(sem["res_ready"], 8 * l + d + 1)
                    square(1 + l, d, x[:, d, 0:end], n_sq)
                if upto and upto[0] == "layer" and upto[1] == l:
                    return

            def evacuate2(g, dst, func, scale=1.0):
                for ci, (t0, w) in enumerate(SEQ[g][4]):
                    q = FIRST_CHUNK[g] + ci
                    act.wait_ge(sem["acc_ready"], q + 1)
                    link(A(dst[:, t0:t0 + w], psum_of(q)[:, 0:w], func, scale=scale))
                    act.sem_inc(sem[f"acc_free{q % 3}"], 1)

            def final(n):
                for j in range(DT):
                    act.wait_ge(sem["t_ready"], 8 * n + j + 1)
                    link(A(x2[:, j], m_t[j % 2], ACT.Copy))
                    act.sem_inc(sem["fin_ready"], 1)
                    if n == 2:
                        square(3, j, x2[:, j], m_sq)

            norm(2, m_rs, CH_LAT)
            final(2)
            for l in layers:
                w2 = lambda name, i: v2[:, l * NV2 + V2[name] + i:l * NV2 + V2[name] + i + 1]
                norm(3 + 2 * l, m_rs, CH_LAT)
                rounded(3 + 2 * l, 2 + 2 * l, m_t, h2_hi, [(0, S, 0)], lambda j, r: 0.0)
                act.wait_ge(sem["h_ready"], 8 * (3 + 2 * l))
                for j in range(2):
                    evacuate2(INDEX[("in2", l, j)], sg_v[j], ACT.Gelu_apprx_tanh)
                    act.sem_inc(sem["sg_ready"], 1)
                act.wait_ge(sem[f"store{1 + l}"], 16)
                for j in range(2):
                    evacuate2(INDEX[("in2", l, 2 + j)], x2[:, j], ACT.Gelu_apprx_tanh)
                for j in range(2):
                    evacuate2(INDEX[("in2", l, 4 + j)], po_x[j][:, 16:], ACT.Copy)
                    act.sem_inc(sem["po_in"], 1)
                def take(name, ci, dst, func=ACT.Copy):
                    g = INDEX[("in2", l, IN2.index(name))]
                    q, (t0, w) = FIRST_CHUNK[g] + ci, SEQ[g][4][ci]
                    act.wait_ge(sem["acc_ready"], q + 1)
                    link(A(dst[:, t0:t0 + w], psum_of(q)[:, 0:w], func))
                    act.sem_inc(sem[f"acc_free{q % 3}"], 1)

                act.wait_ge(sem["sg_turned"], l + 1)
                for t in range(NBLK):
                    link(A(sg_sq, psum[3 + t // 2][:, (t % 2) * 256:(t % 2 + 1) * 256], ACT.Square, accum_out=sg_col[:, t:t + 1]))
                A(sg_col, sg_col, ACT.Sqrt, bias=EPS, scale=1.0 / 256).then_inc(sem["sg_col_ready"], 1)
                for m, name in enumerate(("q0", "k0")):
                    for ci in range(2):
                        take(name, ci, re_raw[m])
                    act.sem_inc(sem["re_raw_ready"], 1)
                for j in range(2):
                    act.wait_ge(sem["po_sum"], 2 * l + j + 1)
                    for ci in range(2):
                        last = A(x2[:, 2 + j, ci * 512:(ci + 1) * 512], psum[3 + ci][:, :], ACT.Copy, scale=w2("bs", j))
                    last.then_inc(sem["po_mixed"], 1)
                act.wait_ge(sem["po_mixed"], 2 * (l + 1))
                act.wait_ge(sem["sg_mixed"], 2 * (l + 1))
                def copy_output(m):
                    act.wait_ge(sem["re_ysum"], m + 1)
                    if m >= 2:
                        act.wait_ge(sem["re_mixed"], m - 1)
                    A(re_y[:, (m % 2) * 512:(m % 2 + 1) * 512], psum[7][:, :], ACT.Copy).then_inc(sem["re_ycopied"], 1)

                def square2(m):
                    act.wait_ge(sem["re_cent"], m + 1)
                    if m:
                        act.wait_ge(sem["re_var"], m)
                    A(re_sq, re_y[:, (m % 2) * 512:(m % 2 + 1) * 512], ACT.Square).then_inc(sem["re_sq_ready"], 1)

                def round_mix2(j):
                    A(h2_hi[:, j], x2[:, j], ACT.Copy).then_inc(sem["hi_ready"], 1)

                def inverse_deviation(m):
                    act.wait_ge(sem["re_var"], m + 1)
                    if m:
                        act.wait_ge(sem["re_mixed"], m)
                    link(A(re_rs, psum[6][:, :], ACT.Ln, bias=EPS))
                    A(re_rs, re_rs, ACT.Exp, scale=-0.5).then_inc(sem["re_sd"], 1)

                for j in range(4):
                    r = 4 * l + j
                    act.wait_ge(sem["re_rot"], 2 * r + 1)
                    act.wait_ge(sem["re_cos"], 2 * r + 1)
                    take(f"v{j}", 0, re_raw[0])
                    take(f"v{j}", 1, re_raw[0])
                    act.sem_inc(sem["re_vt"], 1)
                    take(f"g{j}", 0, x2[:, 4 + j], ACT.Silu)
                    act.wait_ge(sem["re_vt_turned"], r + 1)
                    act.wait_ge(sem["re_clear"], l + 1)
                    for b in range(2):
                        src = psum[3 + b][:, :].rearrange("p (t e) -> p t e", e=P)
                        A(re_v[:, b * 512:(b + 1) * 512], psum[3 + b][:, :], ACT.Copy)
                        for g in range(2):
                            last = A(re_vz[:, 4 * b:4 * b + 4, g, g * HD:(g + 1) * HD], src[:, :, g * HD:(g + 1) * HD], ACT.Copy)
                    last.then_inc(sem["re_v_in"], 1)
                    take(f"g{j}", 1, x2[:, 4 + j], ACT.Silu)
                    if j < 3:
                        take(f"q{j + 1}", 0, re_raw[0])
                    else:
                        round_mix2(0)
                    copy_output(2 * r)
                    if j < 3:
                        take(f"q{j + 1}", 1, re_raw[0])
                        act.sem_inc(sem["re_raw_ready"], 1)
                    else:
                        round_mix2(1)
                    copy_output(2 * r + 1)
                    square2(2 * r)
                    if j < 3:
                        act.wait_ge(sem["re_rot"], 2 * r + 2)
                        act.wait_ge(sem["re_cos"], 2 * r + 2)
                        take(f"k{j + 1}", 0, re_raw[1])
                    else:
                        round_mix2(2)
                    inverse_deviation(2 * r)
                    square2(2 * r + 1)
                    if j < 3:
                        take(f"k{j + 1}", 1, re_raw[1])
                        act.sem_inc(sem["re_raw_ready"], 1)
                    else:
                        round_mix2(3)
                    inverse_deviation(2 * r + 1)
                for j in range(4, DT):
                    act.wait_ge(sem["re_mixed"], 8 * l + 2 * (j - 3))
                    round_mix2(j)
                for d in range(DT):
                    act.wait_ge(sem["res_ready"], 16 + 16 * l + d + 1)
                    square(4 + 2 * l, d, x2[:, d], m_sq)
                norm(4 + 2 * l, m_rs, CH_LAT)
                rounded(4 + 2 * l, 3 + 2 * l, m_t, h2_hi, [(0, S, 0)], lambda j, r: 0.0)
                act.wait_ge(sem["h_ready"], 8 * (4 + 2 * l))
                act.wait_ge(sem["ff_pads"], l + 1)

                def up(f):
                    n = NF * l + f
                    if f >= 2:
                        act.wait_ge(sem["ff_conv"], n - 1)
                    for m in range(2):
                        evacuate2(INDEX[("up", l, 2 * f + m)], ff_up[2 * (f % 2) + m][:, 2:], ACT.Copy)
                    act.sem_inc(sem["ff_up_ready"], 1)

                for f in range(NF):
                    n = NF * l + f
                    up(f)
                    act.wait_ge(sem["ff_conv"], n + 1)
                    A(ff_c[0], ff_c[0], ACT.Silu).then_inc(sem["ff_gated"], 1)
                    act.wait_ge(sem["ff_prod"], n + 1)
                    A(g_hi[:, f % NG], ff_c[1], ACT.Copy).then_inc(sem["ff_hi"], 1)
                for d in range(DT):
                    act.wait_ge(sem["res_ready"], 24 + 16 * l + d + 1)
                    square(5 + 2 * l, d, x2[:, d], f_sq)
            norm(7, m_rs, CH_LAT)
            final(7)

        @block.vector
        def _(dve):
            V = nc.vector
            steps = [0]

            def link(ins):
                steps[0] += 1
                ins.then_inc(sem["dve_step"], 1)
                dve.wait_ge(sem["dve_step"], steps[0])

            def norm(n, nh, xs, ts, rs, parts, scale, hi=None, lo=None, shift=None):
                dve.wait_ge(sem["ms_ready"], n + 1)

                def rest(j):
                    dve.wait_ge(sem["hhi_ready"], 8 * nh + j + 1)
                    for t0, w, r in parts:
                        sl = slice(t0, t0 + w)
                        last = V.scalar_tensor_tensor(lo[:, j, sl], ts[j % 2][:, sl], shift(j, r), hi[:, j, sl].bitcast(F32),
                                                      ALU.add, ALU.subtract)
                    last.then_inc(sem["h_ready"], 1)

                for j in range(DT):
                    if j >= 2 and hi is not None:
                        dve.wait_ge(sem["h_ready"], 8 * nh + j - 1)
                    if j >= 2 and hi is None:
                        dve.wait_ge(sem["fin_ready"], 8 * (n == 7) + j - 1)
                    for t0, w, r in parts:
                        sl = slice(t0, t0 + w)
                        last = V.scalar_tensor_tensor(ts[j % 2][:, sl], xs[:, j, sl], scale(j, r), rs[:, sl], ALU.mult, ALU.mult)
                    last.then_inc(sem["t_ready"], 1)
                    if hi is not None and j:
                        rest(j - 1)
                if hi is not None:
                    rest(DT - 1)

            def modulation(l, m0, m1, src):
                m = mod[:, 48 * l + 2 * m0:48 * l + 2 * m1].rearrange("p (m r) -> p m r", r=2)
                c = l * NV1 + V1["b_mod"]
                b = v1[:, c + m0:c + m1].unsqueeze(2).broadcast_to([P, m1 - m0, 2])
                link(V.tensor_tensor(m, src.rearrange("p (m r) -> p m r", r=2), b, ALU.add))
                if m0 <= 8 < m1:
                    link(V.tensor_scalar(mod[:, 48 * l + 16:48 * l + 32], mod[:, 48 * l + 16:48 * l + 32], 1.0, None, ALU.add))
                    dve.sem_inc(sem["mod_ready"], 1)

            dve.wait_ge(sem["params_in"], 112)
            dve.wait_ge(sem["x_in"], 16)
            link(V.tensor_scalar(nsink[:, :], nsink[:, :], -1.0, None, ALU.mult))
            dve.wait_ge(sem["wm_used"], 16)
            modulation(0, 0, 16, psum[7][:, 0:32])
            for l in layers:
                ml = lambda kind, j, r: mod[:, 48 * l + 2 * (8 * kind + j) + r:48 * l + 2 * (8 * kind + j) + r + 1]
                dve.wait_ge(sem["mod_ready"], l + 1)
                norm(l, l, x, n_t, n_rs, [(0, S, 0), (S, C, 1)], lambda j, r: ml(1, j, r), h_hi, h_lo, lambda j, r: ml(0, j, r))
                chunks = CH_OUT[l]
                c0 = chunk_count(l)
                end = chunks[-1][0] + chunks[-1][1]
                dve.wait_ge(sem["h_ready"], 8 * (l + 1))
                for j in range(2):
                    V.memset(cv_u[j][:, 0:PAD], 0.0)
                    V.memset(cv_u[j][:, PAD + S:3 * PAD + S], 0.0)
                    V.memset(cv_u[j][:, 3 * PAD + T:4 * PAD + T], 0.0)
                vl = lambda name, i: v1[:, l * NV1 + V1[name] + i:l * NV1 + V1[name] + i + 1]
                for j in range(2):
                    g = proj_index(l, f"val{j}")
                    nq = len(SEQ[g][4])
                    for ci, (t0, w) in enumerate(SEQ[g][4]):
                        q = FIRST_CHUNK[g] + ci
                        dve.wait_ge(sem["glu_ready"], GLU0[l] + j * nq + ci + 1)
                        dve.wait_ge(sem["acc_ready"], q + 1)
                        off = PAD + t0 if t0 < S else 3 * PAD + t0
                        link(V.tensor_tensor(cv_u[j][:, off:off + w], psum_of(q)[:, 0:w], cv_sig[:, t0:t0 + w], ALU.mult))
                        dve.sem_inc(sem[f"acc_free{q % 3}"], 1)
                    dve.sem_inc(sem["u_ready"], 1)
                for j in range(2):
                    for i in range(CK):
                        for (o, u0, w) in [(0, 0, S), (S, S + 2 * PAD, C)][:1 if l else 2]:
                            src = cv_u[j][:, u0 + i:u0 + i + w]
                            dst = cv_a[j][:, o:o + w]
                            if i == 0:
                                ins = V.tensor_scalar(dst, src, vl("conv_w", 31 * j), vl("conv_b", j), ALU.mult, ALU.add)
                            else:
                                ins = V.scalar_tensor_tensor(dst, src, vl("conv_w", 31 * j + i), dst, ALU.mult, ALU.add)
                        link(ins)
                    dve.sem_inc(sem["conv_ready"], 1)
                if l == 0:
                    dve.wait_ge(sem["wm_used"], 16 + len(LATE_MOD))
                    modulation(0, 16, 24, psum[7][:, 0:16])
                    modulation(1, 0, 24, psum[7][:, 16:64])
                dve.wait_ge(sem["mean_ready"], l + 1)
                for j in range(2):
                    for ci, (t0, w) in enumerate(chunks):
                        last = V.tensor_tensor(cv_a[j][:, t0:t0 + w], cv_a[j][:, t0:t0 + w], psum[3 + ci][:, 0:w], ALU.subtract)
                    link(last)
                    if j == 1:
                        for jj in range(2):
                            dve.sem_inc(sem["cent_ready"], 1)
                dve.wait_ge(sem["csd_ready"], l + 1)
                link(V.reciprocal(cv_rs[:, 0:end], cv_rs[:, 0:end]))
                for j in range(2):
                    V.tensor_tensor(cv_a[j][:, 0:end], cv_a[j][:, 0:end], cv_rs[:, 0:end], ALU.mult).then_inc(sem["cn_ready"], 1)
                for j in range(2):
                    dve.wait_ge(sem["csilu_ready"], 2 * l + j + 1)
                    dve.wait_ge(sem["gate_ready"], l + 1)
                    V.tensor_tensor(x[:, j, 0:end], x[:, j, 0:end], cv_u[j][:, 0:end], ALU.mult).then_inc(sem["mixc_ready"], 1)
                dve.wait_ge(sem["rope_in"], 16 * (l + 1))

                def rope(n, ctx):
                    dve.wait_ge(sem["rot_ready"], n + 1)
                    dve.wait_ge(sem["cosm_ready"], n + 1)
                    for ci in range(2):
                        sl = slice(ci * 512, (ci + 1) * 512)
                        link(V.tensor_tensor(at_tmp, psum[3 + ci][:, :], at_cs[:, S + ci * 512:S + (ci + 1) * 512], ALU.mult))
                        link(V.tensor_tensor(at_q[:, sl], at_q[:, sl], at_tmp, ALU.add))

                rope(5 * l, True)
                for g in range(2):
                    link(V.tensor_copy(at_kz[g][g * HD:(g + 1) * HD, :], at_q[g * HD:(g + 1) * HD, :]))
                dve.sem_inc(sem["rope_ready"], 1)
                dve.wait_ge(sem["kv_clear"], l + 1)
                dve.sem_inc(sem["kz_ready"], 1)
                per = len(ATT[l]) // 4

                def front(i):
                    j, n, g = ATT[l][i]
                    s = ATT0[l] + i
                    lo, hi, m0 = near(n)
                    wd = (hi - lo) * P
                    b = at_s[i % 4]
                    c = 3 * (i % 4)
                    dve.wait_ge(sem["sc_ready"], s + 1)
                    if s >= 4:
                        dve.wait_ge(sem["pt_ready"], s - 3)
                    if wd:
                        link(V.tensor_tensor(b[:, C:C + wd], psum[4][:, 0:wd], k("local")[:, m0:m0 + wd], ALU.add))
                    dve.sem_inc(sem["scm_ready"], 1)
                    dve.wait_ge(sem["sca_copied"], s + 1)
                    link(V.reduce_max(at_col[:, 12:13], b[:, 0:C + wd], AX))
                    if s >= 4:
                        dve.wait_ge(sem["exp_ready"], s - 3)
                    h = 8 * l + 4 * g + j
                    V.tensor_scalar(at_col[:, c:c + 1], at_col[:, 12:13], -HD ** -0.5, nsink[:, h:h + 1], ALU.mult, ALU.min)\
                     .then_inc(sem["nmax_ready"], 1)

                def back(i):
                    j, n, g = ATT[l][i]
                    s = ATT0[l] + i
                    lo, hi, m0 = near(n)
                    wd = C + (hi - lo) * P
                    b = at_s[i % 4]
                    c = 3 * (i % 4)
                    dve.wait_ge(sem["exp_ready"], s + 1)
                    link(V.tensor_tensor(at_col[:, 13:14], at_col[:, c + 1:c + 2], at_col[:, c + 2:c + 3], ALU.add))
                    link(V.reciprocal(at_col[:, 14:15], at_col[:, 13:14]))
                    V.tensor_scalar(b[:, 0:wd], b[:, 0:wd], at_col[:, 14:15], None, ALU.mult).then_inc(sem["p_ready"], 1)

                def mix(i):
                    j, n, g = ATT[l][i]
                    if g:
                        dve.wait_ge(sem["o_ready"], ATT0[l] + i + 1)
                        m = x[:, 2 + j, n * P:(n + 1) * P]
                        V.tensor_tensor(m, out_bank(i)[:, 0:P], m, ALU.mult).then_inc(sem["mixa_ready"], 1)

                for j in range(4):
                    rope(5 * l + 1 + j, True)
                    dve.sem_inc(sem["rope_ready"], 1)
                    i0, i1 = j * per, (j + 1) * per
                    for i in range(i0, i0 + 3):
                        front(i)
                    for i in range(i0, i1):
                        back(i)
                        if i + 3 < i1:
                            front(i + 3)
                        if i >= i0 + 2:
                            mix(i - 2)
                    mix(i1 - 2)
                    mix(i1 - 1)
                for p in range(NTT // 2):
                    dve.wait_ge(sem["zabs_ready"], NTT // 2 * l + p + 1)
                    last = V.tensor_scalar(gl_la[:, p * 512:(p + 1) * 512], psum[3 + p][:, :], 0.0, None, ALU.min)
                link(last)
                dve.wait_ge(sem["sp_ready"], l + 1)
                link(V.tensor_tensor(gl_la, gl_la, gl_e, ALU.subtract))
                dve.sem_inc(sem["la_ready"], 1)
                for t in range(NTT):
                    dve.wait_ge(sem["v_copied"], NTT * l + t + 1)
                    V.tensor_copy(gl_kt[:, t * P:(t + 1) * P], psum[3 + t % 5][:, 2 * P:3 * P]).then_inc(sem["kt_copied"], 1)
                dve.wait_ge(sem["kt_copied"], NTT * (l + 1))
                dve.wait_ge(sem["proj_in"], l + 1)
                outs = l == 0

                def decayed(n):
                    t, gt = GORD[n], NTT * l + n
                    ts = slice(t * P, (t + 1) * P)
                    dve.wait_ge(sem["ex_ready"], gt + 1)
                    if outs or t < NBLK:
                        xk = gl_x2[n % 2].rearrange("p (d t) -> p d t", t=P)
                        V.tensor_tensor(xk, xk, gl_k[:, ts].unsqueeze(1).broadcast_to([P, 2, P]), ALU.mult).then_inc(sem["xk_ready"], 1)
                        V.tensor_tensor(gl_qd[:, :, ts], gl_q[:, ts].unsqueeze(1).broadcast_to([P, 2, P]),
                                        gl_x1[n % 2][:, 0:2 * P].rearrange("p (d t) -> p d t", t=P), ALU.mult)
                    for c in range(2):
                        last = V.scalar_tensor_tensor(gl_kdz[:, t, c], gl_kt[:, ts].unsqueeze(1).broadcast_to([P, 2, P]),
                                                      k("chunkrows")[:, c:c + 1],
                                                      gl_x1[n % 2][:, 2 * P:4 * P].rearrange("p (d t) -> p d t", t=P), ALU.mult, ALU.mult)
                    last.then_inc(sem["kin_ready"], 1)

                def states(m, src, t, back):
                    link(V.tensor_tensor(gl_uz.rearrange("p (c v) -> p c v", v=256), src.rearrange("p (c v) -> p c v", v=256),
                                         k("heads").unsqueeze(1).broadcast_to([P, 2, 256]), ALU.mult))
                    for i, c in enumerate((1, 0) if back else (0, 1)):
                        d = 4 * t + 2 * back + c
                        link(V.scalar_tensor_tensor(gl_s[(2 * m + i + 1) % 6], gl_s[(2 * m + i) % 6], gl_dec[:, d:d + 1],
                                                    gl_uz[:, c * 256:(c + 1) * 256], ALU.mult, ALU.add))

                link(V.memset(gl_s[0], 0.0))
                decayed(0)
                decayed(1)
                for n, t in enumerate(GORD):
                    gt = NTT * l + n
                    dve.wait_ge(sem["u_sum"], gt + 1)
                    if n >= 2 and outputs(l, n - 2) and (outs or GORD[n - 2] < NBLK):
                        dve.wait_ge(sem["ob_ready"], outputs(l, n - 2))
                    if outs or t < NBLK:
                        bf, bb = (6, 7) if n % 2 == 0 else (3, 4)
                        a3 = gl_a[n % 2].rearrange("p (h t) -> p h t", t=P)
                        b3 = gl_tmp.rearrange("p (h t) -> p h t", t=P)
                        V.tensor_tensor(a3, psum[bf][:, :].rearrange("p (h t) -> p h t", t=P),
                                        k("maskf").unsqueeze(1).broadcast_to([P, 4, P]), ALU.mult)
                        link(V.tensor_tensor(b3, psum[bb][:, :].rearrange("p (h t) -> p h t", t=P),
                                             k("maskb").unsqueeze(1).broadcast_to([P, 4, P]), ALU.mult))
                        link(V.tensor_tensor(gl_a[n % 2], gl_a[n % 2], gl_tmp, ALU.add))
                    states(n, psum[2 * (n % 2)][:, :], t, 0)
                    dve.sem_inc(sem["st_ready"], 1)
                    if n + 2 < NTT:
                        decayed(n + 2)

                def states_back(n):
                    dve.wait_ge(sem["ub_sum"], NTT * l + n + 1)
                    states(n, psum[3 + n % 2][:, :], BORD[n], 1)
                    dve.sem_inc(sem["sb_ready"], 1)

                dve.wait_ge(sem["ob_copied"], outputs(l, NTT - 1))
                link(V.memset(gl_s[0], 0.0))
                states_back(0)
                for n, t in enumerate(BORD):
                    if n + 1 < NTT:
                        states_back(n + 1)
                    if outs or t < NBLK:
                        ts = slice(t * P, (t + 1) * P)
                        dve.wait_ge(sem["obb_ready"], outputs(l, n))
                        V.tensor_tensor(x[:, 6:8, ts], psum[5 + n % 2][:, 0:256].rearrange("p (j t) -> p j t", t=P), x[:, 6:8, ts], ALU.add)\
                         .then_inc(sem["obb_added"], 1)
                def split_rest(j):
                    dve.wait_ge(sem["hi_ready"], 8 * l + j + 1)
                    V.tensor_tensor(h_lo[:, j, 0:end], x[:, j, 0:end], h_hi[:, j, 0:end].bitcast(F32), ALU.subtract)\
                     .then_inc(sem["lo_ready"], 1)

                for j in range(3):
                    split_rest(j)
                for j in range(2):
                    dve.wait_ge(sem["gsd_ready"], 2 * l + j + 1)
                    xs = x[:, 6 + j, 0:end]
                    link(V.tensor_tensor(xs, xs, gl_rs[:, j * T:j * T + end], ALU.mult))
                    V.scalar_tensor_tensor(xs, xs, vl("norm", j), gl_g[j][:, 0:end], ALU.mult, ALU.mult)\
                     .then_inc(sem["gmix_ready"], 1)
                if upto and upto[0] == "in" and upto[1] == l:
                    return
                dve.wait_ge(sem["gmix_ready"], 2 * l + 2)
                for j in range(3, DT):
                    split_rest(j)
                for d in range(DT):
                    n = 8 * l + d
                    g = INDEX[("out1", l, d)]
                    dve.wait_ge(sem[f"xold_in{n % 2}"], 16 * (n // 2 + 1))
                    for ci, (t0, w) in enumerate(SEQ[g][4]):
                        q = FIRST_CHUNK[g] + ci
                        c = 48 * l + 2 * (16 + d) + (t0 >= S)
                        dve.wait_ge(sem["acc_ready"], q + 1)
                        link(V.scalar_tensor_tensor(x[:, d, t0:t0 + w], psum_of(q)[:, 0:w], mod[:, c:c + 1],
                                                    xold1[n % 2][:, t0:t0 + w], ALU.mult, ALU.add))
                        dve.sem_inc(sem[f"acc_free{q % 3}"], 1)
                    dve.sem_inc(sem["res_ready"], 1)
                if upto and upto[0] == "layer" and upto[1] == l:
                    return

            norm(2, None, x, m_t, m_rs, [(0, S, 0)], lambda j, r: v3[:, j:j + 1])
            for l in layers:
                w2 = lambda name, i: v2[:, l * NV2 + V2[name] + i:l * NV2 + V2[name] + i + 1]
                norm(3 + 2 * l, 2 + 2 * l, x2, m_t, m_rs, [(0, S, 0)], lambda j, r: w2("g1", j), h2_hi, h2_lo, lambda j, r: 0.0)
                dve.wait_ge(sem["h_ready"], 8 * (3 + 2 * l))
                dve.wait_ge(sem["m_tables"], 16 + 48 * (l + 1))
                link(V.memset(sg_vz_, 0.0))
                link(V.memset(sg_ws.rearrange("p (h t) -> p h t", t=P)[64:P, :, 0:64], 0.0))
                for b in po_x + po_s:
                    last = V.memset(b[:, 0:16], 0.0)
                link(last)
                for j in range(2):
                    dve.wait_ge(sem["po_in"], 2 * l + j + 1)
                    sums = [po_x[j]]
                    for d in range(2 if j == 0 else 4):
                        src, dst = sums[-1], po_s[d % 2]
                        link(V.tensor_tensor(dst[:, 16:], src[:, 16:], src[:, 16 - 2 ** d:16 - 2 ** d + S], ALU.add))
                        sums.append(dst)
                    for g in range(2):
                        rs_ = slice(g * 64, (g + 1) * 64)
                        sm = sums[-2 + g]
                        link(V.scalar_tensor_tensor(po_p[j][rs_, :], sm[rs_, 16:], k("winv")[rs_, j:j + 1], po_x[j][rs_, 16:], ALU.mult, ALU.subtract))
                        link(V.tensor_tensor(po_p[j][rs_, 0:16], sm[rs_, 16:32], k("cinv")[rs_, j * 16:(j + 1) * 16], ALU.mult))
                        link(V.tensor_tensor(po_p[j][rs_, 0:16], po_p[j][rs_, 0:16], po_x[j][rs_, 16:32], ALU.subtract))
                    dve.sem_inc(sem["po_ready"], 1)
                dve.wait_ge(sem["sg_col_ready"], l + 1)
                link(V.reciprocal(sg_col, sg_col))
                for t in range(NBLK):
                    src = psum[3 + t // 2][:, (t % 2) * 256:(t % 2 + 1) * 256].rearrange("p (h e) -> p h e", e=HD)
                    for o in range(2):
                        last = V.tensor_scalar(sg_vz[:, t, o:4:2, o * HD:(o + 1) * HD], src[:, o:4:2, :], sg_col[:, t:t + 1], None, ALU.mult)
                last.then_inc(sem["sg_vz_ready"], 1)
                for j in range(2):
                    dve.wait_ge(sem["sg_sum"], 2 * l + j + 1)
                    for hf in range(2):
                        tv = sg_tmp.rearrange("p (n t) -> p n t", t=P)
                        link(V.scalar_tensor_tensor(tv, psum[3 + 2 * j + hf][:, :].rearrange("p (n t) -> p n t", t=P), w2("vn", j),
                                                    sg_bs[:, j * P:(j + 1) * P].unsqueeze(1).broadcast_to([P, 4, P]), ALU.mult, ALU.add))
                        xs = x2[:, j, hf * 512:(hf + 1) * 512]
                        link(V.tensor_tensor(xs, xs, sg_tmp, ALU.mult))
                    dve.sem_inc(sem["sg_mixed"], 1)
                def split_rest2(j):
                    dve.wait_ge(sem["hi_ready"], 16 + 8 * l + j + 1)
                    V.tensor_tensor(h2_lo[:, j], x2[:, j], h2_hi[:, j].bitcast(F32), ALU.subtract).then_inc(sem["lo_ready"], 1)

                dve.wait_ge(sem["re_cs_in"], 16 * (l + 1))
                for j in range(4):
                    r = 4 * l + j
                    for m, dst in enumerate((re_q, re_k)):
                        dve.wait_ge(sem["re_rot"], 2 * r + m + 1)
                        dve.wait_ge(sem["re_cos"], 2 * r + m + 1)
                        for ci in range(2):
                            sl = slice(ci * 512, (ci + 1) * 512)
                            b = psum[3 + 2 * m + ci][:, :]
                            link(V.tensor_tensor(b, b, re_cs[:, S + ci * 512:S + (ci + 1) * 512], ALU.mult))
                            link(V.tensor_tensor(dst[:, sl], dst[:, sl], b, ALU.add))
                        dve.sem_inc(sem["re_roped"], 1)
                    dve.wait_ge(sem["re_kt"], r + 1)
                    for b in range(2):
                        V_ = V.tensor_tensor(re_kd[:, b * 512:(b + 1) * 512].rearrange("p (t d) -> p t d", d=P),
                                             psum[5 + b][:, :].rearrange("p (t d) -> p t d", d=P),
                                             k("kdec")[:, j * P:(j + 1) * P].unsqueeze(1).broadcast_to([P, 4, P]), ALU.mult)
                    link(V_)
                    dve.sem_inc(sem["re_kd_ready"], 1)
                    dve.wait_ge(sem["re_usum"], r + 1)
                    for b in range(2):
                        V_ = V.tensor_tensor(re_u[:, b * 512:(b + 1) * 512].rearrange("p (t d) -> p t d", d=P),
                                             psum[5 + b][:, :].rearrange("p (t d) -> p t d", d=P),
                                             k("pairs").unsqueeze(1).broadcast_to([P, 4, P]), ALU.mult)
                    link(V_)
                    for n in range(1, NBLK - 1):
                        link(V.scalar_tensor_tensor(re_u[:, n * P:(n + 1) * P], re_u[:, (n - 1) * P:n * P], k("gam")[:, j:j + 1],
                                                    re_u[:, n * P:(n + 1) * P], ALU.mult, ALU.add))
                    dve.sem_inc(sem["re_states"], 1)
                    for hf in range(2):
                        m = 2 * r + hf
                        dve.wait_ge(sem["re_scores"], m + 1)
                        for g in range(2):
                            h = 2 * j + g
                            V_ = V.tensor_tensor(re_a[:, g * 512:(g + 1) * 512].rearrange("p (n t) -> p n t", t=P),
                                                 psum[3 + g][:, :].rearrange("p (n t) -> p n t", t=P),
                                                 k("dec")[:, h * P:(h + 1) * P].unsqueeze(1).broadcast_to([P, 4, P]), ALU.mult)
                        link(V_)
                        dve.sem_inc(sem["re_am"], 1)
                        if j == 3:
                            split_rest2(hf)
                    for hf in range(2):
                        m = 2 * r + hf
                        ys = re_y[:, hf * 512:(hf + 1) * 512]
                        dve.wait_ge(sem["re_mean"], m + 1)
                        link(V.tensor_tensor(ys, ys, psum[5][:, :], ALU.subtract))
                        dve.sem_inc(sem["re_cent"], 1)
                        if j == 3:
                            split_rest2(2 + hf)
                    for hf in range(2):
                        m = 2 * r + hf
                        ys = re_y[:, hf * 512:(hf + 1) * 512]
                        dve.wait_ge(sem["re_sd"], m + 1)
                        link(V.tensor_tensor(ys, ys, re_rs, ALU.mult))
                        xs = x2[:, 4 + j, hf * 512:(hf + 1) * 512]
                        link(V.scalar_tensor_tensor(xs, ys, w2("cn", j), xs, ALU.mult, ALU.mult))
                        dve.sem_inc(sem["re_mixed"], 1)
                for j in range(4, DT):
                    split_rest2(j)
                for d in range(DT):
                    n = 16 + 8 * l + d
                    g = INDEX[("out2", l, d)]
                    dve.wait_ge(sem[f"xold_in{n % 2}"], 16 * (n // 2 + 1))
                    for ci, (t0, w) in enumerate(SEQ[g][4]):
                        q = FIRST_CHUNK[g] + ci
                        dve.wait_ge(sem["acc_ready"], q + 1)
                        link(V.tensor_tensor(x2[:, d, t0:t0 + w], psum_of(q)[:, 0:w], xold2[n % 2][:, t0:t0 + w], ALU.add))
                        dve.sem_inc(sem[f"acc_free{q % 3}"], 1)
                    dve.sem_inc(sem["res_ready"], 1)
                norm(4 + 2 * l, 3 + 2 * l, x2, m_t, m_rs, [(0, S, 0)], lambda j, r: w2("g2", j), h2_hi, h2_lo, lambda j, r: 0.0)
                dve.wait_ge(sem["h_ready"], 8 * (4 + 2 * l))
                for b in ff_up:
                    link(V.memset(b[:, 0:2], 0.0))
                dve.sem_inc(sem["ff_pads"], 1)
                for f in range(NF):
                    n = NF * l + f
                    dve.wait_ge(sem["ff_up_ready"], n + 1)
                    if f:
                        dve.wait_ge(sem["ff_hi"], n)
                    adds = iter([(d, ci) for d in range(DT) for ci in range(2)] if f in AFTER else [])

                    def add_down(count):
                        for _, (d, ci) in zip(range(count), adds):
                            q, (t0, w) = FIRST_CHUNK[INDEX[("down", l, (AFTER[f], d))]] + ci, CH_LAT[ci]
                            dve.wait_ge(sem["acc_ready"], q + 1)
                            link(V.tensor_tensor(x2[:, d, t0:t0 + w], psum_of(q)[:, 0:w], x2[:, d, t0:t0 + w], ALU.add))
                            dve.sem_inc(sem[f"acc_free{q % 3}"], 1)
                            if f == NF - 1 and ci == 1:
                                dve.sem_inc(sem["res_ready"], 1)

                    between = 0 if f == NF - 1 else 1
                    for m in range(2):
                        u, c, wi = ff_up[2 * (f % 2) + m], ff_c[m], 22 * m + f
                        link(V.tensor_scalar(c, u[:, 2:], w2("conv_w", 88 + wi), w2("conv_b", wi), ALU.mult, ALU.add))
                        add_down(between)
                        link(V.scalar_tensor_tensor(c, u[:, 1:S + 1], w2("conv_w", 44 + wi), c, ALU.mult, ALU.add))
                        add_down(between)
                        link(V.scalar_tensor_tensor(c, u[:, 0:S], w2("conv_w", wi), c, ALU.mult, ALU.add))
                        if m == 0:
                            add_down(between)
                    dve.sem_inc(sem["ff_conv"], 1)
                    add_down(between)
                    dve.wait_ge(sem["ff_gated"], n + 1)
                    link(V.tensor_tensor(ff_c[1], ff_c[1], ff_c[0], ALU.mult))
                    dve.sem_inc(sem["ff_prod"], 1)
                    add_down(between)
                    dve.wait_ge(sem["ff_hi"], n + 1)
                    link(V.tensor_tensor(g_lo[:, f % NG], ff_c[1], g_hi[:, f % NG].bitcast(F32), ALU.subtract))
                    dve.sem_inc(sem["g_ready"], 1)
                    add_down(2 * DT)
            norm(7, None, x2, m_t, m_rs, [(0, S, 0)], lambda j, r: v3[:, 8 + j:9 + j])

        @block.gpsimd
        def _(pool):
            G = nc.gpsimd
            steps = [0]

            def link(ins):
                steps[0] += 1
                ins.then_inc(sem["pool_step"], 1)
                pool.wait_ge(sem["pool_step"], steps[0])

            def split_weights(g):
                kind, l, i, nk, _ = SEQ[g]
                o = (g % 2) * 1024
                sl = slice(o, o + nk * P)
                pool.wait_ge(sem[f"raw_in{g % 2}"], 16 * (g // 2 + 1))
                if g >= 2:
                    pool.wait_ge(sem["acc_ready"], FIRST_CHUNK[g - 1])
                link(G.tensor_copy(w_hi[:, sl], raw[:, sl]))
                link(G.tensor_tensor(w_lo[:, sl], raw[:, sl], w_hi[:, sl].bitcast(F32), ALU.subtract))
                pool.sem_inc(sem["w_split"], 1)

            for l in layers:
                for i in range(6):
                    split_weights(proj_index(l, IN1[i]))
                split_weights(proj_index(l, "bk"))
                pool.wait_ge(sem["mixc_ready"], 2 * (l + 1))
                link(G.memset(at_kz[0][HD:P, :], 0.0))
                link(G.memset(at_kz[1][0:HD, :], 0.0))
                link(G.memset(at_vz_, 0.0))
                pool.sem_inc(sem["kv_clear"], 1)

                def cosines(n):
                    pool.wait_ge(sem["raw_ready"], n + 1)
                    pool.wait_ge(sem["rope_in"], 16 * (l + 1))
                    if n % 5:
                        if n % 5 == 1:
                            pool.wait_ge(sem["kz_ready"], l + 1)
                        else:
                            pool.wait_ge(sem["sc_ready"], ATT0[l] + (n % 5 - 1) * len(ATT[l]) // 4)
                    link(G.tensor_tensor(at_q[:, 0:S], at_raw[:, 0:S], at_cs[:, 0:S], ALU.mult))
                    link(G.tensor_copy(at_q[:, S:T], at_raw[:, S:T]))
                    pool.sem_inc(sem["cosm_ready"], 1)

                split_weights(proj_index(l, "bv"))
                cosines(5 * l)
                for j in range(4):
                    split_weights(proj_index(l, f"q{j}"))
                    split_weights(proj_index(l, f"bg{j}"))
                    cosines(5 * l + 1 + j)
                for name in IN1[16:]:
                    split_weights(proj_index(l, name))
                pool.wait_ge(sem["proj_in"], l + 1)
                for b in gl_vz:
                    link(G.memset(b, 0.0))
                for n, t in enumerate(GORD):
                    if l and t >= NBLK:
                        continue
                    m = outputs(l, n)
                    pool.wait_ge(sem["xk_ready"], m)
                    if n >= 2:
                        pool.wait_ge(sem["u_sum"], NTT * l + n - 1)
                    for dr in range(2):
                        last = G.tensor_tensor(gl_kz[n % 2][:, dr * 512:(dr + 1) * 512].rearrange("p (h t) -> p h t", t=P),
                                               gl_x2[n % 2][:, dr * P:(dr + 1) * P].unsqueeze(1).broadcast_to([P, 4, P]),
                                               k("headrows").unsqueeze(2).broadcast_to([P, 4, P]), ALU.mult)
                        link(last)
                    pool.sem_inc(sem["kz_split"], 1)
                    if n >= 2 and (l == 0 or GORD[n - 2] < NBLK):
                        pool.wait_ge(sem["ob_ready"], outputs(l, n - 2))
                    vz = gl_vz[n % 2].rearrange("p (h e) -> p h e", e=P)
                    vn = gl_v[:, t, :].rearrange("p (h e) -> p h e", e=HD)
                    for o in range(2):
                        link(G.tensor_copy(vz[:, o:4:2, o * HD:(o + 1) * HD], vn[:, o:4:2, :]))
                    pool.sem_inc(sem["gvz_ready"], 1)
                if upto and upto[0] == "in" and upto[1] == l:
                    return
                for d in range(DT):
                    split_weights(INDEX[("out1", l, d)])
                if upto and upto[0] == "layer" and upto[1] == l:
                    return

            for l in layers:
                for i in range(8):
                    split_weights(INDEX[("in2", l, i)])
                pool.wait_ge(sem["po_mixed"], 2 * (l + 1))
                pool.wait_ge(sem["sg_mixed"], 2 * (l + 1))
                link(G.memset(re_kz[0][HD:P, :], 0.0))
                link(G.memset(re_kz[1][0:HD, :], 0.0))
                link(G.memset(re_vz_, 0.0))
                pool.sem_inc(sem["re_clear"], 1)
                pool.wait_ge(sem["re_cs_in"], 16 * (l + 1))
                w2i = lambda name: INDEX[("in2", l, IN2.index(name))]

                def cosines2(r, m, dst):
                    pool.wait_ge(sem["re_raw_ready"], 2 * r + m + 1)
                    if r:
                        pool.wait_ge(sem["re_ysum"], 2 * r)
                    link(G.tensor_tensor(dst, re_raw[m], re_cs[:, 0:S], ALU.mult))
                    pool.sem_inc(sem["re_cos"], 1)

                for j in range(4):
                    r = 4 * l + j
                    split_weights(w2i(f"v{j}"))
                    cosines2(r, 0, re_q)
                    split_weights(w2i(f"g{j}"))
                    cosines2(r, 1, re_k)
                    split_weights(w2i(f"q{j + 1}") if j < 3 else INDEX[("out2", l, 0)])
                    pool.wait_ge(sem["re_roped"], 2 * r + 2)
                    for g in range(2):
                        link(G.tensor_copy(re_kz[g][g * HD:(g + 1) * HD, :], re_k[g * HD:(g + 1) * HD, :]))
                    link(G.tensor_tensor(re_qd.rearrange("p (n t) -> p n t", t=P), re_q.rearrange("p (n t) -> p n t", t=P),
                                         k("qdec")[:, j * P:(j + 1) * P].unsqueeze(1).broadcast_to([P, NBLK, P]), ALU.mult))
                    pool.sem_inc(sem["re_kz_ready"], 1)
                    if j < 3:
                        split_weights(w2i(f"k{j + 1}"))
                for d in range(1, DT):
                    split_weights(INDEX[("out2", l, d)])
                for f in range(NF):
                    split_weights(INDEX[("up", l, 2 * f)])
                    split_weights(INDEX[("up", l, 2 * f + 1)])
                    for d in range(DT if f in AFTER else 0):
                        split_weights(INDEX[("down", l, (AFTER[f], d))])


_NAMES = ["xT", "cT", "w_mod", "w_in1", "w_out1", "w_up", "vec1", "vec2", "vec3", "sinks", "gla_up",
          "w_in2", "w_out2", "w_ffn", "w_down", "a_ws", "a_bs", "b_w", "const", "rope1", "rope2"]


def lay_out(v):
    f = lambda a: np.ascontiguousarray(a, dtype=np.float32)

    def tiles(w, cols):
        w = np.asarray(w)
        out = np.zeros((w.shape[0], len(cols), P, w.shape[1] // P, P), np.float32)
        for i, c in enumerate(cols):
            out[:, i, :, :, :len(c)] = w[:, :, c].reshape(w.shape[0], -1, P, len(c)).transpose(0, 2, 1, 3)
        return out.reshape(w.shape[0], len(cols), P, -1)

    r = lambda o, n: list(range(o, o + n))
    bq, bg = 768, 768 + 512 + 256
    cb = bg + 512
    heads = lambda o, j: r(o + 64 * j, 64) + r(o + 64 * (j + 4), 64)
    cols = {"val0": r(0, P), "val1": r(P, P), "glu0": r(256, P), "glu1": r(384, P), "gate0": r(512, P), "gate1": r(640, P),
            "bk": r(bq + 512, P), "bv": r(bq + 640, P), "cq": r(cb, P), "ck": r(cb + P, P),
            "cv0": r(cb + 256, P), "cv1": r(cb + 384, P), "lr": r(cb + 512, 32), "cg0": r(cb + 544, P), "cg1": r(cb + 672, P)}
    for j in range(4):
        cols[f"q{j}"], cols[f"bg{j}"] = heads(bq, j), heads(bg, j)
    rows = r(0, 256) + sum((heads(256, j) for j in range(4)), []) + r(768, 256)
    cols2 = {"su0": r(0, P), "su1": r(P, P), "sv0": r(256, P), "sv1": r(384, P), "x0": r(512, P), "x1": r(640, P)}
    for j in range(4):
        for a, o in zip("qkvg", (768, 1280, 1792, 2304)):
            cols2[f"{a}{j}"] = r(o + P * j, P)
    per = lambda a: np.asarray(a).reshape(a.shape[:-1] + (-1, P))
    v1 = [np.concatenate([per(v["conv_w"][l]).transpose(1, 0, 2).reshape(62, P)] +
                         [per(v[n][l]) for n in ("conv_b", "conv_ln_w", "conv_ln_b", "gla_norm_w", "b_mod")]) for l in range(2)]
    v2 = [np.concatenate([per(v[n + "_2"][l]) for n in ("norm1_g", "a_vnorm_g", "b_scale", "c_norm_g", "norm2_g")] +
                         [per(v["conv_w_2"][l]).reshape(132, P), per(v["conv_b_2"][l])]) for l in range(2)]
    up = np.zeros((2, P, 256), np.float32)
    for d in range(2):
        up[:, 16 * d:16 * (d + 1), P * d:P * (d + 1)] = v["gla_w_up"][:, d]
        up[:, 32, P * d:P * (d + 1)] = v["gla_b_up"][:, d]
    tok = np.concatenate([v["x"][0], v["ctx"][0]])
    dff = NF * P
    bw = np.zeros((2, 2, P, P), np.float32)
    for g in range(4):
        o = 64 * (g % 2)
        bw[:, g // 2, o:o + 64, o:o + 64] = v["b_w_2"][:, g]
    wd = np.asarray(v["w_down_2"])
    ffn = sum(([r(f * P, P), r(dff + f * P, P)] for f in range(NF)), [])
    return {
        "xT": f(tok.T.reshape(DT, P, T).transpose(1, 0, 2)),
        "cT": f(np.stack([v["c"][0], v["c_ctx"]], -1).reshape(DT, P, 2).transpose(1, 0, 2).reshape(P, 16)),
        "w_mod": tiles(v["w_mod"], [r(P * i, P) for i in range(24)]),
        "w_in1": tiles(v["w_in"], [cols[n] for n in IN1]),
        "w_out1": tiles(np.asarray(v["w_out"])[:, rows], [r(P * i, P) for i in range(8)]),
        "w_up": f(np.zeros(1)) if False else f(up),
        "vec1": f(np.concatenate(v1).T), "vec2": f(np.concatenate(v2).T),
        "vec3": f(np.concatenate([per(v["final_norm_w"]), per(v["final_g_2"])]).T),
        "sinks": f(np.broadcast_to(np.asarray(v["attn_sink"]).reshape(1, 16), (P, 16))),
        "gla_up": f(up),
        "w_in2": tiles(v["w_in_2"], [cols2[n] for n in IN2]),
        "w_out2": tiles(v["w_out_2"], [r(P * i, P) for i in range(8)]),
        "w_ffn": tiles(v["w_up_2"], ffn),
        "w_down": f(wd.reshape(2, NF, P, DT, P).transpose(0, 3, 2, 1, 4).reshape(2, DT, P, dff)),
        "a_ws": f(np.asarray(v["a_ws_2"]).transpose(0, 3, 1, 2).reshape(2, P, 512)),
        "a_bs": f(np.asarray(v["a_bs_2"]).reshape(2, 2, 2, 1, P).repeat(64, 3).reshape(2, 2, P, P).transpose(0, 2, 1, 3).reshape(2, P, 256)),
        "b_w": f(bw.transpose(0, 2, 1, 3).reshape(2, P, 256)),
        "const": CONSTS, "rope1": rope_tables()[0], "rope2": rope_tables()[1],
    }


def kernel(**inputs):
    import concourse.bacc as bacc
    from concourse.bass_utils import run_bass_kernel_spmd as run

    arrays = lay_out(inputs)
    nc = bacc.Bacc("TRN2", target_bir_lowering=False, num_devices=1)
    args = [nc.dram_tensor(n, arrays[n].shape, F32, kind="ExternalInput").ap() for n in _NAMES]
    out = nc.dram_tensor("out", (P, DT, S), F32, kind="ExternalOutput").ap()
    two_mixers(nc, *args, out)
    r = run(nc, [{n: arrays[n] for n in _NAMES}], core_ids=[0])
    return np.ascontiguousarray(r.results[0]["out"].transpose(1, 0, 2).reshape(D, S).T)[None]
```
